# Optimizing a Trainium2 kernel written in Bass

```python
import math
import jax, jax.numpy as jnp
from jax import lax
import numpy as np

D_MODEL = 1024
BATCH = 1
SEQ = 256
DEPTH = 2

N_MIXERS = 2
N_RWKV_LAYERS = (DEPTH + 1) // 2
N_DSA_LAYERS = DEPTH // 2
N_META = 16
D_FF = 2816
NORM_EPS = 1e-6
HEAD_DIM = 64
ROPE_DIM = HEAD_DIM // 4
ROPE_THETA = 500000.0
RWKV_HEADS = D_MODEL // HEAD_DIM
D_DECAY_LORA = 64
D_AAA_LORA = 64
D_GATE_LORA = 160
RWKV_LN_EPS = 64e-5
ATT_HEADS = D_MODEL // HEAD_DIM
ATT_KV_HEADS = 4
ATT_GROUP = ATT_HEADS // ATT_KV_HEADS
IDX_HEADS = 8
IDX_DIM = 64
TOPK_MAX = 256
Q_BLOCK = 128
ATT_Q_W = ATT_HEADS * HEAD_DIM
ATT_KV_W = ATT_KV_HEADS * HEAD_DIM
IDX_Q_W = IDX_HEADS * IDX_DIM
ATT_SPLITS = (ATT_Q_W, ATT_Q_W + ATT_KV_W, ATT_Q_W + 2 * ATT_KV_W,
              ATT_Q_W + 2 * ATT_KV_W + IDX_Q_W, ATT_Q_W + 2 * ATT_KV_W + IDX_Q_W + IDX_DIM)
ATT_IN_W = ATT_Q_W + 2 * ATT_KV_W + IDX_Q_W + IDX_DIM + IDX_HEADS


def rms_norm(x, g, eps=NORM_EPS):
    xf = x.astype(jnp.float32)
    y = xf * lax.rsqrt(jnp.mean(xf * xf, axis=-1, keepdims=True) + eps)
    return y.astype(x.dtype) * g

def swiglu(h, w_in, w_out):
    gate, up = jnp.split(h @ w_in, 2, axis=-1)
    return (jax.nn.silu(gate) * up) @ w_out

def rope_tables(n_pos, dtype):
    inv = ROPE_THETA ** (-jnp.arange(0, ROPE_DIM, 2, dtype=jnp.float32) / ROPE_DIM)
    ang = jnp.arange(n_pos, dtype=jnp.float32)[:, None] * inv[None, :]
    return jnp.cos(ang).astype(dtype), jnp.sin(ang).astype(dtype)

def partial_rope(x, cos, sin):
    half = ROPE_DIM // 2
    x1 = x[..., :half]
    x2 = x[..., half:ROPE_DIM]
    c = cos[None, :, None, :]
    s = sin[None, :, None, :]
    return jnp.concatenate([x1 * c - x2 * s, x2 * c + x1 * s, x[..., ROPE_DIM:]], axis=-1)

def wkv7_scan(r, w, k, v, a, b):
    B, T, H, N = r.shape
    xs = tuple(jnp.moveaxis(t.astype(jnp.float32), 1, 0) for t in (r, w, k, v, a, b))

    def step(S, inp):
        r_t, w_t, k_t, v_t, a_t, b_t = inp
        sa = jnp.einsum("bhij,bhj->bhi", S, a_t)
        S = S * w_t[:, :, None, :] + sa[..., None] * b_t[:, :, None, :] + v_t[..., None] * k_t[:, :, None, :]
        y = jnp.einsum("bhij,bhj->bhi", S, r_t)
        return S, y

    S0 = jnp.zeros((B, H, N, N), jnp.float32)
    _, ys = lax.scan(step, S0, xs)
    return jnp.moveaxis(ys, 0, 1).astype(r.dtype)

def rwkv7_time_mix(h, mix, w_r, w_k, w_v, w_o, w0, w1, w2, a0, a1, a2, g1, g2,
                   k_k, k_a, r_k, lnx_g, lnx_b):
    B, T, D = h.shape
    H, N = RWKV_HEADS, HEAD_DIM
    xx = jnp.pad(h, ((0, 0), (1, 0), (0, 0)))[:, :-1] - h
    xm = h[None] + xx[None] * mix[:, None, None, :]
    xr, xw, xk, xv, xa, xg = xm[0], xm[1], xm[2], xm[3], xm[4], xm[5]
    r = xr @ w_r
    k = xk @ w_k
    v = xv @ w_v
    w_log = -jax.nn.softplus(-(w0 + jnp.tanh(xw @ w1) @ w2)) - 0.5
    a = jax.nn.sigmoid(a0 + (xa @ a1) @ a2)
    g = jax.nn.sigmoid(xg @ g1) @ g2
    kk = (k * k_k).reshape(B, T, H, N).astype(jnp.float32)
    kk = (kk / jnp.maximum(jnp.sqrt(jnp.sum(kk * kk, axis=-1, keepdims=True)), 1e-12)).astype(h.dtype)
    k = k * (1.0 + (a - 1.0) * k_a)
    decay = jnp.exp(-jnp.exp(w_log.astype(jnp.float32)))
    rh = r.reshape(B, T, H, N)
    kh = k.reshape(B, T, H, N)
    vh = v.reshape(B, T, H, N)
    ah = a.reshape(B, T, H, N)
    y = wkv7_scan(rh, decay.reshape(B, T, H, N), kh, vh, -kk, kk * ah)
    yf = y.astype(jnp.float32)
    mu = jnp.mean(yf, axis=-1, keepdims=True)
    var = jnp.mean((yf - mu) ** 2, axis=-1, keepdims=True)
    yn = ((yf - mu) * lax.rsqrt(var + RWKV_LN_EPS)).astype(h.dtype).reshape(B, T, D) * lnx_g + lnx_b
    bonus = (jnp.sum(rh * kh * r_k, axis=-1, keepdims=True) * vh).reshape(B, T, D)
    return ((yn + bonus) * g) @ w_o

def dsa_attention(h, w_in, q_g, k_g, w_o, cos, sin, topk):
    B, T, D = h.shape
    q, k, v, qi, ki, wi = jnp.split(h @ w_in, ATT_SPLITS, axis=-1)
    q = partial_rope(rms_norm(q.reshape(B, T, ATT_HEADS, HEAD_DIM), q_g), cos, sin)
    k = partial_rope(rms_norm(k.reshape(B, T, ATT_KV_HEADS, HEAD_DIM), k_g), cos, sin)
    v = v.reshape(B, T, ATT_KV_HEADS, HEAD_DIM)
    qi = partial_rope(qi.reshape(B, T, IDX_HEADS, IDX_DIM), cos, sin)
    ki = partial_rope(ki[:, :, None, :], cos, sin)[:, :, 0, :]
    wi = wi * (IDX_HEADS ** -0.5 * IDX_DIM ** -0.5)

    n_blk = -(-T // Q_BLOCK)
    pad = n_blk * Q_BLOCK - T

    def to_blocks(t):
        t = jnp.pad(t, [(0, 0), (0, pad)] + [(0, 0)] * (t.ndim - 2))
        return jnp.moveaxis(t.reshape((B, n_blk, Q_BLOCK) + t.shape[2:]), 1, 0)

    starts = jnp.arange(n_blk, dtype=jnp.int32) * Q_BLOCK
    kpos = jnp.arange(T, dtype=jnp.int32)
    scale = HEAD_DIM ** -0.5

    def block(args):
        qb, qib, wib, start = args
        qpos = start + jnp.arange(Q_BLOCK, dtype=jnp.int32)
        rel = jax.nn.relu(jnp.einsum("bqhd,bkd->bqhk", qib, ki))
        score = jnp.einsum("bqh,bqhk->bqk", wib, rel).astype(jnp.float32)
        causal = kpos[None, :] <= qpos[:, None]
        score = jnp.where(causal[None], score, -jnp.inf)
        _, idx = lax.top_k(score, topk)
        valid = idx <= qpos[None, :, None]
        kg = jax.vmap(lambda kb, ib: kb[ib])(k, idx)
        vg = jax.vmap(lambda vb, ib: vb[ib])(v, idx)
        qg = qb.reshape(B, Q_BLOCK, ATT_KV_HEADS, ATT_GROUP, HEAD_DIM)
        logits = jnp.einsum("bqgrd,bqkgd->bqgrk", qg, kg).astype(jnp.float32) * scale
        logits = jnp.where(valid[:, :, None, None, :], logits, -jnp.inf)
        p = jax.nn.softmax(logits, axis=-1).astype(v.dtype)
        o = jnp.einsum("bqgrk,bqkgd->bqgrd", p, vg)
        return o.reshape(B, Q_BLOCK, ATT_Q_W)

    out = lax.map(block, (to_blocks(q), to_blocks(qi), to_blocks(wi), starts))
    out = jnp.moveaxis(out, 0, 1).reshape(B, n_blk * Q_BLOCK, ATT_Q_W)[:, :T]
    return out @ w_o

def first_inputs(seed: int = 0) -> dict:
    key = jax.random.key(seed)
    ks = jax.random.split(key, 32)
    f32 = jnp.float32

    def nrm(k, shape, scale):
        return jax.random.normal(k, shape, f32) * scale

    D = D_MODEL
    A = N_RWKV_LAYERS
    S = N_DSA_LAYERS
    return {
        "x": nrm(ks[0], (BATCH, SEQ, D), 1.0),
        "meta": nrm(ks[1], (N_META, D), 1.0),
        "norm_g": 1.0 + nrm(ks[2], (DEPTH, 3, D), 0.02),
        "ffn_w_in": nrm(ks[3], (DEPTH, 2, D, 2 * D_FF), D ** -0.5),
        "ffn_w_out": nrm(ks[4], (DEPTH, 2, D_FF, D), D_FF ** -0.5),
        "rk_mix": jax.random.uniform(ks[5], (A, 6, D), f32),
        "rk_w_r": nrm(ks[6], (A, D, D), D ** -0.5),
        "rk_w_k": nrm(ks[7], (A, D, D), D ** -0.5),
        "rk_w_v": nrm(ks[8], (A, D, D), D ** -0.5),
        "rk_w_o": nrm(ks[9], (A, D, D), D ** -0.5),
        "rk_w0": -0.6 + nrm(ks[10], (A, D), 0.3),
        "rk_w1": nrm(ks[11], (A, D, D_DECAY_LORA), D ** -0.5),
        "rk_w2": nrm(ks[12], (A, D_DECAY_LORA, D), 0.1 * D_DECAY_LORA ** -0.5),
        "rk_a0": nrm(ks[13], (A, D), 0.1),
        "rk_a1": nrm(ks[14], (A, D, D_AAA_LORA), D ** -0.5),
        "rk_a2": nrm(ks[15], (A, D_AAA_LORA, D), 0.1 * D_AAA_LORA ** -0.5),
        "rk_g1": nrm(ks[16], (A, D, D_GATE_LORA), D ** -0.5),
        "rk_g2": nrm(ks[17], (A, D_GATE_LORA, D), D_GATE_LORA ** -0.5),
        "rk_k_k": 0.85 + nrm(ks[18], (A, D), 0.05),
        "rk_k_a": 1.0 + nrm(ks[19], (A, D), 0.05),
        "rk_r_k": nrm(ks[20], (A, RWKV_HEADS, HEAD_DIM), 0.1),
        "rk_lnx_g": 1.0 + nrm(ks[21], (A, D), 0.02),
        "rk_lnx_b": nrm(ks[22], (A, D), 0.02),
        "at_w_in": nrm(ks[23], (S, D, ATT_IN_W), D ** -0.5),
        "at_q_g": 1.0 + nrm(ks[24], (S, HEAD_DIM), 0.02),
        "at_k_g": 1.0 + nrm(ks[25], (S, HEAD_DIM), 0.02),
        "at_w_o": nrm(ks[26], (S, ATT_Q_W, D), ATT_Q_W ** -0.5),
    }

def first_block(x, meta, norm_g, ffn_w_in, ffn_w_out, rk_mix, rk_w_r, rk_w_k, rk_w_v, rk_w_o,
              rk_w0, rk_w1, rk_w2, rk_a0, rk_a1, rk_a2, rk_g1, rk_g2, rk_k_k, rk_k_a, rk_r_k,
              rk_lnx_g, rk_lnx_b, at_w_in, at_q_g, at_k_g, at_w_o):
    B, L, D = x.shape
    topk = min(TOPK_MAX, L // 4)
    h = jnp.concatenate([jnp.broadcast_to(meta.astype(x.dtype)[None], (B, N_META, D)), x], axis=1)
    T = h.shape[1]
    cos, sin = rope_tables(T, x.dtype)
    for i in range(DEPTH):
        g = norm_g[i]
        h = h + 0.5 * swiglu(rms_norm(h, g[0]), ffn_w_in[i, 0], ffn_w_out[i, 0])
        hn = rms_norm(h, g[1])
        j = i // N_MIXERS
        if i % N_MIXERS == 0:
            h = h + rwkv7_time_mix(hn, rk_mix[j], rk_w_r[j], rk_w_k[j], rk_w_v[j], rk_w_o[j],
                                   rk_w0[j], rk_w1[j], rk_w2[j], rk_a0[j], rk_a1[j], rk_a2[j],
                                   rk_g1[j], rk_g2[j], rk_k_k[j], rk_k_a[j], rk_r_k[j],
                                   rk_lnx_g[j], rk_lnx_b[j])
        else:
            h = h + dsa_attention(hn, at_w_in[j], at_q_g[j], at_k_g[j], at_w_o[j], cos, sin, topk)
        h = h + 0.5 * swiglu(rms_norm(h, g[2]), ffn_w_in[i, 1], ffn_w_out[i, 1])
    return h[:, N_META:]


DEPTH_2 = 1

RET_HEADS = 4
RET_DV = D_MODEL // RET_HEADS
RET_DK = RET_DV // 2
RET_CHUNK = 128
SC_WIDTH = D_MODEL
CONV_WIDTH = 3
NSA_DH = 64
NSA_HEADS = D_MODEL // NSA_DH
NSA_KV_HEADS = 4
NSA_HPG = NSA_HEADS // NSA_KV_HEADS
CMP_BLOCK = 32
CMP_STRIDE = 16
CMP_HIDDEN = 256
SLC_BLOCK = 64
N_SELECT = 16
WINDOW = 512
Q_CHUNK = 64
D_FF_2 = ((8 * D_MODEL // 3 + 127) // 128) * 128
N_BRANCH = 3
EPS = 1e-6
NEG = -1e30
FORCE = 1e6

RET_QK_W = RET_HEADS * RET_DK
RET_V_W = RET_HEADS * RET_DV
NSA_Q_W = NSA_HEADS * NSA_DH
NSA_KV_W = NSA_KV_HEADS * NSA_DH
IN_SPLITS = (RET_QK_W, RET_QK_W, RET_V_W, RET_V_W, SC_WIDTH, SC_WIDTH, SC_WIDTH,
             NSA_Q_W, 6 * NSA_KV_W, 3 * NSA_HEADS, N_BRANCH * D_MODEL)
IN_WIDTH = sum(IN_SPLITS)
IN_OFFSETS = tuple(np.cumsum(IN_SPLITS)[:-1].tolist())


def rms_norm_2(x, w):
    xf = x.astype(jnp.float32)
    y = xf * lax.rsqrt(jnp.mean(xf * xf, axis=-1, keepdims=True) + EPS)
    return (y * w.astype(jnp.float32)).astype(x.dtype)

def causal_dwconv(x, w):
    c = x.shape[-1]
    return lax.conv_general_dilated(x, w[:, None, :].astype(x.dtype), window_strides=(1,),
                                    padding=((CONV_WIDTH - 1, 0),),
                                    dimension_numbers=('NWC', 'WIO', 'NWC'),
                                    feature_group_count=c)

def rotary(x, cos, sin):
    x1, x2 = jnp.split(x, 2, axis=-1)
    return jnp.concatenate([x1 * cos - x2 * sin, x1 * sin + x2 * cos], axis=-1)

def retention(q, k, v, g, norm_w):
    b, s = q.shape[:2]
    dt = q.dtype
    pos = jnp.arange(s, dtype=jnp.float32)
    theta = 10000.0 ** (-jnp.linspace(0.0, 1.0, RET_DK // 2, dtype=jnp.float32))
    ang = pos[:, None] * theta[None, :]
    cos = jnp.cos(ang)[None, :, None, :].astype(dt)
    sin = jnp.sin(ang)[None, :, None, :].astype(dt)
    q = rotary(q, cos, sin)
    k = rotary(k, cos, sin) * (RET_DK ** -0.5)
    log_gamma = jnp.log1p(-(2.0 ** (-5.0 - jnp.arange(RET_HEADS, dtype=jnp.float32))))
    c = RET_CHUNK
    n = s // c
    qc = q.reshape(b, n, c, RET_HEADS, RET_DK)
    kc = k.reshape(b, n, c, RET_HEADS, RET_DK)
    vc = v.reshape(b, n, c, RET_HEADS, RET_DV)
    j = jnp.arange(c, dtype=jnp.float32)
    rel = j[:, None] - j[None, :]
    dmask = jnp.where(rel >= 0, jnp.exp(log_gamma[:, None, None] * jnp.maximum(rel, 0.0)), 0.0).astype(dt)
    scores = jnp.einsum('bnqhd,bnkhd->bnhqk', qc, kc) * dmask
    o_intra = jnp.einsum('bnhqk,bnkhv->bnqhv', scores, vc)
    zeta = jnp.exp(log_gamma[:, None] * (c - 1 - j)[None, :]).astype(dt)
    kv = jnp.einsum('bnchd,bnchv,hc->nbhdv', kc, vc, zeta)
    chunk_decay = jnp.exp(log_gamma * c).astype(dt)[None, :, None, None]

    def step(state, kv_i):
        return state * chunk_decay + kv_i, state

    _, prev = lax.scan(step, jnp.zeros((b, RET_HEADS, RET_DK, RET_DV), dt), kv)
    xi = jnp.exp(log_gamma[:, None] * (j + 1.0)[None, :]).astype(dt)
    o_cross = jnp.einsum('bnchd,nbhdv,hc->bnchv', qc, prev, xi)
    o = (o_intra + o_cross).reshape(b, s, RET_HEADS, RET_DV).astype(jnp.float32)
    mu = jnp.mean(o, axis=-1, keepdims=True)
    var = jnp.mean(jnp.square(o - mu), axis=-1, keepdims=True)
    o = ((o - mu) * lax.rsqrt(var + EPS)).reshape(b, s, RET_V_W) * norm_w.astype(jnp.float32)
    return (jax.nn.silu(g.astype(jnp.float32)) * o).astype(dt)

def compress(kv, pos, w1, w2):
    b, s = kv.shape[:2]
    nc = (s - CMP_BLOCK) // CMP_STRIDE + 1
    idx = np.arange(nc)[:, None] * CMP_STRIDE + np.arange(CMP_BLOCK)[None, :]
    blk = kv[:, idx] + pos[None, None, :, None, :]
    blk = blk.transpose(0, 1, 3, 2, 4).reshape(b, nc, NSA_KV_HEADS, CMP_BLOCK * NSA_DH)
    return jax.nn.gelu(blk @ w1) @ w2

def nsa_attention(q, kc_raw, vc_raw, ks, vs, kw, vw, gates, cmp_pos, cmp_w1, cmp_w2):
    b, s = q.shape[:2]
    dt = q.dtype
    scale = NSA_DH ** -0.5
    kc = compress(kc_raw, cmp_pos[0], cmp_w1[0], cmp_w2[0])
    vc = compress(vc_raw, cmp_pos[1], cmp_w1[1], cmp_w2[1])
    nc = kc.shape[1]
    ns = s // SLC_BLOCK
    n_sel = min(N_SELECT, ns)
    ci = np.arange(nc) * CMP_STRIDE
    sj = np.arange(ns) * SLC_BLOCK
    overlap = jnp.asarray(((ci[:, None] < sj[None, :] + SLC_BLOCK) &
                           (ci[:, None] + CMP_BLOCK > sj[None, :])).astype(np.float32))
    cmp_end = jnp.asarray(ci + CMP_BLOCK - 1)
    ks_blk = ks.reshape(b, ns, SLC_BLOCK, NSA_KV_HEADS, NSA_DH).transpose(0, 3, 1, 2, 4)
    vs_blk = vs.reshape(b, ns, SLC_BLOCK, NSA_KV_HEADS, NSA_DH).transpose(0, 3, 1, 2, 4)
    kw_pad = jnp.pad(kw, ((0, 0), (WINDOW, 0), (0, 0), (0, 0)))
    vw_pad = jnp.pad(vw, ((0, 0), (WINDOW, 0), (0, 0), (0, 0)))
    qg = q.reshape(b, s, NSA_KV_HEADS, NSA_HPG, NSA_DH)
    bi = jnp.arange(b)[:, None, None, None]
    gi = jnp.arange(NSA_KV_HEADS)[None, :, None, None]
    blk_ids = jnp.arange(ns)

    def chunk(cidx):
        t0 = cidx * Q_CHUNK
        t = t0 + jnp.arange(Q_CHUNK)
        qc = lax.dynamic_slice_in_dim(qg, t0, Q_CHUNK, axis=1)
        s1 = jnp.einsum('bqghd,bcgd->bghqc', qc, kc).astype(jnp.float32) * scale
        valid1 = cmp_end[None, :] <= t[:, None]
        any1 = (t >= CMP_BLOCK - 1).astype(jnp.float32)[:, None]
        p1 = jax.nn.softmax(jnp.where(valid1, s1, NEG), axis=-1) * any1
        o_cmp = jnp.einsum('bghqc,bcgd->bqghd', p1.astype(dt), vc)
        imp = jnp.einsum('bghqc,cs->bgqs', p1, overlap)
        cur = t // SLC_BLOCK
        causal_blk = blk_ids[None, :] * SLC_BLOCK <= t[:, None]
        forced = (blk_ids[None, :] == 0) | (blk_ids[None, :] == cur[:, None]) | (blk_ids[None, :] == cur[:, None] - 1)
        imp = jnp.where(forced & causal_blk, FORCE, imp)
        imp = jnp.where(causal_blk, imp, NEG)
        _, idx = lax.top_k(imp, n_sel)
        kg = ks_blk[bi, gi, idx]
        vg = vs_blk[bi, gi, idx]
        s2 = jnp.einsum('bqghd,bgqnld->bghqnl', qc, kg).astype(jnp.float32) * scale
        kpos2 = idx[..., None] * SLC_BLOCK + jnp.arange(SLC_BLOCK)
        mask2 = kpos2 <= t[None, None, :, None, None]
        s2 = jnp.where(mask2[:, :, None], s2, NEG)
        p2 = jax.nn.softmax(s2.reshape(s2.shape[:4] + (-1,)), axis=-1).reshape(s2.shape)
        o_slc = jnp.einsum('bghqnl,bgqnld->bqghd', p2.astype(dt), vg)
        kwc = lax.dynamic_slice_in_dim(kw_pad, t0, Q_CHUNK + WINDOW, axis=1)
        vwc = lax.dynamic_slice_in_dim(vw_pad, t0, Q_CHUNK + WINDOW, axis=1)
        kpos3 = t0 - WINDOW + jnp.arange(Q_CHUNK + WINDOW)
        mask3 = (kpos3[None, :] <= t[:, None]) & (kpos3[None, :] > t[:, None] - WINDOW) & (kpos3[None, :] >= 0)
        s3 = jnp.einsum('bqghd,brgd->bghqr', qc, kwc).astype(jnp.float32) * scale
        p3 = jax.nn.softmax(jnp.where(mask3, s3, NEG), axis=-1)
        o_win = jnp.einsum('bghqr,brgd->bqghd', p3.astype(dt), vwc)
        return o_cmp, o_slc, o_win

    o_cmp, o_slc, o_win = lax.map(chunk, jnp.arange(s // Q_CHUNK))

    def unchunk(o):
        return o.transpose(1, 0, 2, 3, 4, 5).reshape(b, s, NSA_HEADS, NSA_DH)

    o = (gates[..., 0:1] * unchunk(o_cmp) + gates[..., 1:2] * unchunk(o_slc)
         + gates[..., 2:3] * unchunk(o_win))
    return o.reshape(b, s, NSA_Q_W)

def token_mixer(h, w_in, ret_norm_w, w_ret_out, sc_conv_w, w_sc_out,
                cmp_pos, cmp_w1, cmp_w2, w_nsa_out, w_mix_out):
    b, s, _ = h.shape
    z = h @ w_in
    rq, rk, rv, rg, sb, sc, sx, nq, nkv, ng, mg = jnp.split(z, IN_OFFSETS, axis=-1)
    y_ret = retention(rq.reshape(b, s, RET_HEADS, RET_DK), rk.reshape(b, s, RET_HEADS, RET_DK),
                      rv.reshape(b, s, RET_HEADS, RET_DV), rg, ret_norm_w)
    y_sc = sb * causal_dwconv(sc * sx, sc_conv_w)
    k_c, v_c, k_s, v_s, k_w, v_w = jnp.split(nkv.reshape(b, s, 6 * NSA_KV_HEADS, NSA_DH), 6, axis=2)
    y_nsa = nsa_attention(nq.reshape(b, s, NSA_HEADS, NSA_DH), k_c, v_c, k_s, v_s, k_w, v_w,
                          jax.nn.sigmoid(ng).reshape(b, s, NSA_HEADS, 3), cmp_pos, cmp_w1, cmp_w2)
    g_ret, g_sc, g_nsa = jnp.split(jax.nn.sigmoid(mg), N_BRANCH, axis=-1)
    merged = g_ret * (y_ret @ w_ret_out) + g_sc * (y_sc @ w_sc_out) + g_nsa * (y_nsa @ w_nsa_out)
    return merged @ w_mix_out

def conv_glu_ffn(h, w_up, conv_w, w_down):
    u = causal_dwconv(h @ w_up, conv_w)
    a, v = jnp.split(u, 2, axis=-1)
    return (jax.nn.silu(a) * v) @ w_down

def second_inputs(seed: int = 0) -> dict:
    key = jax.random.key(seed)
    ks = jax.random.split(key, 17)
    nrm = jax.random.normal
    f32 = jnp.float32
    return {
        'x': nrm(ks[0], (BATCH, SEQ, D_MODEL), f32),
        'attn_norm_w': 1.0 + 0.02 * nrm(ks[1], (DEPTH_2, D_MODEL), f32),
        'w_in': nrm(ks[2], (DEPTH_2, D_MODEL, IN_WIDTH), f32) * D_MODEL ** -0.5,
        'ret_norm_w': 1.0 + 0.02 * nrm(ks[3], (DEPTH_2, RET_V_W), f32),
        'w_ret_out': nrm(ks[4], (DEPTH_2, RET_V_W, D_MODEL), f32) * RET_V_W ** -0.5,
        'sc_conv_w': nrm(ks[5], (DEPTH_2, CONV_WIDTH, SC_WIDTH), f32) * CONV_WIDTH ** -0.5,
        'w_sc_out': nrm(ks[6], (DEPTH_2, SC_WIDTH, D_MODEL), f32) * SC_WIDTH ** -0.5,
        'nsa_cmp_pos': 0.02 * nrm(ks[7], (DEPTH_2, 2, CMP_BLOCK, NSA_DH), f32),
        'nsa_cmp_w1': nrm(ks[8], (DEPTH_2, 2, CMP_BLOCK * NSA_DH, CMP_HIDDEN), f32) * (CMP_BLOCK * NSA_DH) ** -0.5,
        'nsa_cmp_w2': nrm(ks[9], (DEPTH_2, 2, CMP_HIDDEN, NSA_DH), f32) * CMP_HIDDEN ** -0.5,
        'w_nsa_out': nrm(ks[10], (DEPTH_2, NSA_Q_W, D_MODEL), f32) * NSA_Q_W ** -0.5,
        'w_mix_out': nrm(ks[11], (DEPTH_2, D_MODEL, D_MODEL), f32) * D_MODEL ** -0.5,
        'ffn_norm_w': 1.0 + 0.02 * nrm(ks[12], (DEPTH_2, D_MODEL), f32),
        'w_ffn_up': nrm(ks[13], (DEPTH_2, D_MODEL, 2 * D_FF_2), f32) * D_MODEL ** -0.5,
        'ffn_conv_w': nrm(ks[14], (DEPTH_2, CONV_WIDTH, 2 * D_FF_2), f32) * CONV_WIDTH ** -0.5,
        'w_ffn_down': nrm(ks[15], (DEPTH_2, D_FF_2, D_MODEL), f32) * D_FF_2 ** -0.5,
        'final_norm_w': 1.0 + 0.02 * nrm(ks[16], (D_MODEL,), f32),
    }

def second_block(x, attn_norm_w, w_in, ret_norm_w, w_ret_out, sc_conv_w, w_sc_out,
              nsa_cmp_pos, nsa_cmp_w1, nsa_cmp_w2, w_nsa_out, w_mix_out,
              ffn_norm_w, w_ffn_up, ffn_conv_w, w_ffn_down, final_norm_w):
    for l in range(DEPTH_2):
        h = rms_norm_2(x, attn_norm_w[l])
        x = x + token_mixer(h, w_in[l], ret_norm_w[l], w_ret_out[l], sc_conv_w[l], w_sc_out[l],
                            nsa_cmp_pos[l], nsa_cmp_w1[l], nsa_cmp_w2[l], w_nsa_out[l], w_mix_out[l])
        h = rms_norm_2(x, ffn_norm_w[l])
        x = x + conv_glu_ffn(h, w_ffn_up[l], ffn_conv_w[l], w_ffn_down[l])
    return rms_norm_2(x, final_norm_w)


def setup_inputs(seed=0):
    out = dict(first_inputs(seed))
    for name, value in second_inputs(seed + 1).items():
        if name != "x":
            out[name + "_2"] = value
    return out


def reference(
    x, meta, norm_g, ffn_w_in, ffn_w_out, rk_mix, rk_w_r, rk_w_k, rk_w_v, rk_w_o, rk_w0, rk_w1,
    rk_w2, rk_a0, rk_a1, rk_a2, rk_g1, rk_g2, rk_k_k, rk_k_a, rk_r_k, rk_lnx_g, rk_lnx_b,
    at_w_in, at_q_g, at_k_g, at_w_o, attn_norm_w_2, w_in_2, ret_norm_w_2, w_ret_out_2,
    sc_conv_w_2, w_sc_out_2, nsa_cmp_pos_2, nsa_cmp_w1_2, nsa_cmp_w2_2, w_nsa_out_2,
    w_mix_out_2, ffn_norm_w_2, w_ffn_up_2, ffn_conv_w_2, w_ffn_down_2, final_norm_w_2,
):
    x = first_block(
        x, meta, norm_g, ffn_w_in, ffn_w_out, rk_mix, rk_w_r, rk_w_k, rk_w_v, rk_w_o, rk_w0,
        rk_w1, rk_w2, rk_a0, rk_a1, rk_a2, rk_g1, rk_g2, rk_k_k, rk_k_a, rk_r_k, rk_lnx_g,
        rk_lnx_b, at_w_in, at_q_g, at_k_g, at_w_o,
    )
    return second_block(
        x, attn_norm_w_2, w_in_2, ret_norm_w_2, w_ret_out_2, sc_conv_w_2, w_sc_out_2,
        nsa_cmp_pos_2, nsa_cmp_w1_2, nsa_cmp_w2_2, w_nsa_out_2, w_mix_out_2, ffn_norm_w_2,
        w_ffn_up_2, ffn_conv_w_2, w_ffn_down_2, final_norm_w_2,
    )


_drawn_inputs = setup_inputs


def setup_inputs(seed=0):
    import zlib

    import numpy as np

    out = dict(_drawn_inputs(seed))
    spreads = {}
    factors = {'rk_w1': 2.879,
     'rk_w2': 3.019,
     'rk_k_k': 2.696,
     'at_q_g': 8.0,
     'at_k_g': 8.0,
     'attn_norm_w_2': 3.171,
     'ret_norm_w_2': 39.097,
     'nsa_cmp_pos_2': 200.0,
     'ffn_norm_w_2': 15.925,
     'final_norm_w_2': 20.354,
     'nsa_cmp_w1_2': 3.472,
     'nsa_cmp_w2_2': 3.124}
    for name, (base, spread) in spreads.items():
        noise = np.random.default_rng([zlib.crc32(name.encode()), seed]).standard_normal(out[name].shape)
        drawn = base * np.exp(spread * noise) if base else spread * noise
        out[name] = __import__('jax').numpy.asarray(drawn.astype(out[name].dtype))
    for name, factor in factors.items():
        out[name] = (out[name] * factor).astype(out[name].dtype)
    return out
```

```python
from contextlib import ExitStack

import numpy as np

import concourse.bass as bass
from concourse import mybir

ALU = mybir.AluOpType
ACT = mybir.ActivationFunctionType
F32 = mybir.dt.float32
AX_X = mybir.AxisListType.X

P = 128
D = 1024
DT = D // P
SEQ = 256
N_META = 16
T = SEQ + N_META
CHUNKS = [(0, N_META), (N_META, P), (N_META + P, P)]
HD = 64
FF = 2816
FT = FF // P
N_CMP = 15
RING = 6
PER = 16
LEVELS = 7
NEG = -1e30

STAGES = [
    ("ffn", DT, 2 * FT), ("ffn_out", FT, DT),
    ("rk_r", DT, 8), ("rk_k", DT, 8), ("rk_v", DT, 8), ("rk_w1", DT, 1), ("rk_w2", 1, 8),
    ("rk_a1", DT, 1), ("rk_a2", 1, 8), ("rk_g1", DT, 2), ("rk_g2", 2, 8), ("rk_o", DT, 8),
    ("ffn", DT, 2 * FT), ("ffn_out", FT, DT),
    ("ffn", DT, 2 * FT), ("ffn_out", FT, DT),
    ("at_in", DT, 20), ("at_o", DT, 8),
    ("ffn", DT, 2 * FT), ("ffn_out", FT, DT),
    ("ret_in", DT, 24), ("ret_out", DT, 8), ("ret_mg", DT, 8),
    ("sc_in", DT, 24), ("sc_out", DT, 8), ("sc_mg", DT, 8),
    ("nsa_in", DT, 29), ("cmp_k1", 16, 2), ("cmp_k2", 2, 1), ("cmp_v1", 16, 2), ("cmp_v2", 2, 1),
    ("nsa_out", DT, 8), ("nsa_mg", DT, 8),
    ("mix_out", DT, 8),
    ("ffn2", DT, 2 * FT), ("ffn_out", FT, DT),
]


def stage_starts():
    starts, at = [], 0
    for name, kt, nt in STAGES:
        if name in ("ffn", "ffn2"):
            at = -(-at // PER) * PER
        starts.append(at)
        at += kt * nt
    return starts, -(-at // PER)


STARTS, N_SLOTS = stage_starts()

PARAMS = {}


def _param(name, columns):
    PARAMS[name] = (sum(c for _, c in PARAMS.values()), columns)


for _n, _c in (("norm", 48), ("mix", 48), ("w0", 8), ("a0", 8), ("k_k", 8), ("k_a", 8), ("r_k", 8),
               ("lnx_g", 8), ("lnx_b", 8), ("q_g", 1), ("k_g", 1), ("norm2", 8), ("ret_norm", 8),
               ("sc_conv", 24), ("cmp_pos", 32), ("ffn_norm2", 8), ("ffn_conv", 132), ("final", 8)):
    _param(_n, _c)
N_PARAM = sum(c for _, c in PARAMS.values())

CONSTS = {}


def _const(name, *shape):
    CONSTS[name] = (sum(int(np.prod(s)) for _, s in CONSTS.values()), shape)


for _n, _s in (("ident", (P,)), ("ones", (P,)), ("head_ones", (P,)), ("rope_swap", (P,)), ("ret_swap", (P,)),
               ("level", (LEVELS, P)), ("tri", (2, P)), ("reset", (T,)), ("cos", (T,)), ("sin", (T,)),
               ("ret_cos", (SEQ,)), ("ret_sin", (SEQ,)), ("causal", (3, T)), ("neg", (3, T)),
               ("neg_cmp", (2, N_CMP)), ("any_cmp", (2,)), ("eps", (3,))):
    _const(_n, *_s)
N_CONST = sum(int(np.prod(s)) for _, s in CONSTS.values())
EPS_RMS, EPS_LNX, EPS_RET = range(3)


def constants():
    c = {n: np.zeros((P,) + s, np.float32) for n, (_, s) in CONSTS.items()}
    r = np.arange(P)
    c["ident"][:] = np.eye(P)
    c["ones"][:] = 1
    c["head_ones"][:] = (r[:, None] // HD == r[None, :] // HD)
    for name, width, half in (("rope_swap", HD, 8), ("ret_swap", P, 64)):
        for base in range(0, P, width):
            for d in range(half):
                c[name][base + d + half, base + d] = -1
                c[name][base + d, base + half + d] = 1
    for n in range(LEVELS):
        m = 1 << n
        t, s = r[:, None], r[None, :]
        c["level"][:, n] = (t // (2 * m) == s // (2 * m)) & (t // m % 2 == 1) & (s // m % 2 == 0)
    c["tri"][:, 0] = r[:, None] < r[None, :]
    c["tri"][:, 1] = r[:, None] <= r[None, :]
    c["reset"][:] = 1
    for t0, _ in CHUNKS:
        c["reset"][:, t0] = 0
    inv = (np.float32(500000.0) ** (-np.arange(0, 16, 2, dtype=np.float32) / 16)).astype(np.float32)
    ang = (np.arange(T, dtype=np.float32)[:, None] * inv).astype(np.float32)
    d = r % HD
    c["cos"][:] = np.where(d[:, None] < 16, np.cos(ang).T[d % 8], 1)
    c["sin"][:] = np.where(d[:, None] < 16, np.sin(ang).T[d % 8], 0)
    theta = (np.float32(10000.0) ** (-np.linspace(0, 1, 64, dtype=np.float32))).astype(np.float32)
    ang = (np.arange(SEQ, dtype=np.float32)[:, None] * theta).astype(np.float32)
    c["ret_cos"][:] = np.cos(ang).T[r % 64]
    c["ret_sin"][:] = np.sin(ang).T[r % 64]
    for n, (t0, size) in enumerate(CHUNKS):
        c["causal"][:, n] = np.arange(T)[None] <= t0 + r[:, None]
    c["neg"][:] = (c["causal"] - 1) * -NEG
    for n in range(2):
        t = n * P + r
        c["neg_cmp"][:, n] = np.where(np.arange(N_CMP) * 16 + 31 <= t[:, None], 0, NEG)
        c["any_cmp"][:, n] = t >= 31
    c["eps"][:] = (1e-6, 64e-5, 1e-6)
    return np.concatenate([c[n].reshape(P, -1) for n in CONSTS], axis=1)


def retention_decay():
    gamma = np.log1p(-(2.0 ** (-5.0 - np.arange(4))))
    key = np.arange(P)[:, None, None] + np.arange(2)[None, :, None] * P
    rel = np.arange(SEQ)[None, None, :] - key
    out = [np.where(rel >= 0, np.exp(g * np.maximum(rel, 0)), 0) * P ** -0.5 for g in gamma]
    return np.stack(out, axis=1).astype(np.float32).reshape(P, -1)


def build(nc, stream, x_in, params, consts, decay, out):
    with ExitStack() as ctx:
        def sb(name, shape):
            return ctx.enter_context(nc.sbuf_tensor(name, shape, F32))

        class Semaphores(dict):
            def __missing__(self, name):
                self[name] = ctx.enter_context(nc.semaphore(name))
                return self[name]

        S = Semaphores()

        X = sb("X", [P, DT, T])
        H = sb("H", [P, DT, T])
        T0 = sb("T0", [P, DT, T])
        T1 = sb("T1", [P, DT, T])
        T2 = sb("T2", [P, DT, T])
        A = sb("A", [P, 48, T])
        wring = sb("wring", [P, RING, PER * P])
        par = sb("par", [P, N_PARAM])
        con = sb("con", [P, N_CONST])
        rms = sb("rms", [P, 2, T])
        group = sb("group", [P, 7744])
        small = sb("small", [P, 704])
        ps = ctx.enter_context(nc.psum_tensor("ps", [P, 8, 512], F32))

        def const(name):
            at, shape = CONSTS[name]
            v = con[:, at:at + int(np.prod(shape))]
            return v.rearrange("p (a b) -> p a b", a=shape[0]) if len(shape) == 2 else v

        def param(name, n=0):
            at = PARAMS[name][0] + 8 * n
            return par[:, at:at + 8]

        def column(name, n=0):
            at = PARAMS[name][0] + n
            return par[:, at:at + 1]

        def eps(n):
            at = CONSTS["eps"][0] + n
            return con[:, at:at + 1]

        def carve(owner, *shapes):
            at, views = 0, []
            for shape in shapes:
                n = int(np.prod(shape))
                v = owner[:, at:at + n]
                if len(shape) == 2:
                    v = v.rearrange("p (a b) -> p a b", a=shape[0])
                if len(shape) == 3:
                    v = v.rearrange("p (a b c) -> p a b c", a=shape[0], b=shape[1])
                if len(shape) == 4:
                    v = v.rearrange("p (a b c d) -> p a b c d", a=shape[0], b=shape[1], c=shape[2])
                views.append(v)
                at += n
            assert at <= owner.shape[1], at
            return views

        ident, ones, head_ones = const("ident"), const("ones"), const("head_ones")
        rope_swap, ret_swap, level, tri = const("rope_swap"), const("ret_swap"), const("level"), const("tri")

        silu_out, conv_in, conv_out = carve(group, (2, T), (2, 2, T), (2, 2, T))
        (rk_ar, rk_bkv, rk_tm, rk_lb, rk_lk, rk_x, rk_xt, rk_ym, rk_z, rk_sa, rk_s, rk_sc) = carve(
            group, (2, 2, T), (3, 2, T), (6, P), (4, 2, P), (4, 2, P), (4, P), (4, P), (4, P), (4, HD), (4, HD),
            (2, HD), (2, 2))
        rk_mid, rk_mid_exp, rk_end = carve(small, (3, 8), (3, 8), (3, 8))
        (rk_lora,) = carve(group, (4, T))
        (at_q, at_kg, at_vg, at_p, at_pt, at_vtm, at_gg, at_max, at_sum, at_inv, ns_blk) = carve(
            group, (2, T), (2, T), (6, HD), (4, T), (3, 4, P), (4, 256), (2, 12), (4,), (4,), (4,),
            (16, 4 * N_CMP))
        (ns_gate, ns_cmp_hid, ns_cmp_k, ns_cmp_v, ns_kc, ns_vc, ds_wi, ds_top) = carve(
            small, (2, 48), (2, 4 * N_CMP), (4 * N_CMP,), (4, HD), (N_CMP,), (HD,), (2, 8), (8,))
        ret_vt = A[:, 24:32, :].rearrange("p a t -> p (a t)")[:, 0:2048].rearrange("p (c j v) -> p c j v", c=2, j=8)
        ret_st = A[:, 32:40, :].rearrange("p a t -> p (a t)")[:, 0:2048].rearrange("p (h c q) -> p h c q", h=4, c=2)
        ret_decay = T1[:, :, :].rearrange("p a t -> p (a t)")[:, 0:2048]

        DSA_STEPS = [(c, c, t0, C, 0, at_kg[:, 0, 0:t0 + C], T1[:, c, 0:t0 + C],
                      [(k0, KC, at_vg[0:KC, kc, :]) for kc, (k0, KC) in enumerate(CHUNKS[:c + 1])], True, True)
                     for c, (t0, C) in enumerate(CHUNKS)]
        NSA_STEPS = []
        for c in range(2):
            t0, keys = N_META + c * P, (c + 1) * P
            NSA_STEPS.append((3 * c, c, t0, P, 0, ns_kc[:, :], const("neg_cmp")[:, c, :],
                              [(0, N_CMP, ns_vc[0:N_CMP, :])], True, False))
            for b in range(2):
                NSA_STEPS.append((3 * c + 1 + b, c, t0, P, 1 + b, at_kg[:, b, N_META:N_META + keys],
                                  const("neg")[:, 1 + c, N_META:N_META + keys],
                                  [(kc * P, P, at_vg[:, 2 * kc + b, :]) for kc in range(c + 1)], False, b == 1))

        block = ctx.enter_context(nc.Block())
        TB = slice(N_META, T)

        EMPTIED_BY = {"rk_o": "dve", "at_o": "dve", "mix_out": "dve", "ffn_out": "dve", "cmp_v2": "act"}
        tiles_before, act_before, dve_before, owners = [], [], [], []
        n_act = n_dve = 2
        for name, kt, nt in STAGES:
            tiles_before.append(len(owners))
            act_before.append(n_act)
            dve_before.append(n_dve)
            for i in range(nt):
                if name == "ffn":
                    by = "act" if i % 2 == 0 else "dve"
                else:
                    by = EMPTIED_BY.get(name, "act")
                if by == "act":
                    n_act += 1
                    owners.append(("act_emptied", n_act))
                else:
                    n_dve += 1
                    owners.append(("dve_emptied", n_dve))

        def stage_number(name, nth=0):
            return [i for i, s in enumerate(STAGES) if s[0] == name][nth]

        def tiles_done(name, nth=0):
            s = stage_number(name, nth)
            return tiles_before[s] + STAGES[s][2]

        @block.sync
        def _(sp):
            sp.dma_start(con[:, :], consts).then_inc(S["consts_loaded"], 16)
            sp.dma_start(par[:, :], params).then_inc(S["consts_loaded"], 16)
            sp.dma_start(X[:, :, :], x_in).then_inc(S["x_loaded"], 16)
            loaded = [S[f"slot{i}_loaded"] for i in range(RING)]

            def load(slot, number):
                sp.dma_start(wring[:, slot, :], stream[number]).then_inc(loaded[slot], 16)

            for n in range(RING):
                load(n, n)
            rounds = N_SLOTS // RING
            with sp.Fori(1, rounds) as r:
                for n in range(RING):
                    sp.wait_ge(S["slots_used"], r * RING + (n - RING + 2))
                    sp.dma_start(wring[:, n, :], stream[bass.ds(r * RING + n, 1)].rearrange("a p n -> p (a n)")
                                 ).then_inc(loaded[n], 16)
            for number in range(rounds * RING, N_SLOTS):
                sp.wait_ge(S["slots_used"], number - RING + 2)
                load(number % RING, number)
            sp.wait_ge(S["final_ready"], DT)
            sp.dma_start(out.rearrange("p (a t) -> p a t", a=DT), H[:, :, TB]).then_inc(S["out_stored"], 16)
            sp.wait_ge(S["out_stored"], 16)

        @block.tensor
        def _(pe):
            used_pending = [True]

            def weight_tile(pos, turn=None):
                number, j = divmod(pos, PER)
                slot = number % RING
                if j == 0:
                    value = 16 * (number // RING + 1)
                    pe.wait_ge(S[f"slot{slot}_loaded"], value if turn is None else turn * 16 + value)
                return wring[:, slot, j * P:(j + 1) * P]

            def out_tile(bank, pos, rhs, kt, turn=None, size=T, before_k=None):
                for k in range(kt):
                    w = weight_tile(pos + k, turn)
                    if before_k:
                        before_k(k)
                    mm = pe.matmul(ps[:, bank, 0:size], w, rhs(k), start=(k == 0), stop=(k == kt - 1))
                    if k == kt - 1:
                        mm.then_inc(S["linear_ready"], 1)
                    elif used_pending[0]:
                        mm.then_inc(S["slots_used"], 1)
                        used_pending[0] = False
                    if (pos + k) % PER == PER - 1:
                        assert not used_pending[0]
                        used_pending[0] = True

            def bank_free(tile):
                if tile >= 4:
                    name, value = owners[tile - 4]
                    pe.wait_ge(S[name], value)

            def linear(name, rhs, nth=0, size=T, before_k=None):
                s = stage_number(name, nth)
                _, kt, nt = STAGES[s]
                for i in range(nt):
                    tile = tiles_before[s] + i
                    bank_free(tile)
                    out_tile(tile % 4, STARTS[s] + i * kt, rhs, kt, None, size, before_k if i == 0 else None)

            def feed_forward(s, norm, size, tokens):
                base, a, d = tiles_before[s], act_before[s], dve_before[s]
                conv = STAGES[s][0] == "ffn2"
                for tile in range(base, base + 4):
                    if tile >= 4:
                        bank_free(tile)
                pe.wait_ge(S["h_ready"], DT * (norm + 1))

                def pair(turn, p):
                    for half in range(2):
                        if conv:
                            value = a + 2 * (p - 2) + half + 1
                            pe.wait_ge(S["act_emptied"], turn * 2 * RING + value if turn is not None else value)
                        elif half == 0:
                            pe.wait_ge(S["act_emptied"], turn * RING + (a + p - 1) if turn is not None else a + p - 1)
                        else:
                            pe.wait_ge(S["dve_emptied"], turn * RING + (d + p - 1) if turn is not None else d + p - 1)
                        out_tile((base + 2 * p + half) % 4, STARTS[s] + (2 * p + half) * DT,
                                 lambda k: H[:, k, tokens], DT, turn, size)

                if STARTS[s] and STARTS[s] > STARTS[s - 1] + STAGES[s - 1][1] * STAGES[s - 1][2]:
                    assert not used_pending[0]
                    used_pending[0] = True
                assert used_pending[0]
                turns = FT // RING
                with pe.Fori(0, turns) as turn:
                    for p in range(RING):
                        pair(turn, p)
                for p in range(turns * RING, FT):
                    pair(None, p)

                def hidden_there(k):
                    if conv or k >= FT - 2:
                        pe.wait_ge(S["hidden_ready"] if conv else S["dve_emptied"],
                                   k + 3 if conv else d + k + 1)
                return hidden_there

            def norm_sum(n, size, tokens):
                pe.wait_ge(S["squares_ready"], n + 1)
                for k in range(DT):
                    mm = pe.matmul(ps[:, 4, 0:size], ones, T0[:, k, tokens], start=(k == 0), stop=(k == DT - 1))
                mm.then_inc(S["square_sum_ready"], 1)

            def per_tile(weights, source, banks, size, done):
                for i, bank in enumerate(banks):
                    mm = pe.matmul(ps[:, bank, 0:size], weights, source(i), start=True, stop=True)
                mm.then_inc(S[done], 1)

            def settle(C):
                if C < 32:
                    pe.sem_inc(S["few_rows_waited"], 1)

            def rk_chunk(g, c, t0, C, lv, lx):
                step = g * 3 + (c + 1)
                now = slice(t0, t0 + C)
                heads = [(2 * par + u, par, u, HD * par) for par in range(2) for u in range(2)]
                nl = C.bit_length() - 1
                if c == 0:
                    pe.wait_ge(S["rk_staged"], g + 1)
                settle(C)
                for i in range(3):
                    for u in range(2):
                        n = 2 * i + u
                        mm = pe.transpose(ps[0:C, n // 4, n % 4 * P:(n % 4 + 1) * P], rk_bkv[:, i, u, now], ident)
                mm.then_inc(S["rk_turned"], 1)
                pe.wait_ge(S["rk_y_copied"], step)
                if c:
                    pe.wait_ge(S["rk_state_ready"], g * 2 + c)
                settle(C)
                for i, bank in ((0, 2), (1, 4)):
                    for q, par, u, p in heads:
                        o = ps[0:C, bank + par, u * 256:(u + 1) * 256].rearrange("p (a t) -> p a t", a=2)[:, :, 0:C]
                        mm = pe.matmul(o, rk_bkv[p:p + HD, i, u, now], rk_ar[p:p + HD, u, :, now],
                                       start=True, stop=True)
                mm.then_inc(S["rk_products_ready"], 1)
                pe.wait_ge(S["rk_masked"], step)
                pe.wait_ge(S["rk_tm_copied"], step)
                settle(C)
                for n in range(nl):
                    if n:
                        pe.wait_ge(S["rk_x_ready"], g * 15 + (lx + n))
                        settle(C)
                    for q in range(4):
                        x = rk_x[0:C, q, 0:C] if n else ident[0:C, 0:C]
                        mm = pe.matmul(ps[0:C, 2, q * P:q * P + C], rk_lb[0:C, q, 0, 0:C], x, start=True, stop=True)
                    mm.then_inc(S["rk_lx_ready"], 1)
                    pe.wait_ge(S["rk_lx_masked"], g * 18 + (lv + n + 1))
                    if n:
                        pe.wait_ge(S["rk_xt_ready"], g * 18 + (lv + n))
                    settle(C)
                    for q in range(4):
                        xt = rk_xt[0:C, q, 0:C] if n else ident[0:C, 0:C]
                        y, eye = rk_ym[0:C, q, 0:C], ident[0:C, 0:C]
                        if n < nl - 1:
                            o = ps[0:C, 0, q * P:q * P + C]
                            pe.matmul(o, xt, y, start=True, stop=False)
                            pe.matmul(o, xt, eye, start=False, stop=True)
                        o = ps[0:C, 1, q * P:q * P + C]
                        pe.matmul(o, y, xt, start=True, stop=False)
                        mm = pe.matmul(o, eye, xt, start=False, stop=True)
                    mm.then_inc(S["rk_xx_ready"], 1)
                for q, par, u, p in heads:
                    o = ps[0:C, 4 + par, u * HD:(u + 1) * HD]
                    if c:
                        pe.matmul(o, rk_ar[p:p + HD, u, 0, now], rk_s[p:p + HD, u, :], start=True, stop=False)
                    mm = pe.matmul(o, rk_lk[0:C, q, 0, 0:C], rk_tm[0:C, 4 + u, p:p + HD], start=(c == 0), stop=True)
                mm.then_inc(S["rk_z_ready"], 1)
                pe.wait_ge(S["rk_z_copied"], step)
                pe.wait_ge(S["rk_xt_ready"], g * 18 + (lv + nl))
                settle(C)
                for q in range(4):
                    mm = pe.matmul(ps[0:C, 6, q * HD:(q + 1) * HD], rk_xt[0:C, q, 0:C], rk_z[0:C, q, :],
                                   start=True, stop=True)
                mm.then_inc(S["rk_sa_ready"], 1)
                pe.wait_ge(S["rk_sa_copied"], step)
                settle(0)
                for q, par, u, p in heads:
                    o = ps[p:p + HD, 2 + par, u * P:u * P + C]
                    if c:
                        pe.matmul(o, rk_s[p:p + HD, u, :], rk_ar[p:p + HD, u, 1, now], start=True, stop=False)
                    pe.matmul(o, rk_sa[0:C, q, :], rk_lb[0:C, q, 1, 0:C], start=(c == 0), stop=False)
                    mm = pe.matmul(o, rk_tm[0:C, 4 + u, p:p + HD], rk_lk[0:C, q, 1, 0:C], start=False, stop=True)
                mm.then_inc(S["rk_y_ready"], 1)
                if c < 2:
                    for q, par, u, p in heads:
                        o = ps[p:p + HD, 4 + par, u * HD:(u + 1) * HD]
                        pe.matmul(o, rk_tm[0:C, u, p:p + HD], rk_sa[0:C, q, :], start=True, stop=False)
                        mm = pe.matmul(o, rk_tm[0:C, 2 + u, p:p + HD], rk_tm[0:C, 4 + u, p:p + HD],
                                       start=False, stop=True)
                    mm.then_inc(S["rk_s_ready"], 1)

            def attend(g, pre, steps, o_bank):
                count, chunks = len(steps), steps[-1][1] + 1
                pe.wait_ge(S[pre + "_staged"], g + 1)
                settle(steps[0][3])
                for n, c, t0, C, _, keys, _, parts, first, last in steps:
                    nk = keys.shape[1]
                    for h in range(4):
                        p = HD * (h % 2)
                        mm = pe.matmul(ps[0:C, h, 0:nk], at_q[p:p + HD, h // 2, t0:t0 + C], keys[p:p + HD, :],
                                       start=True, stop=True)
                    mm.then_inc(S[pre + "_logits"], 1)
                    pe.wait_ge(S[pre + "_probs"], g * count + (n + 1))
                    settle(C)
                    for kc, (k0, KC, _) in enumerate(parts):
                        for h in range(4):
                            mm = pe.transpose(ps[0:KC, 4 + kc, h * P:h * P + C], at_p[0:C, h, k0:k0 + KC],
                                              ident[0:C, 0:C])
                    mm.then_inc(S[pre + "_turned_probs"], 1)
                    pe.wait_ge(S[pre + "_probs_copied"], g * count + (n + 1))
                    if first:
                        pe.wait_ge(S[pre + "_o_copied"], g * chunks + (c + 1))
                    settle(C)
                    for h in range(4):
                        p, u = HD * (h % 2), h // 2
                        for kc, (k0, KC, values) in enumerate(parts):
                            mm = pe.matmul(ps[p:p + HD, o_bank(u), u * P:u * P + C], values,
                                           at_pt[0:KC, kc, h, 0:C], start=(first and kc == 0),
                                           stop=(last and kc == len(parts) - 1))
                    if last:
                        mm.then_inc(S[pre + "_o_ready"], 1)

            pe.sem_inc(S["act_emptied"], 2)
            pe.sem_inc(S["dve_emptied"], 2)
            pe.wait_ge(S["consts_loaded"], 32)
            full = slice(0, T)
            pe_norm = lambda n: norm_sum(n, T, full)

            pe_norm(0)
            there = feed_forward(0, 0, T, full)
            linear("ffn_out", lambda k: A[:, k, :], 0, before_k=there)

            pe_norm(1)
            for i, (name, buf) in enumerate((("rk_r", T0), ("rk_k", T2), ("rk_v", T0))):
                pe.wait_ge(S["rk_mixed"], 8 * (i + 1))
                linear(name, lambda k, buf=buf: buf[:, k, :])
            pe.wait_ge(S["rk_mixed"], 32)
            linear("rk_w1", lambda k: T2[:, k, :])
            pe.wait_ge(S["act_emptied"], owners[tiles_done("rk_w1") - 1][1])
            linear("rk_w2", lambda k: rk_lora[:, 0, :])
            pe.wait_ge(S["rk_mixed"], 40)
            linear("rk_a1", lambda k: T0[:, k, :])
            pe.wait_ge(S["act_emptied"], owners[tiles_done("rk_a1") - 1][1])
            linear("rk_a2", lambda k: rk_lora[:, 1, :])
            pe.wait_ge(S["rk_mixed"], 48)
            linear("rk_g1", lambda k: T2[:, k, :])
            pe.wait_ge(S["act_emptied"], owners[tiles_done("rk_g1") - 1][1])
            linear("rk_g2", lambda k: rk_lora[:, 2 + k, :])
            pe.wait_ge(S["rk_kk_squared"], 1)
            pe.wait_ge(S["act_emptied"], owners[tiles_done("rk_g2") - 1][1])
            per_tile(head_ones, lambda i: T1[:, i, :], range(8), T, "rk_kk_summed")
            pe.wait_ge(S["rk_bonus_in"], 1)
            per_tile(head_ones, lambda i: T1[:, i, :], range(8), T, "rk_bonus_summed")
            pe.wait_ge(S["rk_prepared"], 1)
            with pe.Fori(0, 4) as g:
                for c, (t0, C) in enumerate(CHUNKS):
                    rk_chunk(g, c, t0, C, (0, 4, 11)[c], (0, 3, 9)[c])
            pe.wait_ge(S["rk_y_copied"], 13)
            pe.wait_ge(S["rk_state_ready"], 8)
            per_tile(head_ones, lambda i: A[:, 24 + i, :], range(8), T, "rk_y_summed")
            pe.wait_ge(S["rk_y_squared"], 1)
            per_tile(head_ones, lambda i: T1[:, i, :], range(8), T, "rk_y_var")
            pe.wait_ge(S["rk_out_ready"], 1)
            linear("rk_o", lambda k: T0[:, k, :])

            pe_norm(2)
            there = feed_forward(stage_number("ffn", 1), 2, T, full)
            linear("ffn_out", lambda k: A[:, k, :], 1, before_k=there)
            pe_norm(3)
            there = feed_forward(stage_number("ffn", 2), 3, T, full)
            linear("ffn_out", lambda k: A[:, k, :], 2, before_k=there)

            pe_norm(4)
            pe.wait_ge(S["h_ready"], DT * 5)
            linear("at_in", lambda k: H[:, k, :])
            pe.wait_ge(S["ds_squared"], 1)
            per_tile(head_ones, lambda i: A[:, 20 + i, :], range(8), T, "ds_summed")
            pe.wait_ge(S["ds_rooted"], 1)
            per_tile(head_ones, lambda i: A[:, 28 + i, :], range(4), T, "ds_summed")
            pe.wait_ge(S["ds_normed"], 1)
            pe.wait_ge(S["ds_rooted"], 2)
            for i, first, count in ((0, 0, 8), (1, 8, 4), (2, 14, 5)):
                if i:
                    pe.wait_ge(S["ds_roped"], i)
                per_tile(rope_swap, lambda j: A[:, first + j, :], range(count), T, "ds_swapped")
            pe.wait_ge(S["ds_roped"], 3)
            for c, (t0, C) in enumerate(CHUNKS):
                for j in range(2):
                    pe.transpose(ps[0:C, c, j * P:(j + 1) * P], A[:, 12 + j, t0:t0 + C], ident)
                mm = pe.transpose(ps[0:C, c, 2 * P:3 * P], A[:, 19, t0:t0 + C], ident)
            mm.then_inc(S["ds_turned"], 1)
            pe.wait_ge(S["ds_turned_copied"], 1)
            for n, (t0, C) in enumerate(CHUNKS[1:]):
                if n:
                    pe.wait_ge(S["ds_relu"], n)
                for h in range(8):
                    p = HD * (h % 2)
                    mm = pe.matmul(ps[:, h, 0:T], A[p:p + HD, 14 + h // 2, t0:t0 + C], A[p:p + HD, 18, :],
                                   start=True, stop=True)
                mm.then_inc(S["ds_index_ready"], 1)
            pe.wait_ge(S["ds_relu"], 2)
            pe.wait_ge(S["ds_selected"], 2)
            with pe.Fori(0, 4) as g:
                attend(g, "ds", DSA_STEPS, lambda u: 7)
            pe.wait_ge(S["ds_o_copied"], 13)
            linear("at_o", lambda k: T2[:, k, :])
            pe_norm(5)
            there = feed_forward(stage_number("ffn", 3), 5, T, full)
            linear("ffn_out", lambda k: A[:, k, :], 3, before_k=there)

            norm_sum(6, SEQ, TB)
            pe.wait_ge(S["h_ready"], DT * 7)
            linear("ret_in", lambda k: H[:, k, TB], size=SEQ)
            pe.wait_ge(S["act_emptied"], owners[tiles_done("ret_in") - 1][1])
            per_tile(ret_swap, lambda i: A[:, i, TB], range(8), SEQ, "ret_swapped")
            pe.wait_ge(S["ret_roped"], 1)
            for c in range(2):
                for j in range(8):
                    mm = pe.transpose(ps[:, 2 * c + j // 4, (j % 4) * P:(j % 4 + 1) * P],
                                      A[:, 8 + j, N_META + c * P:N_META + (c + 1) * P], ident)
            mm.then_inc(S["ret_v_turned"], 1)
            for h in range(4):
                for kc in range(2):
                    mm = pe.matmul(ps[:, 4 + h, kc * SEQ:(kc + 1) * SEQ],
                                   A[:, 4 + h, N_META + kc * P:N_META + (kc + 1) * P], A[:, h, TB],
                                   start=True, stop=True)
            mm.then_inc(S["ret_scores"], 1)
            pe.wait_ge(S["ret_v_copied"], 1)
            pe.wait_ge(S["ret_masked"], 1)
            for j in range(8):
                for kc in range(2):
                    mm = pe.matmul(ps[:, j, 0:SEQ], ret_vt[:, kc, j, :], ret_st[:, j // 2, kc, :],
                                   start=(kc == 0), stop=(kc == 1))
            mm.then_inc(S["ret_o_ready"], 1)
            pe.wait_ge(S["ret_o_copied"], 1)
            for h in range(4):
                for j in range(2):
                    mm = pe.matmul(ps[:, h, 0:SEQ], ones, A[:, 40 + 2 * h + j, TB], start=(j == 0), stop=(j == 1))
            mm.then_inc(S["ret_summed"], 1)
            pe.wait_ge(S["ret_squared"], 1)
            for h in range(4):
                for j in range(2):
                    mm = pe.matmul(ps[:, h, 0:SEQ], ones, T0[:, 2 * h + j, TB], start=(j == 0), stop=(j == 1))
            mm.then_inc(S["ret_var"], 1)
            pe.wait_ge(S["ret_y_ready"], 1)
            linear("ret_out", lambda k: T0[:, k, TB], size=SEQ)
            linear("ret_mg", lambda k: H[:, k, TB], size=SEQ)
            pe.wait_ge(S["merged"], 1)
            linear("sc_in", lambda k: H[:, k, TB], size=SEQ)
            pe.wait_ge(S["sc_y_ready"], 1)
            linear("sc_out", lambda k: T0[:, k, TB], size=SEQ)
            linear("sc_mg", lambda k: H[:, k, TB], size=SEQ)
            pe.wait_ge(S["merged"], 2)

            linear("nsa_in", lambda k: H[:, k, TB], size=SEQ)
            pe.wait_ge(S["act_emptied"], owners[tiles_done("nsa_in") - 1][1])
            for c in range(2):
                t0 = N_META + c * P
                for j in range(4):
                    pe.transpose(ps[:, 4 + c, j * P:(j + 1) * P], A[:, 24 + j, t0:t0 + P], ident)
                mm = pe.transpose(ps[:, 6, c * P:(c + 1) * P], A[:, 28, t0:t0 + P], ident)
            mm.then_inc(S["ns_turned"], 1)
            pe.wait_ge(S["ns_blocks"], 1)
            linear("cmp_k1", lambda k: ns_blk[:, k, :], size=4 * N_CMP)
            pe.wait_ge(S["act_emptied"], owners[tiles_done("cmp_k1") - 1][1])
            linear("cmp_k2", lambda k: ns_cmp_hid[:, k, :], size=4 * N_CMP)
            pe.wait_ge(S["ns_blocks"], 2)
            pe.wait_ge(S["act_emptied"], owners[tiles_done("cmp_k2") - 1][1])
            linear("cmp_v1", lambda k: ns_blk[:, k, :], size=4 * N_CMP)
            pe.wait_ge(S["act_emptied"], owners[tiles_done("cmp_v1") - 1][1])
            s = stage_number("cmp_v2")
            tile = tiles_before[s]
            bank_free(tile)
            w = [weight_tile(STARTS[s] + k) for k in range(2)]
            assert STARTS[s] % PER < PER - 2
            for g in range(4):
                for k in range(2):
                    mm = pe.matmul(ps[0:N_CMP, tile % 4, g * HD:(g + 1) * HD],
                                   ns_cmp_hid[:, k, g * N_CMP:(g + 1) * N_CMP], w[k][:, 0:HD],
                                   start=(k == 0), stop=(k == 1))
            mm.then_inc(S["linear_ready"], 1)
            pe.wait_ge(S["act_emptied"], owners[tile][1])
            pe.wait_ge(S["ns_turned_copied"], 1)
            with pe.Fori(0, 4) as g:
                attend(g, "ns", NSA_STEPS, lambda u: 7 - u)
            pe.wait_ge(S["ns_o_copied"], 9)
            linear("nsa_out", lambda k: T1[:, k, TB], size=SEQ)
            linear("nsa_mg", lambda k: H[:, k, TB], size=SEQ)
            pe.wait_ge(S["merged"], 3)
            linear("mix_out", lambda k: T2[:, k, TB], size=SEQ)
            norm_sum(7, SEQ, TB)
            there = feed_forward(stage_number("ffn2"), 7, SEQ, TB)
            linear("ffn_out", lambda k: A[:, k, TB], 4, size=SEQ, before_k=there)
            norm_sum(8, SEQ, TB)

        @block.scalar
        def _(act):
            def copy(o, i, scale=1.0):
                return act.activation(o, i, ACT.Copy, scale=scale)

            def linear(name, put, func=lambda i: ACT.Copy, bias=None, nth=0, size=T):
                s = stage_number(name, nth)
                for i in range(STAGES[s][2]):
                    tile = tiles_before[s] + i
                    act.wait_ge(S["linear_ready"], tile + 1)
                    kw = {} if bias is None else {"bias": bias[:, i:i + 1]}
                    act.activation(put(i), ps[:, tile % 4, 0:size], func(i), **kw).then_inc(S["act_emptied"], 1)

            def norm(n, size, tokens):
                if n:
                    act.wait_ge(S["x_updated"], n)
                else:
                    act.wait_ge(S["x_loaded"], 16)
                act.activation(T0[:, :, tokens], X[:, :, tokens], ACT.Square).then_inc(S["squares_ready"], 1)
                act.wait_ge(S["square_sum_ready"], n + 1)
                if n:
                    act.wait_ge(S["h_ready"], DT * n)
                act.activation(rms[:, 0, 0:size], ps[:, 4, 0:size], ACT.Sqrt, bias=eps(EPS_RMS), scale=1.0 / D
                               ).then_inc(S["rms_ready"], 1)

            def feed_forward(s):
                base, d = tiles_before[s], dve_before[s]
                with act.Fori(0, FT // 2) as turn:
                    for p in range(2):
                        act.wait_ge(S["linear_ready"], turn * 4 + (base + 2 * p + 1))
                        act.wait_ge(S["dve_emptied"], turn * 2 + (d + p - 1))
                        act.activation(silu_out[:, p, :], ps[:, (base + 2 * p) % 4, 0:T], ACT.Silu
                                       ).then_inc(S["act_emptied"], 1)

            def conv_feed_forward(s):
                base = tiles_before[s]
                with act.Fori(0, FT // 2) as turn:
                    for p in range(2):
                        act.wait_ge(S["conved"], turn * 4 + (2 * p + 2))
                        for half in range(2):
                            act.wait_ge(S["linear_ready"], turn * 4 + (base + 2 * p + half + 1))
                            copy(conv_in[:, p, half, TB], ps[:, (base + 2 * p + half) % 4, 0:SEQ]
                                 ).then_inc(S["act_emptied"], 1)
                        act.wait_ge(S["conved"], turn * 4 + (2 * p + 5))
                        act.wait_ge(S["hidden_ready"], turn * 2 + (p + 1))
                        act.activation(silu_out[:, p, TB], conv_out[:, p, 0, TB], ACT.Silu).then_inc(S["silu_ready"], 1)

            def rk_chunk(g, c, t0, C, lv):
                step = g * 3 + (c + 1)
                act.wait_ge(S["rk_turned"], step)
                copy(rk_tm[0:C, 0:4, :], ps[0:C, 0, :].rearrange("p (a t) -> p a t", a=4))
                copy(rk_tm[0:C, 4:6, :], ps[0:C, 1, 0:256].rearrange("p (a t) -> p a t", a=2)
                     ).then_inc(S["rk_tm_copied"], 1)
                for n in range(C.bit_length() - 1):
                    act.wait_ge(S["rk_xx_ready"], g * 18 + (lv + n + 1))
                    copy(rk_xt[0:C, :, 0:C], ps[0:C, 1, :].rearrange("p (a t) -> p a t", a=4)[:, :, 0:C]
                         ).then_inc(S["rk_xt_ready"], 1)
                act.wait_ge(S["rk_sa_ready"], step)
                copy(rk_sa[0:C, :, :], ps[0:C, 6, 0:256].rearrange("p (a t) -> p a t", a=4)
                     ).then_inc(S["rk_sa_copied"], 1)
                act.wait_ge(S["rk_y_ready"], step)
                for par in range(2):
                    p = HD * par
                    ins = copy(A[p:p + HD, bass.ds(g * 2 + 24, 2), t0:t0 + C],
                               ps[p:p + HD, 2 + par, 0:256].rearrange("p (a t) -> p a t", a=2)[:, :, 0:C])
                ins.then_inc(S["rk_y_copied"], 1)

            def attend(g, pre, steps, put):
                count = len(steps)
                chunks = steps[-1][1] + 1
                for n, c, t0, C, _, keys, _, parts, first, last in steps:
                    nk = keys.shape[1]
                    act.wait_ge(S[pre + "_max"], g * count + (n + 1))
                    for h in range(4):
                        ins = act.activation(at_p[0:C, h, 0:nk], at_p[0:C, h, 0:nk], ACT.Exp, bias=at_max[0:C, h:h + 1],
                                             accum_out=at_sum[0:C, h:h + 1])
                    ins.then_inc(S[pre + "_exp"], 1)
                    act.wait_ge(S[pre + "_turned_probs"], g * count + (n + 1))
                    for kc, (k0, KC, _) in enumerate(parts):
                        ins = copy(at_pt[0:KC, kc, :, 0:C],
                                   ps[0:KC, 4 + kc, :].rearrange("p (a t) -> p a t", a=4)[:, :, 0:C])
                    ins.then_inc(S[pre + "_probs_copied"], 1)
                    if last:
                        act.wait_ge(S[pre + "_o_ready"], g * chunks + (c + 1))
                        put(g, t0, C).then_inc(S[pre + "_o_copied"], 1)

            full = slice(0, T)
            act.wait_ge(S["consts_loaded"], 32)
            norm(0, T, full)
            feed_forward(0)
            norm(1, T, full)
            linear("rk_r", lambda i: A[:, i, :])
            linear("rk_k", lambda i: A[:, 8 + i, :])
            linear("rk_v", lambda i: A[:, 16 + i, :])
            linear("rk_w1", lambda i: rk_lora[:, 0, :], lambda i: ACT.Tanh)
            linear("rk_w2", lambda i: A[:, 24 + i, :], lambda i: ACT.Sigmoid, param("w0"))
            linear("rk_a1", lambda i: rk_lora[:, 1, :])
            linear("rk_a2", lambda i: A[:, 32 + i, :], lambda i: ACT.Sigmoid, param("a0"))
            linear("rk_g1", lambda i: rk_lora[:, 2 + i, :], lambda i: ACT.Sigmoid)
            linear("rk_g2", lambda i: A[:, 40 + i, :])
            act.wait_ge(S["rk_kk_clamped"], 1)
            act.activation(T1[:, :, :], T1[:, :, :], ACT.Sqrt).then_inc(S["rk_kk_rooted"], 1)
            act.wait_ge(S["rk_logs_ready"], 1)
            act.activation(T1[:, :, :], T1[:, :, :], ACT.Exp).then_inc(S["rk_exps_ready"], 1)
            act.activation(A[:, 24:32, :], T2[:, :, :], ACT.Exp).then_inc(S["rk_exps_ready"], 1)
            act.drain()
            act.activation(T2[:, :, :], T2[:, :, :], ACT.Exp, scale=-1.0).then_inc(S["rk_exps_ready"], 1)
            act.activation(rk_mid_exp[:, :, :], rk_mid[:, :, :], ACT.Exp).then_inc(S["rk_exps_ready"], 1)
            act.sem_inc(S["rk_y_copied"], 1)
            with act.Fori(0, 4) as g:
                for c, (t0, C) in enumerate(CHUNKS):
                    rk_chunk(g, c, t0, C, (0, 4, 11)[c])
            act.wait_ge(S["rk_y_var"], 1)
            act.activation(T1[:, :, :], ps[:, :, 0:T], ACT.Sqrt, bias=eps(EPS_LNX), scale=1.0 / HD
                           ).then_inc(S["rk_y_rooted"], 1)
            norm(2, T, full)
            feed_forward(stage_number("ffn", 1))
            norm(3, T, full)
            feed_forward(stage_number("ffn", 2))
            norm(4, T, full)
            linear("at_in", lambda i: A[:, i, :])
            for n, (first, count) in enumerate(((20, 8), (28, 4))):
                act.wait_ge(S["ds_summed"], n + 1)
                act.activation(A[:, first:first + count, :], ps[:, 0:count, 0:T], ACT.Sqrt, bias=eps(EPS_RMS),
                               scale=1.0 / HD).then_inc(S["ds_rooted"], 1)
            act.wait_ge(S["ds_turned"], 1)
            for c, (t0, C) in enumerate(CHUNKS):
                ins = copy(at_vtm[0:C, c, :], ps[0:C, c, 0:256])
                if c:
                    ins = copy(ds_wi[:, c - 1, :], ps[:, c, 256:264], scale=8 ** -0.5 * HD ** -0.5)
            ins.then_inc(S["ds_turned_copied"], 1)
            for n in range(2):
                act.wait_ge(S["ds_index_ready"], n + 1)
                if n:
                    act.wait_ge(S["ds_scored"], n)
                act.activation(T0[:, :, :], ps[:, :, 0:T], ACT.Relu).then_inc(S["ds_relu"], 1)
            act.sem_inc(S["ds_o_copied"], 1)

            def put_ds(g, t0, C):
                return copy(T2[:, bass.ds(g * 2, 2), t0:t0 + C],
                            ps[:, 7, 0:256].rearrange("p (a t) -> p a t", a=2)[:, :, 0:C])

            with act.Fori(0, 4) as g:
                attend(g, "ds", DSA_STEPS, put_ds)
            norm(5, T, full)
            feed_forward(stage_number("ffn", 3))

            norm(6, SEQ, TB)
            act.dma_start(ret_decay, decay).then_inc(S["decay_loaded"], 16)
            linear("ret_in", lambda i: A[:, i, TB], lambda i: ACT.Silu if i >= 16 else ACT.Copy, size=SEQ)
            act.wait_ge(S["ret_v_turned"], 1)
            copy(ret_vt.rearrange("p c j v -> p (c j v)"), ps[:, 0:4, :].rearrange("p a b -> p (a b)")
                 ).then_inc(S["ret_v_copied"], 1)
            act.wait_ge(S["ret_o_ready"], 1)
            copy(A[:, 40:48, TB], ps[:, :, 0:SEQ]).then_inc(S["ret_o_copied"], 1)
            act.wait_ge(S["ret_var"], 1)
            act.activation(T1[:, 0:4, TB], ps[:, 0:4, 0:SEQ], ACT.Sqrt, bias=eps(EPS_RET), scale=1.0 / SEQ
                           ).then_inc(S["ret_rooted"], 1)
            linear("ret_out", lambda i: A[:, i, TB], size=SEQ)
            linear("ret_mg", lambda i: A[:, 8 + i, TB], lambda i: ACT.Sigmoid, size=SEQ)
            act.wait_ge(S["merged"], 1)
            linear("sc_in", lambda i: A[:, i, TB], size=SEQ)
            linear("sc_out", lambda i: A[:, 24 + i, TB], size=SEQ)
            linear("sc_mg", lambda i: A[:, 32 + i, TB], lambda i: ACT.Sigmoid, size=SEQ)
            act.wait_ge(S["merged"], 2)
            linear("nsa_in", lambda i: A[:, i, TB], lambda i: ACT.Sigmoid if i == 28 else ACT.Copy, size=SEQ)
            act.wait_ge(S["ns_turned"], 1)
            for c in range(2):
                copy(at_vtm[:, 2 * c:2 * c + 2, :], ps[:, 4 + c, :].rearrange("p (a v) -> p a v", a=2))
                ins = copy(ns_gate[:, c, :], ps[:, 6, c * P:c * P + 48])
            ins.then_inc(S["ns_turned_copied"], 1)
            linear("cmp_k1", lambda i: ns_cmp_hid[:, i, :], lambda i: ACT.Gelu_apprx_tanh, size=4 * N_CMP)
            linear("cmp_k2", lambda i: ns_cmp_k[:, :], size=4 * N_CMP)
            linear("cmp_v1", lambda i: ns_cmp_hid[:, i, :], lambda i: ACT.Gelu_apprx_tanh, size=4 * N_CMP)
            tile = tiles_before[stage_number("cmp_v2")]
            act.wait_ge(S["linear_ready"], tile + 1)
            copy(ns_cmp_v[0:N_CMP, :, :], ps[0:N_CMP, tile % 4, 0:256].rearrange("p (a v) -> p a v", a=4)
                 ).then_inc(S["act_emptied"], 1)
            act.sem_inc(S["ns_o_copied"], 1)

            def put_ns(g, t0, C):
                copy(T1[:, bass.ds(g * 2, 1), t0:t0 + C], ps[:, 7:8, 0:C])
                return copy(T1[:, bass.ds(g * 2 + 1, 1), t0:t0 + C], ps[:, 6:7, P:P + C])

            with act.Fori(0, 4) as g:
                attend(g, "ns", NSA_STEPS, put_ns)
            linear("nsa_out", lambda i: A[:, i, TB], size=SEQ)
            linear("nsa_mg", lambda i: A[:, 8 + i, TB], lambda i: ACT.Sigmoid, size=SEQ)
            norm(7, SEQ, TB)
            conv_feed_forward(stage_number("ffn2"))
            norm(8, SEQ, TB)

        @block.vector
        def _(dve):
            def tt(o, a, b, op):
                return dve.tensor_tensor(o, a, b, op)

            def stt(o, a, scalar, b, op0, op1):
                return dve.scalar_tensor_tensor(out=o, in0=a, scalar=scalar, in1=b, op0=op0, op1=op1)

            def tiles_of(v, n, size):
                return v.unsqueeze(2).to_broadcast([P, n, size])

            def tokens_of(v, n):
                return v.unsqueeze(1).to_broadcast([v.shape[0], n, v.shape[1]])

            def norm(n, size, tokens, gain, done="h_ready"):
                dve.wait_ge(S["rms_ready"], n + 1)
                dve.reciprocal(rms[:, 1, 0:size], rms[:, 0, 0:size])
                dve.drain()
                for k in range(DT):
                    stt(H[:, k, tokens], X[:, k, tokens], gain[:, k:k + 1], rms[:, 1, 0:size], ALU.mult, ALU.mult
                        ).then_inc(S[done], 1)

            def feed_forward(s):
                base, a = tiles_before[s], act_before[s]
                with dve.Fori(0, FT // 2) as turn:
                    for p in range(2):
                        dve.wait_ge(S["linear_ready"], turn * 4 + (base + 2 * p + 2))
                        dve.wait_ge(S["act_emptied"], turn * 2 + (a + p + 1))
                        tt(A[:, bass.ds(turn * 2 + p, 1), :], ps[:, (base + 2 * p + 1) % 4:(base + 2 * p + 1) % 4 + 1, 0:T],
                           silu_out[:, p:p + 1, :], ALU.mult).then_inc(S["dve_emptied"], 1)

            def conv_feed_forward(s):
                a = act_before[s]
                at = PARAMS["ffn_conv"][0]
                dve.memset(conv_in[:, :, :, N_META - 2:N_META], 0.0)
                dve.drain()
                dve.sem_inc(S["conved"], 4)
                dve.sem_inc(S["hidden_ready"], 2)
                with dve.Fori(0, FT // 2) as turn:
                    for p in range(2):
                        for half in range(2):
                            tap = lambda n: par[:, bass.ds(turn * 2 + (at + 44 * n + 22 * half + p), 1)]
                            src, dst = conv_in[:, p, half, :], conv_out[:, p, half, TB]
                            dve.wait_ge(S["act_emptied"], turn * 4 + (a + 2 * p + half + 1))
                            dve.tensor_scalar(dst, src[:, TB], tap(2), None, ALU.mult)
                            dve.drain()
                            stt(dst, src[:, N_META - 1:T - 1], tap(1), dst, ALU.mult, ALU.add)
                            dve.drain()
                            stt(dst, src[:, N_META - 2:T - 2], tap(0), dst, ALU.mult, ALU.add
                                ).then_inc(S["conved"], 1)
                        dve.drain()
                        dve.wait_ge(S["silu_ready"], turn * 2 + (p + 1))
                        tt(A[:, bass.ds(turn * 2 + p, 1), TB], silu_out[:, p:p + 1, TB], conv_out[:, p:p + 1, 1, TB],
                           ALU.mult).then_inc(S["hidden_ready"], 1)

            def residual(name, nth=0, size=T, tokens=slice(0, T), factor=1.0):
                s = stage_number(name, nth)
                for i in range(DT):
                    tile = tiles_before[s] + i
                    dve.wait_ge(S["linear_ready"], tile + 1)
                    stt(X[:, i, tokens], ps[:, tile % 4, 0:size], factor, X[:, i, tokens], ALU.mult, ALU.add
                        ).then_inc(S["dve_emptied"], 1)
                dve.drain()
                dve.sem_inc(S["x_updated"], 1)

            def rk_prepare():
                dve.drain()
                tt(T1[:, :, 1:T], H[:, :, 0:T - 1], H[:, :, 1:T], ALU.subtract)
                dve.tensor_scalar(T1[:, :, 0:1], H[:, :, 0:1], -1.0, None, ALU.mult)
                dve.drain()
                names = ("rk_r", "rk_k", "rk_v", "rk_w1", "rk_a1", "rk_g1")
                for i, m in enumerate((0, 2, 3, 1, 4, 5)):
                    if i >= 2:
                        dve.wait_ge(S["linear_ready"], tiles_done(names[i - 2]))
                    for k in range(DT):
                        stt((T0, T2)[i % 2][:, k, :], T1[:, k, :], param("mix", m)[:, k:k + 1], H[:, k, :],
                            ALU.mult, ALU.add).then_inc(S["rk_mixed"], 1)
                R, K, V, W, B, G = (A[:, 8 * i:8 * i + 8, :] for i in range(6))
                dve.wait_ge(S["act_emptied"], owners[tiles_done("rk_g2") - 1][1])
                tt(T0[:, :, :], K, tiles_of(param("k_k"), DT, T), ALU.mult)
                dve.drain()
                tt(T1[:, :, :], T0[:, :, :], T0[:, :, :], ALU.mult).then_inc(S["rk_kk_squared"], 1)
                tt(T2[:, :, :], R, tiles_of(param("r_k"), DT, T), ALU.mult)
                dve.wait_ge(S["rk_kk_summed"], 1)
                dve.tensor_scalar(T1[:, :, :], ps[:, :, 0:T], 1e-24, None, ALU.max).then_inc(S["rk_kk_clamped"], 1)
                stt(H[:, :, :], B, -1.0, tiles_of(param("k_a"), DT, T), ALU.add, ALU.mult)
                dve.drain()
                stt(K, H[:, :, :], 1.0, K, ALU.add, ALU.mult)
                dve.wait_ge(S["rk_kk_rooted"], 1)
                dve.reciprocal(T1[:, :, :], T1[:, :, :])
                dve.drain()
                tt(T0[:, :, :], T0[:, :, :], T1[:, :, :], ALU.mult)
                dve.drain()
                tt(B, B, T0[:, :, :], ALU.mult)
                tt(T1[:, :, :], T2[:, :, :], K, ALU.mult).then_inc(S["rk_bonus_in"], 1)
                dve.tensor_scalar(W, W, -float(np.exp(-0.5)), None, ALU.mult)
                dve.drain()
                for k in range(DT):
                    dve.tensor_tensor_scan(T2[:, k, :], const("reset"), A[:, 24 + k, :], 0.0, ALU.mult, ALU.add)
                dve.wait_ge(S["rk_bonus_summed"], 1)
                tt(H[:, :, :], ps[:, :, 0:T], V, ALU.mult)
                dve.drain()
                for c, (t0, C) in enumerate(CHUNKS):
                    dve.tensor_copy(rk_mid[:, c, :], T2[:, :, t0 + C // 2])
                dve.drain()
                for c, (t0, C) in enumerate(CHUNKS):
                    tt(T2[:, :, t0:t0 + C], T2[:, :, t0:t0 + C], tiles_of(rk_mid[:, c, :], DT, C), ALU.subtract)
                dve.drain()
                tt(T1[:, :, :], T2[:, :, :], W, ALU.subtract)
                dve.drain()
                dve.sem_inc(S["rk_logs_ready"], 1)
                dve.wait_ge(S["rk_exps_ready"], 1)
                stt(T0[:, :, :], T0[:, :, :], -1.0, T1[:, :, :], ALU.mult, ALU.mult)
                dve.wait_ge(S["rk_exps_ready"], 2)
                tt(R, R, W, ALU.mult)
                for c, (t0, C) in enumerate(CHUNKS):
                    dve.tensor_copy(rk_end[:, c, :], A[:, 24:32, t0 + C - 1])
                dve.wait_ge(S["rk_exps_ready"], 3)
                tt(B, B, T2[:, :, :], ALU.mult)
                tt(K, K, T2[:, :, :], ALU.mult)
                dve.wait_ge(S["rk_exps_ready"], 4)
                dve.drain()
                tt(rk_end[:, 0:2, :], rk_end[:, 0:2, :], rk_mid_exp[:, 1:3, :], ALU.mult)
                dve.drain()
                dve.sem_inc(S["rk_prepared"], 1)

            def rk_chunk(g, c, t0, C, lv):
                step = g * 3 + (c + 1)
                nl = C.bit_length() - 1
                dve.wait_ge(S["rk_products_ready"], step)
                mask = tri[0:C, :, 0:C].unsqueeze(1).to_broadcast([C, 4, 2, C])
                for bank, o in ((2, rk_lb), (4, rk_lk)):
                    v = ps[0:C, bank:bank + 2, :].rearrange("p b (u a t) -> p (b u) a t", u=2, a=2)[:, :, :, 0:C]
                    ins = tt(o[0:C, :, :, 0:C], v, mask, ALU.mult)
                ins.then_inc(S["rk_masked"], 1)
                for n in range(nl):
                    dve.wait_ge(S["rk_lx_ready"], g * 18 + (lv + n + 1))
                    tt(rk_ym[0:C, :, 0:C], ps[0:C, 2, :].rearrange("p (a t) -> p a t", a=4)[:, :, 0:C],
                       tokens_of(level[0:C, n, 0:C], 4), ALU.mult).then_inc(S["rk_lx_masked"], 1)
                    if n < nl - 1:
                        dve.wait_ge(S["rk_xx_ready"], g * 18 + (lv + n + 1))
                        dve.tensor_copy(rk_x[0:C, :, 0:C], ps[0:C, 0, :].rearrange("p (a t) -> p a t", a=4)[:, :, 0:C]
                                        ).then_inc(S["rk_x_ready"], 1)
                dve.wait_ge(S["rk_z_ready"], step)
                dve.tensor_copy(rk_z[0:C, :, :].rearrange("p (b u) v -> p b (u v)", b=2), ps[0:C, 4:6, 0:P]
                                ).then_inc(S["rk_z_copied"], 1)
                if c < 2:
                    dve.wait_ge(S["rk_s_ready"], g * 2 + (c + 1))
                    for par in range(2):
                        p = slice(HD * par, HD * par + HD)
                        v = ps[p, 4 + par, 0:P].rearrange("p (u v) -> p u v", u=2)
                        scale = rk_sc[p, c, :].unsqueeze(2).to_broadcast([HD, 2, HD])
                        if c:
                            tt(rk_s[p, :, :], v, rk_s[p, :, :], ALU.add)
                            dve.drain()
                            ins = tt(rk_s[p, :, :], rk_s[p, :, :], scale, ALU.mult)
                        else:
                            ins = tt(rk_s[p, :, :], v, scale, ALU.mult)
                    ins.then_inc(S["rk_state_ready"], 1)

            def rk_stage(g):
                dve.wait_ge(S["rk_y_copied"], g * 3 + 1)
                for i, src in enumerate((T0[:, bass.ds(g * 2, 2), :], A[:, bass.ds(g * 2, 2), :])):
                    dve.tensor_copy(rk_ar[:, :, i, :], src)
                for i, first in enumerate((32, 8, 16)):
                    dve.tensor_copy(rk_bkv[:, i, :, :], A[:, bass.ds(g * 2 + first, 2), :])
                dve.tensor_copy(rk_sc[:, :, :], rk_end[:, 0:2, bass.ds(g * 2, 2)])
                dve.drain()
                dve.sem_inc(S["rk_staged"], 1)

            def rk_finish():
                Y = A[:, 24:32, :]
                dve.wait_ge(S["rk_y_summed"], 1)
                stt(Y, ps[:, :, 0:T], -1.0 / HD, Y, ALU.mult, ALU.add)
                dve.drain()
                tt(T1[:, :, :], Y, Y, ALU.mult).then_inc(S["rk_y_squared"], 1)
                dve.wait_ge(S["rk_y_rooted"], 1)
                dve.reciprocal(T1[:, :, :], T1[:, :, :])
                dve.drain()
                tt(Y, Y, T1[:, :, :], ALU.mult)
                dve.drain()
                for k in range(DT):
                    dve.tensor_scalar(A[:, 24 + k, :], A[:, 24 + k, :], param("lnx_g")[:, k:k + 1],
                                      param("lnx_b")[:, k:k + 1], ALU.mult, ALU.add)
                dve.drain()
                tt(Y, Y, H[:, :, :], ALU.add)
                dve.drain()
                tt(T0[:, :, :], Y, A[:, 40:48, :], ALU.mult).then_inc(S["rk_out_ready"], 1)

            def rope(first, count, swapped):
                tt(T0[:, 0:count, :], ps[:, 0:count, 0:T], tokens_of(const("sin"), count), ALU.mult)
                x = A[:, first:first + count, :]
                tt(x, x, tokens_of(const("cos"), count), ALU.mult)
                dve.drain()
                tt(x, x, T0[:, 0:count, :], ALU.add).then_inc(S[swapped], 1)

            def attend(g, pre, steps, gates):
                count = len(steps)
                for n, c, t0, C, branch, keys, bias, parts, first, last in steps:
                    nk = keys.shape[1]
                    p = at_p[0:C, :, 0:nk]
                    dve.wait_ge(S[pre + "_logits"], g * count + (n + 1))
                    stt(p, ps[0:C, 0:4, 0:nk], HD ** -0.5, tokens_of(bias[0:C, :], 4), ALU.mult, ALU.add)
                    dve.drain()
                    dve.tensor_reduce(at_max[0:C, :], p, AX_X, ALU.max, negate=True).then_inc(S[pre + "_max"], 1)
                    dve.wait_ge(S[pre + "_exp"], g * count + (n + 1))
                    dve.reciprocal(at_inv[0:C, :], at_sum[0:C, :])
                    dve.drain()
                    if gates:
                        tt(at_inv[0:C, :], at_inv[0:C, :],
                           at_gg[:, c, :].rearrange("p (h b) -> p b h", b=3)[:, branch, :], ALU.mult)
                        dve.drain()
                    tt(p, p, at_inv[0:C, :].unsqueeze(2).to_broadcast([C, 4, nk]), ALU.mult
                       ).then_inc(S[pre + "_probs"], 1)

            def ds_select(n):
                c = n + 1
                score, a, b = T2[:, 0, :], T2[:, 1, :], T2[:, 2, :]
                dve.wait_ge(S["ds_relu"], n + 1)
                dve.tensor_scalar(score, T0[:, 0, :], ds_wi[:, n, 0:1], None, ALU.mult)
                for h in range(1, 8):
                    dve.drain()
                    ins = stt(score, T0[:, h, :], ds_wi[:, n, h:h + 1], score, ALU.mult, ALU.add)
                ins.then_inc(S["ds_scored"], 1)
                dve.drain()
                tt(score, score, const("causal")[:, c, :], ALU.mult)
                dve.drain()
                tt(a, score, const("neg")[:, c, :], ALU.add)
                for _ in range(8):
                    dve.drain()
                    dve.max(ds_top[:, :], a)
                    dve.drain()
                    dve.match_replace(b, ds_top[:, :], a, -3e38)
                    a, b = b, a
                dve.drain()
                stt(b, a, -2e38, const("causal")[:, c, :], ALU.is_lt, ALU.mult)
                dve.drain()
                dve.tensor_scalar(T1[:, c, :], b, -NEG, NEG, ALU.mult, ALU.add).then_inc(S["ds_selected"], 1)

            full = slice(0, T)
            dve.wait_ge(S["consts_loaded"], 32)
            norm(0, T, full, param("norm", 0))
            feed_forward(0)
            residual("ffn_out", 0, factor=0.5)
            norm(1, T, full, param("norm", 1))
            rk_prepare()
            with dve.Fori(0, 4) as g:
                rk_stage(g)
                for c, (t0, C) in enumerate(CHUNKS):
                    rk_chunk(g, c, t0, C, (0, 4, 11)[c])
            rk_finish()
            residual("rk_o")
            norm(2, T, full, param("norm", 2))
            feed_forward(stage_number("ffn", 1))
            residual("ffn_out", 1, factor=0.5)
            norm(3, T, full, param("norm", 3))
            feed_forward(stage_number("ffn", 2))
            residual("ffn_out", 2, factor=0.5)
            norm(4, T, full, param("norm", 4))
            dve.wait_ge(S["act_emptied"], owners[tiles_done("at_in") - 1][1])
            tt(A[:, 20:32, :], A[:, 0:12, :], A[:, 0:12, :], ALU.mult).then_inc(S["ds_squared"], 1)
            dve.wait_ge(S["ds_rooted"], 2)
            dve.reciprocal(A[:, 20:32, :], A[:, 20:32, :])
            dve.drain()
            stt(A[:, 0:8, :], A[:, 0:8, :], column("q_g"), A[:, 20:28, :], ALU.mult, ALU.mult)
            stt(A[:, 8:12, :], A[:, 8:12, :], column("k_g"), A[:, 28:32, :], ALU.mult, ALU.mult
                ).then_inc(S["ds_normed"], 1)
            for n, (first, count) in enumerate(((0, 8), (8, 4), (14, 5))):
                dve.wait_ge(S["ds_swapped"], n + 1)
                dve.drain()
                rope(first, count, "ds_roped")
            dve.tensor_copy(T1[:, 0, :], const("neg")[:, 0, :])
            dve.wait_ge(S["ds_turned_copied"], 1)
            for n in range(2):
                ds_select(n)
            with dve.Fori(0, 4) as g:
                dve.wait_ge(S["ds_o_copied"], g * 3 + 1)
                dve.tensor_copy(at_q[:, :, :], A[:, bass.ds(g * 2, 2), :])
                dve.tensor_copy(at_kg[:, 0:1, :], A[:, bass.ds(g + 8, 1), :])
                dve.tensor_copy(at_vg[0:N_META, 0:1, :], at_vtm[0:N_META, 0:1, bass.ds(g * HD, HD)])
                dve.tensor_copy(at_vg[:, 1:3, :], at_vtm[:, 1:3, bass.ds(g * HD, HD)])
                dve.drain()
                dve.sem_inc(S["ds_staged"], 1)
                attend(g, "ds", DSA_STEPS, False)
            residual("at_o")
            norm(5, T, full, param("norm", 5))
            feed_forward(stage_number("ffn", 3))
            residual("ffn_out", 3, factor=0.5)

            norm(6, SEQ, TB, param("norm2"))
            dve.wait_ge(S["ret_swapped"], 1)
            tt(T0[:, :, TB], ps[:, :, 0:SEQ], tokens_of(const("ret_sin"), DT), ALU.mult)
            tt(A[:, 0:8, TB], A[:, 0:8, TB], tokens_of(const("ret_cos"), DT), ALU.mult)
            dve.drain()
            tt(A[:, 0:8, TB], A[:, 0:8, TB], T0[:, :, TB], ALU.add).then_inc(S["ret_roped"], 1)
            dve.wait_ge(S["ret_scores"], 1)
            dve.wait_ge(S["decay_loaded"], 16)
            tt(ret_st.rearrange("p h c q -> p (h c q)"), ps[:, 4:8, :].rearrange("p a b -> p (a b)"), ret_decay,
               ALU.mult).then_inc(S["ret_masked"], 1)
            dve.wait_ge(S["ret_summed"], 1)
            pair = lambda v, j: v.rearrange("p (h j) t -> p h j t", j=2)[:, :, j, :]
            for j in range(2):
                o = pair(A[:, 40:48, TB], j)
                stt(o, ps[:, 0:4, 0:SEQ], -1.0 / SEQ, o, ALU.mult, ALU.add)
            dve.drain()
            tt(T0[:, :, TB], A[:, 40:48, TB], A[:, 40:48, TB], ALU.mult).then_inc(S["ret_squared"], 1)
            dve.wait_ge(S["ret_rooted"], 1)
            dve.reciprocal(T1[:, 4:8, TB], T1[:, 0:4, TB])
            dve.drain()
            for j in range(2):
                o = pair(A[:, 40:48, TB], j)
                tt(o, o, T1[:, 4:8, TB], ALU.mult)
            dve.drain()
            for k in range(DT):
                ins = stt(T0[:, k, TB], A[:, 40 + k, TB], param("ret_norm")[:, k:k + 1], A[:, 16 + k, TB],
                          ALU.mult, ALU.mult)
            ins.then_inc(S["ret_y_ready"], 1)
            dve.wait_ge(S["act_emptied"], owners[tiles_done("ret_mg") - 1][1])
            tt(T2[:, :, TB], A[:, 0:8, TB], A[:, 8:16, TB], ALU.mult).then_inc(S["merged"], 1)
            dve.wait_ge(S["act_emptied"], owners[tiles_done("sc_in") - 1][1])
            tt(A[:, 8:16, TB], A[:, 8:16, TB], A[:, 16:24, TB], ALU.mult)
            dve.memset(A[:, 8:16, N_META - 2:N_META], 0.0)
            for tap in (2, 1, 0):
                dve.drain()
                for k in range(DT):
                    w = param("sc_conv", tap)[:, k:k + 1]
                    src = A[:, 8 + k, N_META - 2 + tap:T - 2 + tap]
                    if tap == 2:
                        dve.tensor_scalar(T0[:, k, TB], src, w, None, ALU.mult)
                    else:
                        stt(T0[:, k, TB], src, w, T0[:, k, TB], ALU.mult, ALU.add)
            dve.drain()
            tt(T0[:, :, TB], T0[:, :, TB], A[:, 0:8, TB], ALU.mult).then_inc(S["sc_y_ready"], 1)
            dve.wait_ge(S["act_emptied"], owners[tiles_done("sc_mg") - 1][1])
            tt(A[:, 24:32, TB], A[:, 24:32, TB], A[:, 32:40, TB], ALU.mult)
            dve.drain()
            tt(T2[:, :, TB], T2[:, :, TB], A[:, 24:32, TB], ALU.add).then_inc(S["merged"], 1)
            dve.wait_ge(S["act_emptied"], owners[tiles_done("nsa_in") - 1][1])
            for kv in range(2):
                if kv:
                    dve.wait_ge(S["linear_ready"], tiles_done("cmp_k1"))
                for half in range(2):
                    p = slice(HD * half, HD * half + HD)
                    for m0 in range(2):
                        for g in range(4):
                            src = A[p, 8 + 4 * kv + g, TB].rearrange("p (c l) -> p l c", l=16)
                            o = ns_blk[p, 8 * m0:8 * m0 + 8, g * N_CMP:(g + 1) * N_CMP]
                            at = PARAMS["cmp_pos"][0] + 16 * kv + 8 * m0
                            pos = par[p, at:at + 8].unsqueeze(2).to_broadcast([HD, 8, N_CMP])
                            ins = tt(o, src[:, half::2, m0:m0 + N_CMP], pos, ALU.add)
                ins.then_inc(S["ns_blocks"], 1)
            dve.wait_ge(S["ns_turned_copied"], 1)
            for c in range(2):
                at = CONSTS["any_cmp"][0] + c
                o = ns_gate[:, c, :].rearrange("p (h b) -> p b h", b=3)[:, 0, :]
                dve.tensor_scalar(o, o, con[:, at:at + 1], None, ALU.mult)
            dve.wait_ge(S["act_emptied"], owners[tiles_done("cmp_v2") - 1][1])
            dve.drain()
            with dve.Fori(0, 4) as g:
                dve.wait_ge(S["ns_o_copied"], g * 2 + 1)
                dve.tensor_copy(at_q[:, :, TB], A[:, bass.ds(g * 2, 2), TB])
                for b in range(2):
                    dve.tensor_copy(at_kg[:, b:b + 1, TB], A[:, bass.ds(g + (16 + 4 * b), 1), TB])
                dve.tensor_copy(at_vg[:, 0:4, :], at_vtm[:, :, bass.ds(g * HD, HD)])
                dve.tensor_copy(ns_kc[:, :], ns_cmp_k[:, bass.ds(g * N_CMP, N_CMP)])
                dve.tensor_copy(ns_vc[0:N_CMP, :], ns_cmp_v[0:N_CMP, bass.ds(g, 1), :].rearrange("p a v -> p (a v)"))
                dve.tensor_copy(at_gg[:, :, :], ns_gate[:, :, bass.ds(g * 12, 12)])
                dve.drain()
                dve.sem_inc(S["ns_staged"], 1)
                attend(g, "ns", NSA_STEPS, True)
            dve.wait_ge(S["act_emptied"], owners[tiles_done("nsa_mg") - 1][1])
            tt(A[:, 0:8, TB], A[:, 0:8, TB], A[:, 8:16, TB], ALU.mult)
            dve.drain()
            tt(T2[:, :, TB], T2[:, :, TB], A[:, 0:8, TB], ALU.add).then_inc(S["merged"], 1)
            residual("mix_out", size=SEQ, tokens=TB)
            norm(7, SEQ, TB, param("ffn_norm2"))
            conv_feed_forward(stage_number("ffn2"))
            residual("ffn_out", 4, SEQ, TB)
            norm(8, SEQ, TB, param("final"), "final_ready")


def weight_stream(inp):
    def tiles(w, interleave=False):
        k, n = w.shape
        kt, nt = -(-k // P), -(-n // P)
        if (k, n) != (kt * P, nt * P):
            w = np.pad(w, ((0, kt * P - k), (0, nt * P - n)))
        t = w.reshape(kt, P, nt, P).transpose(2, 0, 1, 3)
        if interleave:
            t = np.stack([t[:nt // 2], t[nt // 2:]], axis=1)
        return t.reshape(kt * nt, P, P)

    def twice(w):
        k, n = w.shape
        return np.repeat(w.reshape(k, n // HD, 1, HD), 2, axis=2).reshape(k, 2 * n)

    def ffn(i, j):
        return [tiles(inp["ffn_w_in"][i, j], True)], [tiles(inp["ffn_w_out"][i, j])]

    at = inp["at_w_in"][0]
    z = inp["w_in_2"][0]
    cut = np.cumsum([0, 512, 512, 1024, 1024, 1024, 1024, 1024, 1024, 1536, 48, 3072])
    z = [z[:, a:b] for a, b in zip(cut[:-1], cut[1:])]
    kc, vc, ks, vs, kw, vw = np.split(z[8], 6, axis=1)
    mg = np.split(z[10], 3, axis=1)
    many = lambda *ws: [tiles(w) for w in ws]
    per_stage = [
        *ffn(0, 0), many(inp["rk_w_r"][0]), many(inp["rk_w_k"][0]), many(inp["rk_w_v"][0]),
        many(inp["rk_w1"][0]), many(inp["rk_w2"][0]), many(inp["rk_a1"][0]), many(inp["rk_a2"][0]),
        many(inp["rk_g1"][0]), many(inp["rk_g2"][0]), many(inp["rk_w_o"][0]),
        *ffn(0, 1), *ffn(1, 0),
        many(at[:, :1024], twice(at[:, 1024:1280]), at[:, 1280:1536], at[:, 1536:2048], twice(at[:, 2048:2112]),
             at[:, 2112:]),
        many(inp["at_w_o"][0]), *ffn(1, 1),
        many(z[0], z[1], z[2], z[3]), many(inp["w_ret_out_2"][0]), many(mg[0]),
        many(z[4], z[5], z[6]), many(inp["w_sc_out_2"][0]), many(mg[1]),
        many(z[7], twice(kc), twice(vc), twice(ks), twice(kw), vs, vw, z[9]),
        many(inp["nsa_cmp_w1_2"][0, 0]), many(twice(inp["nsa_cmp_w2_2"][0, 0])),
        many(inp["nsa_cmp_w1_2"][0, 1]), many(inp["nsa_cmp_w2_2"][0, 1]),
        many(inp["w_nsa_out_2"][0]), many(mg[2]), many(inp["w_mix_out_2"][0]),
        [tiles(inp["w_ffn_up_2"][0], True)], [tiles(inp["w_ffn_down_2"][0])],
    ]
    out = np.zeros((N_SLOTS * PER, P, P), np.float32)
    assert len(per_stage) == len(STAGES)
    for start, (name, kt, nt), parts in zip(STARTS, STAGES, per_stage):
        assert sum(len(t) for t in parts) == kt * nt, name
        for t in parts:
            out[start:start + len(t)] = t
            start += len(t)
    return np.ascontiguousarray(out.reshape(N_SLOTS, PER, P, P).transpose(0, 2, 1, 3)).reshape(N_SLOTS, P, PER * P)


def parameters(inp):
    f = lambda v: np.reshape(v, (-1, P)).T
    pos = inp["nsa_cmp_pos_2"][0].reshape(2, 16, P)
    cols = {
        "norm": f(inp["norm_g"]), "mix": f(inp["rk_mix"]), "w0": f(inp["rk_w0"]), "a0": f(inp["rk_a0"]),
        "k_k": f(inp["rk_k_k"]), "k_a": f(inp["rk_k_a"]), "r_k": f(inp["rk_r_k"]), "lnx_g": f(inp["rk_lnx_g"]),
        "lnx_b": f(inp["rk_lnx_b"]), "q_g": f(np.tile(inp["at_q_g"][0], 2)), "k_g": f(np.tile(inp["at_k_g"][0], 2)),
        "norm2": f(inp["attn_norm_w_2"]), "ret_norm": f(inp["ret_norm_w_2"]), "sc_conv": f(inp["sc_conv_w_2"]),
        "cmp_pos": f(pos), "ffn_norm2": f(inp["ffn_norm_w_2"]), "ffn_conv": f(inp["ffn_conv_w_2"]),
        "final": f(inp["final_norm_w_2"]),
    }
    for name, (_, n) in PARAMS.items():
        assert cols[name].shape[1] == n, name
    return np.concatenate([cols[n] for n in PARAMS], axis=1)


def kernel(**inputs):
    import concourse.bacc as _bacc
    from concourse.bass_utils import run_bass_kernel_spmd as _run

    inp = {k: np.asarray(v) for k, v in inputs.items()}
    x = np.concatenate([inp["meta"], inp["x"][0]], axis=0)
    arrays = {
        "stream": weight_stream(inp),
        "x_in": x.T.reshape(DT, P, T).transpose(1, 0, 2),
        "params": parameters(inp),
        "consts": constants(),
        "decay": retention_decay(),
    }
    arrays = {k: np.ascontiguousarray(v) for k, v in arrays.items()}
    nc = _bacc.Bacc("TRN2", target_bir_lowering=False, num_devices=1)
    args = [nc.dram_tensor(k, v.shape, F32, kind="ExternalInput").ap() for k, v in arrays.items()]
    out = nc.dram_tensor("out", (P, DT * SEQ), F32, kind="ExternalOutput").ap()
    build(nc, *args, out)
    got = _run(nc, [arrays], core_ids=[0]).results[0]["out"]
    return np.ascontiguousarray(np.reshape(got, (P, DT, SEQ)).transpose(2, 1, 0)).reshape(1, SEQ, D)
```

```python
from contextlib import ExitStack

import numpy as np

import concourse.bass as bass
from concourse import mybir

ALU = mybir.AluOpType
ACT = mybir.ActivationFunctionType
F32 = mybir.dt.float32
F32R = mybir.dt.float32r
AX_X = mybir.AxisListType.X

P = 128
D = 1024
DT = D // P
SEQ = 256
N_META = 16
T = SEQ + N_META
CHUNKS = [(0, N_META), (N_META, P), (N_META + P, P)]
HD = 64
FF = 2816
FT = FF // P
N_CMP = 15
RING = 6
PER = 16
HALF = PER // 2
SPLIT_RING = 4
FFN_SLOTS = 3 * FT * DT // PER
LEVELS = 7
NEG = -1e30

STAGES = [
    ("ffn", DT, 2 * FT), ("ffn_out", FT, DT),
    ("rk_r", DT, 8), ("rk_k", DT, 8), ("rk_v", DT, 8), ("rk_w1", DT, 1), ("rk_w2", 1, 8),
    ("rk_a1", DT, 1), ("rk_a2", 1, 8), ("rk_g1", DT, 2), ("rk_g2", 2, 8), ("rk_o", DT, 8),
    ("ffn", DT, 2 * FT), ("ffn_out", FT, DT),
    ("ffn", DT, 2 * FT), ("ffn_out", FT, DT),
    ("at_in", DT, 20), ("at_o", DT, 8),
    ("ffn", DT, 2 * FT), ("ffn_out", FT, DT),
    ("ret_in", DT, 24), ("ret_out", DT, 8), ("ret_mg", DT, 8),
    ("sc_in", DT, 24), ("sc_out", DT, 8), ("sc_mg", DT, 8),
    ("nsa_in", DT, 29), ("cmp_k1", 16, 2), ("cmp_k2", 2, 1), ("cmp_v1", 16, 2), ("cmp_v2", 2, 1),
    ("nsa_out", DT, 8), ("nsa_mg", DT, 8),
    ("mix_out", DT, 8),
    ("ffn2", DT, 2 * FT), ("ffn_out", FT, DT),
]


def stage_starts():
    starts, at = [], 0
    for name, kt, nt in STAGES:
        if name in ("ffn", "ffn2"):
            at = -(-at // PER) * PER
        starts.append(at)
        at += kt * nt
    return starts, -(-at // PER)


STARTS, N_SLOTS = stage_starts()

PARAMS = {}


def _param(name, columns):
    PARAMS[name] = (sum(c for _, c in PARAMS.values()), columns)


for _n, _c in (("norm", 48), ("mix", 48), ("w0", 8), ("a0", 8), ("k_k", 8), ("k_a", 8), ("r_k", 8),
               ("lnx_g", 8), ("lnx_b", 8), ("q_g", 1), ("k_g", 1), ("norm2", 8), ("ret_norm", 8),
               ("sc_conv", 24), ("cmp_pos", 32), ("ffn_norm2", 8), ("ffn_conv", 132), ("final", 8)):
    _param(_n, _c)
N_PARAM = sum(c for _, c in PARAMS.values())

CONSTS = {}


def _const(name, *shape):
    CONSTS[name] = (sum(int(np.prod(s)) for _, s in CONSTS.values()), shape)


for _n, _s in (("ident", (P,)), ("ones", (P,)), ("head_ones", (P,)), ("rope_swap", (P,)), ("ret_swap", (P,)),
               ("level", (LEVELS, P)), ("level_0t", (P,)), ("tri", (2, P)), ("reset", (T,)), ("cos", (T,)), ("sin", (T,)),
               ("ret_cos", (SEQ,)), ("ret_sin", (SEQ,)), ("causal", (3, T)), ("neg", (3, T)),
               ("neg_cmp", (2, N_CMP)), ("any_cmp", (2,)), ("eps", (3,))):
    _const(_n, *_s)
N_CONST = sum(int(np.prod(s)) for _, s in CONSTS.values())
EPS_RMS, EPS_LNX, EPS_RET = range(3)


def constants():
    c = {n: np.zeros((P,) + s, np.float32) for n, (_, s) in CONSTS.items()}
    r = np.arange(P)
    c["ident"][:] = np.eye(P)
    c["ones"][:] = 1
    c["head_ones"][:] = (r[:, None] // HD == r[None, :] // HD)
    for name, width, half in (("rope_swap", HD, 8), ("ret_swap", P, 64)):
        for base in range(0, P, width):
            for d in range(half):
                c[name][base + d + half, base + d] = -1
                c[name][base + d, base + half + d] = 1
    for n in range(LEVELS):
        m = 1 << n
        t, s = r[:, None], r[None, :]
        c["level"][:, n] = (t // (2 * m) == s // (2 * m)) & (t // m % 2 == 1) & (s // m % 2 == 0)
    c["level_0t"][:] = c["level"][:, 0].T
    c["tri"][:, 0] = r[:, None] < r[None, :]
    c["tri"][:, 1] = r[:, None] <= r[None, :]
    c["reset"][:] = 1
    for t0, _ in CHUNKS:
        c["reset"][:, t0] = 0
    inv = (np.float32(500000.0) ** (-np.arange(0, 16, 2, dtype=np.float32) / 16)).astype(np.float32)
    ang = (np.arange(T, dtype=np.float32)[:, None] * inv).astype(np.float32)
    d = r % HD
    c["cos"][:] = np.where(d[:, None] < 16, np.cos(ang).T[d % 8], 1)
    c["sin"][:] = np.where(d[:, None] < 16, np.sin(ang).T[d % 8], 0)
    theta = (np.float32(10000.0) ** (-np.linspace(0, 1, 64, dtype=np.float32))).astype(np.float32)
    ang = (np.arange(SEQ, dtype=np.float32)[:, None] * theta).astype(np.float32)
    c["ret_cos"][:] = np.cos(ang).T[r % 64]
    c["ret_sin"][:] = np.sin(ang).T[r % 64]
    for n, (t0, size) in enumerate(CHUNKS):
        c["causal"][:, n] = np.arange(T)[None] <= t0 + r[:, None]
    c["neg"][:] = (c["causal"] - 1) * -NEG
    for n in range(2):
        t = n * P + r
        c["neg_cmp"][:, n] = np.where(np.arange(N_CMP) * 16 + 31 <= t[:, None], 0, NEG)
        c["any_cmp"][:, n] = t >= 31
    c["eps"][:] = (1e-6, 64e-5, 1e-6)
    return np.concatenate([c[n].reshape(P, -1) for n in CONSTS], axis=1)


def retention_decay():
    gamma = np.log1p(-(2.0 ** (-5.0 - np.arange(4))))
    key = np.arange(P)[:, None, None] + np.arange(2)[None, :, None] * P
    rel = np.arange(SEQ)[None, None, :] - key
    out = [np.where(rel >= 0, np.exp(g * np.maximum(rel, 0)), 0) * P ** -0.5 for g in gamma]
    return np.stack(out, axis=1).astype(np.float32).reshape(P, -1)


def build(nc, stream, x_in, params, consts, decay, out):
    with ExitStack() as ctx:
        class Semaphores(dict):
            def __missing__(self, name):
                self[name] = ctx.enter_context(nc.semaphore(name))
                return self[name]

        S = Semaphores()

        place = [-(-nc.sbuf_base // 32) * 32]

        def at_next(name, shape, dtype=F32):
            t = nc.alloc_sbuf_tensor_at(name, shape, dtype, offset=place[0])
            place[0] += -(-int(np.prod(shape[1:])) * 4 // 32) * 32
            return t

        X = at_next("X", [P, DT, T])
        wring = at_next("wring", [P, RING, PER * P])
        par = at_next("par", [P, N_PARAM])
        con = at_next("con", [P, N_CONST])
        rms = at_next("rms", [P, 2, T])
        small = at_next("small", [P, 704])
        shared = place[0]
        H = at_next("H", [P, DT, T])
        T0 = at_next("T0", [P, DT, T])
        T1 = at_next("T1", [P, DT, T])
        T2 = at_next("T2", [P, DT, T])
        A = at_next("A", [P, 48, T])
        group = at_next("group", [P, 9664])
        place[0] = shared
        w_high = at_next("w_high", [P, SPLIT_RING, HALF * P], F32R)
        w_low = at_next("w_low", [P, SPLIT_RING, HALF * P], F32R)
        in_high = at_next("in_high", [P, DT, T], F32R)
        in_low = at_next("in_low", [P, DT, T], F32R)
        hid_high = at_next("hid_high", [P, FT, T], F32R)
        hid_low = at_next("hid_low", [P, FT, T], F32R)
        normed = at_next("normed", [P, DT, T])
        silu_out = at_next("silu_out", [P, 2, T])
        hidden = at_next("hidden", [P, 2, T])
        conv_in = at_next("conv_in", [P, 2, 2, T])
        conv_out = at_next("conv_out", [P, 2, 2, T])
        ps = ctx.enter_context(nc.psum_tensor("ps", [P, 8, 512], F32))

        def const(name):
            at, shape = CONSTS[name]
            v = con[:, at:at + int(np.prod(shape))]
            return v.rearrange("p (a b) -> p a b", a=shape[0]) if len(shape) == 2 else v

        def param(name, n=0):
            at = PARAMS[name][0] + 8 * n
            return par[:, at:at + 8]

        def column(name, n=0):
            at = PARAMS[name][0] + n
            return par[:, at:at + 1]

        def eps(n):
            at = CONSTS["eps"][0] + n
            return con[:, at:at + 1]

        def carve(owner, *shapes):
            at, views = 0, []
            for shape in shapes:
                n = int(np.prod(shape))
                v = owner[:, at:at + n]
                if len(shape) == 2:
                    v = v.rearrange("p (a b) -> p a b", a=shape[0])
                if len(shape) == 3:
                    v = v.rearrange("p (a b c) -> p a b c", a=shape[0], b=shape[1])
                if len(shape) == 4:
                    v = v.rearrange("p (a b c d) -> p a b c d", a=shape[0], b=shape[1], c=shape[2])
                views.append(v)
                at += n
            assert at <= owner.shape[1], at
            return views

        ident, ones, head_ones = const("ident"), const("ones"), const("head_ones")
        rope_swap, ret_swap, level, tri = const("rope_swap"), const("ret_swap"), const("level"), const("tri")

        RK_ORDER = (1, 2, 0)
        RK_LEVELS = [C.bit_length() - 1 for _, C in CHUNKS]
        rk_ar, rk_bkv, rk_s, rk_sc, *rest = carve(
            group, (2, 2, T), (3, 2, T), (2, 2, HD), (2, 2), *[(6, P)] * 3, *[(4, 2, C) for _, C in CHUNKS] * 2)
        rk_tm, rk_lb, rk_lk = rest[0:3], rest[3:6], rest[6:9]
        rest = carve(T1[:, :, :].rearrange("p a t -> p (a t)"), *[(4, C) for _, C in CHUNKS] * 2)
        rk_x, rk_xt = rest[0:3], rest[3:6]
        *rk_ym, rk_z, rk_sa = carve(T2[:, :, :].rearrange("p a t -> p (a t)"), *[(4, C) for _, C in CHUNKS],
                                    (4, HD), (4, HD))
        rk_mid, rk_mid_exp, rk_end = carve(small, (3, 8), (3, 8), (3, 8))
        (rk_lora,) = carve(group, (4, T))
        (at_q, at_kg, at_vg, at_p, at_pt, at_vtm, at_gg, at_max, at_sum, at_inv, ns_blk) = carve(
            group, (2, T), (2, T), (6, HD), (2, 4, T), (3, 4, P), (4, 256), (2, 12), (2, 4), (2, 4), (2, 4),
            (16, 4 * N_CMP))
        (ns_gate, ns_cmp_hid, ns_cmp_k, ns_cmp_v, ns_kc, ns_vc, ds_wi, ds_top) = carve(
            small, (2, 48), (2, 4 * N_CMP), (4 * N_CMP,), (4, HD), (N_CMP,), (HD,), (2, 8), (8,))
        ret_vt = A[:, 24:32, :].rearrange("p a t -> p (a t)")[:, 0:2048].rearrange("p (c j v) -> p c j v", c=2, j=8)
        ret_st = A[:, 32:40, :].rearrange("p a t -> p (a t)")[:, 0:2048].rearrange("p (h c q) -> p h c q", h=4, c=2)
        ret_decay = T1[:, :, :].rearrange("p a t -> p (a t)")[:, 0:2048]

        DSA_STEPS = [(c, c, t0, C, 0, at_kg[:, 0, 0:t0 + C], T1[:, c, 0:t0 + C],
                      [(k0, KC, at_vg[0:KC, kc, :]) for kc, (k0, KC) in enumerate(CHUNKS[:c + 1])], True, True)
                     for c, (t0, C) in enumerate(CHUNKS)]
        NSA_STEPS = []
        for c in range(2):
            t0, keys = N_META + c * P, (c + 1) * P
            NSA_STEPS.append((3 * c, c, t0, P, 0, ns_kc[:, :], const("neg_cmp")[:, c, :],
                              [(0, N_CMP, ns_vc[0:N_CMP, :])], True, False))
            for b in range(2):
                NSA_STEPS.append((3 * c + 1 + b, c, t0, P, 1 + b, at_kg[:, b, N_META:N_META + keys],
                                  const("neg")[:, 1 + c, N_META:N_META + keys],
                                  [(kc * P, P, at_vg[:, 2 * kc + b, :]) for kc in range(c + 1)], False, b == 1))

        block = ctx.enter_context(nc.Block())
        TB = slice(N_META, T)

        def rk_level_bank(c, i):
            C = CHUNKS[c][1]
            bank, at = ((6 + i // 2, i % 2 * 256), (i, 0), (3 + i, 0))[c]
            return ps[0:C, bank, at:at + 4 * C].rearrange("p (q t) -> p q t", q=4)

        EMPTIED_BY = {"rk_o": "dve", "at_o": "dve", "mix_out": "dve", "ffn_out": "dve", "cmp_v2": "act"}
        tiles_before, act_before, dve_before, owners = [], [], [], []
        n_act = n_dve = 2
        for name, kt, nt in STAGES:
            tiles_before.append(len(owners))
            act_before.append(n_act)
            dve_before.append(n_dve)
            for i in range(nt):
                if name == "ffn":
                    by = "act" if i % 2 == 0 else "dve"
                else:
                    by = EMPTIED_BY.get(name, "act")
                if by == "act":
                    n_act += 1
                    owners.append(("act_emptied", n_act))
                else:
                    n_dve += 1
                    owners.append(("dve_emptied", n_dve))

        def slot_of_ffn(n):
            return any(0 <= n - STARTS[i] // PER < FFN_SLOTS for i, st in enumerate(STAGES) if st[0] in ("ffn", "ffn2"))

        FFN_STAGES = [i for i, st in enumerate(STAGES) if st[0] in ("ffn", "ffn2")]
        FFN_NORMS = (0, 2, 3, 5, 7)

        def stage_number(name, nth=0):
            return [i for i, s in enumerate(STAGES) if s[0] == name][nth]

        def tiles_done(name, nth=0):
            s = stage_number(name, nth)
            return tiles_before[s] + STAGES[s][2]

        @block.sync
        def _(sp):
            sp.dma_start(con[:, :], consts).then_inc(S["consts_loaded"], 16)
            sp.dma_start(par[:, :], params).then_inc(S["consts_loaded"], 16)
            sp.dma_start(X[:, :, :], x_in).then_inc(S["x_loaded"], 16)
            loaded = [S[f"slot{i}_loaded"] for i in range(RING)]

            def load(slot, number):
                sp.dma_start(wring[:, slot, :], stream[number]).then_inc(loaded[slot], 16)

            for n in range(RING):
                load(n, n)
            runs = []
            counts = {"slots_split": 0, "slots_used": 0}
            for n in range(N_SLOTS - RING):
                name = "slots_split" if slot_of_ffn(n) else "slots_used"
                counts[name] += 1
                if runs and runs[-1][2] == name:
                    runs[-1][1] += 1
                else:
                    runs.append([n + RING, 1, name, counts[name]])
            for first, count, name, value in runs:
                whole = count // RING * RING
                if whole > RING:
                    with sp.Fori(0, count // RING) as r:
                        for n in range(RING):
                            slot = (first + n) % RING
                            sp.wait_ge(S[name], r * RING + (value + n))
                            sp.dma_start(wring[:, slot, :], stream[bass.ds(r * RING + (first + n), 1)].rearrange(
                                "a p n -> p (a n)")).then_inc(loaded[slot], 16)
                else:
                    whole = 0
                for n in range(whole, count):
                    sp.wait_ge(S[name], value + n)
                    load((first + n) % RING, first + n)
            sp.wait_ge(S["final_ready"], DT)
            sp.dma_start(out.rearrange("p (a t) -> p a t", a=DT), H[:, :, TB]).then_inc(S["out_stored"], 16)
            sp.wait_ge(S["out_stored"], 16)

        @block.tensor
        def _(pe):
            used_pending = [False]
            half_pending = [True]

            def weight_tile(pos, turn=None):
                number, j = divmod(pos, PER)
                slot = number % RING
                if j == 0:
                    value = 16 * (number // RING + 1)
                    pe.wait_ge(S[f"slot{slot}_loaded"], value if turn is None else turn * 16 + value)
                return wring[:, slot, j * P:(j + 1) * P]

            def out_tile(bank, pos, rhs, kt, turn=None, size=T, before_k=None):
                for k in range(kt):
                    w = weight_tile(pos + k, turn)
                    if before_k:
                        before_k(k)
                    mm = pe.matmul(ps[:, bank, 0:size], w, rhs(k), start=(k == 0), stop=(k == kt - 1))
                    if k == kt - 1:
                        mm.then_inc(S["linear_ready"], 1)
                    elif used_pending[0]:
                        mm.then_inc(S["slots_used"], 1)
                        used_pending[0] = False
                    if (pos + k) % PER == PER - 1:
                        assert not used_pending[0]
                        used_pending[0] = True

            def bank_free(tile):
                if tile >= 4:
                    name, value = owners[tile - 4]
                    pe.wait_ge(S[name], value)

            def split_out_tile(f, bank, first, kt, high, low, turn=None, size=T, before_k=None):
                for k in range(kt):
                    half, j = divmod(2 * FFN_SLOTS * f * HALF + first + k, HALF)
                    if j == 0:
                        pe.wait_ge(S["w_split"], half + 1 if turn is None else turn * 2 * RING + (half + 1))
                    w = slice(j * P, (j + 1) * P)
                    wh, wl = w_high[:, half % SPLIT_RING, w], w_low[:, half % SPLIT_RING, w]
                    if before_k:
                        before_k(k)
                    o = ps[:, bank, 0:size]
                    mm = pe.matmul(o, wh, high(k), start=(k == 0), stop=False)
                    if half_pending[0]:
                        mm.then_inc(S["halves_used"], 1)
                        half_pending[0] = False
                    pe.matmul(o, wh, low(k), start=False, stop=False)
                    mm = pe.matmul(o, wl, high(k), start=False, stop=(k == kt - 1))
                    if j == HALF - 1:
                        half_pending[0] = True
                mm.then_inc(S["linear_ready"], 1)

            def linear(name, rhs, nth=0, size=T, before_k=None):
                s = stage_number(name, nth)
                _, kt, nt = STAGES[s]
                for i in range(nt):
                    tile = tiles_before[s] + i
                    bank_free(tile)
                    out_tile(tile % 4, STARTS[s] + i * kt, rhs, kt, None, size, before_k if i == 0 else None)

            def feed_forward(f, size=T, tokens=slice(0, T)):
                s = FFN_STAGES[f]
                base, a, d = tiles_before[s], act_before[s], dve_before[s]
                conv = STAGES[s][0] == "ffn2"
                for tile in range(base, base + 4):
                    if tile >= 4:
                        bank_free(tile)

                def pair(turn, p):
                    for half in range(2):
                        if conv:
                            value, step, name = a + 2 * (p - 2) + half + 1, 2 * RING, "act_emptied"
                        elif half == 0:
                            value, step, name = a + p - 1, RING, "act_emptied"
                        else:
                            value, step, name = d + p - 1, RING, "dve_emptied"
                        pe.wait_ge(S[name], value if turn is None else turn * step + value)
                        there = None
                        if p == half == 0:
                            there = lambda k: pe.wait_ge(S["in_split"], DT * f + k + 1)
                        split_out_tile(f, (base + 2 * p + half) % 4, (2 * p + half) * DT, DT,
                                       lambda k: in_high[:, k, tokens], lambda k: in_low[:, k, tokens],
                                       turn, size, there)

                assert half_pending[0]
                alone = FT % RING
                for p in range(alone):
                    pair(None, p)
                with pe.Fori(0, FT // RING) as turn:
                    for p in range(alone, alone + RING):
                        pair(turn, p)
                s += 1
                for i in range(DT):
                    tile = tiles_before[s] + i
                    bank_free(tile)
                    split_out_tile(f, tile % 4, 2 * FT * DT + i * FT, FT,
                                   lambda k: hid_high[:, k, tokens], lambda k: hid_low[:, k, tokens], None, size,
                                   (lambda k: pe.wait_ge(S["hidden_split"], FT * f + k + 1)) if i == 0 else None)

            def norm_sum(n, size, tokens):
                if n in FFN_NORMS:
                    s = FFN_STAGES[FFN_NORMS.index(n)]
                    if s and STARTS[s] > STARTS[s - 1] + STAGES[s - 1][1] * STAGES[s - 1][2]:
                        assert not used_pending[0]
                        used_pending[0] = True
                squares = normed if n in FFN_NORMS else T0
                pe.wait_ge(S["squares_ready"], n + 1)
                for k in range(DT):
                    mm = pe.matmul(ps[:, 4, 0:size], ones, squares[:, k, tokens], start=(k == 0), stop=(k == DT - 1))
                    if k == 0 and used_pending[0] and n in FFN_NORMS:
                        mm.then_inc(S["slots_used"], 1)
                        used_pending[0] = False
                mm.then_inc(S["square_sum_ready"], 1)

            def per_tile(weights, source, banks, size, done):
                for i, bank in enumerate(banks):
                    mm = pe.matmul(ps[:, bank, 0:size], weights, source(i), start=True, stop=True)
                mm.then_inc(S[done], 1)

            def settle(C):
                if C < 32:
                    pe.sem_inc(S["few_rows_waited"], 1)

            rk_heads = [(2 * par + u, par, u, HD * par) for par in range(2) for u in range(2)]

            def rk_products(g, j, c):
                t0, C = CHUNKS[c]
                now = slice(t0, t0 + C)
                if j:
                    pe.wait_ge(S["rk_tm_copied"], g * 3 + j)
                settle(C)
                for i in range(3):
                    for u in range(2):
                        n = 2 * i + u
                        mm = pe.transpose(ps[0:C, n // 4, n % 4 * P:(n % 4 + 1) * P], rk_bkv[:, i, u, now], ident)
                mm.then_inc(S["rk_turned"], 1)
                for i, bank in ((0, (2, 6)[j % 2]), (1, 4)):
                    if i and j:
                        pe.wait_ge(S["rk_masked"], g * 6 + 2 * j)
                        settle(C)
                    for q, par, u, p in rk_heads:
                        o = ps[0:C, bank + par, u * 256:(u + 1) * 256].rearrange("p (a t) -> p a t", a=2)[:, :, 0:C]
                        mm = pe.matmul(o, rk_bkv[p:p + HD, i, u, now], rk_ar[p:p + HD, u, :, now],
                                       start=True, stop=True)
                    mm.then_inc(S["rk_products_ready"], 1)

            def rk_under(g, c, n):
                C, nl = CHUNKS[c][1], RK_LEVELS[c]
                if n:
                    pe.wait_ge(S[f"rk_x{c}_added"], g * (2 * nl - 1) + (2 * n - 1))
                    settle(C)
                for q in range(4):
                    mm = pe.matmul(rk_level_bank(c, 0)[:, q, :], rk_lb[c][0:C, q, 0, :],
                                   rk_x[c][0:C, q, :] if n else ident[0:C, 0:C], start=True, stop=True)
                mm.then_inc(S[f"rk_under{c}_ready"], 1)

            def rk_merge(g, c, n):
                C, nl = CHUNKS[c][1], RK_LEVELS[c]
                pe.wait_ge(S[f"rk_x{c}_added"], g * (2 * nl - 1) + 2 * n)
                pe.wait_ge(S[f"rk_under{c}_masked"], g * (nl - 1) + n)
                settle(C)
                for q in range(4):
                    xt, y = rk_xt[c][0:C, q, :], rk_ym[c][0:C, q, :]
                    if n < nl - 1:
                        pe.matmul(rk_level_bank(c, 1)[:, q, :], xt, y, start=True, stop=True)
                    mm = pe.matmul(rk_level_bank(c, 2)[:, q, :], y, xt, start=True, stop=True)
                mm.then_inc(S[f"rk_merge{c}_ready"], 1)

            def rk_state(g, c):
                t0, C = CHUNKS[c]
                step = g * 3 + (c + 1)
                now = slice(t0, t0 + C)
                tm, lb, lk = rk_tm[c], rk_lb[c], rk_lk[c]
                if c:
                    pe.wait_ge(S["rk_state_ready"], g * 2 + c)
                for q, par, u, p in rk_heads:
                    o = ps[0:C, par, u * HD:(u + 1) * HD]
                    if c:
                        pe.matmul(o, rk_ar[p:p + HD, u, 0, now], rk_s[p:p + HD, c - 1, u, :], start=True, stop=False)
                    mm = pe.matmul(o, lk[0:C, q, 0, :], tm[0:C, 4 + u, p:p + HD], start=(c == 0), stop=True)
                mm.then_inc(S["rk_z_ready"], 1)
                pe.wait_ge(S["rk_z_copied"], step)
                pe.wait_ge(S[f"rk_x{c}_added"], (g + 1) * (2 * RK_LEVELS[c] - 1))
                settle(C)
                for q in range(4):
                    mm = pe.matmul(ps[0:C, 3, q * HD:(q + 1) * HD], rk_xt[c][0:C, q, :], rk_z[0:C, q, :],
                                   start=True, stop=True)
                mm.then_inc(S["rk_sa_ready"], 1)
                pe.wait_ge(S["rk_sa_copied"], step)
                settle(0)
                if c < 2:
                    for q, par, u, p in rk_heads:
                        o = ps[p:p + HD, 6 + par, u * HD:(u + 1) * HD]
                        pe.matmul(o, tm[0:C, u, p:p + HD], rk_sa[0:C, q, :], start=True, stop=False)
                        mm = pe.matmul(o, tm[0:C, 2 + u, p:p + HD], tm[0:C, 4 + u, p:p + HD],
                                       start=False, stop=True)
                    mm.then_inc(S["rk_s_ready"], 1)
                pe.wait_ge(S["rk_y_copied"], step)
                if c == 0:
                    pe.wait_ge(S["rk_x2_added"], (g + 1) * (2 * RK_LEVELS[2] - 1))
                settle(0)
                for q, par, u, p in rk_heads:
                    o = ps[p:p + HD, 4 + par, u * P:u * P + C]
                    if c:
                        pe.matmul(o, rk_s[p:p + HD, c - 1, u, :], rk_ar[p:p + HD, u, 1, now], start=True, stop=False)
                    pe.matmul(o, rk_sa[0:C, q, :], lb[0:C, q, 1, :], start=(c == 0), stop=False)
                    mm = pe.matmul(o, tm[0:C, 4 + u, p:p + HD], lk[0:C, q, 1, :], start=False, stop=True)
                mm.then_inc(S["rk_y_ready"], 1)

            def attend(g, pre, steps, o_bank):
                count, chunks = len(steps), steps[-1][1] + 1

                def logits(n, c, t0, C, _, keys, *rest):
                    if n == 0:
                        pe.wait_ge(S[pre + "_staged"], g + 1)
                    else:
                        pe.wait_ge(S[pre + "_biased"], g * count + n)
                    settle(C)
                    for h in range(4):
                        p = HD * (h % 2)
                        mm = pe.matmul(ps[0:C, h, 0:keys.shape[1]], at_q[p:p + HD, h // 2, t0:t0 + C],
                                       keys[p:p + HD, :], start=True, stop=True)
                    mm.then_inc(S[pre + "_logits"], 1)

                def values(n, c, t0, C, _, keys, bias, parts, first, last):
                    pe.wait_ge(S[pre + "_probs"], g * count + (n + 1))
                    settle(C)
                    for kc, (k0, KC, _) in enumerate(parts):
                        for h in range(4):
                            mm = pe.transpose(ps[0:KC, 4 + kc, h * P:h * P + C], at_p[0:C, n % 2, h, k0:k0 + KC],
                                              ident[0:C, 0:C])
                    mm.then_inc(S[pre + "_turned_probs"], 1)
                    pe.wait_ge(S[pre + "_probs_copied"], g * count + (n + 1))
                    if first:
                        pe.wait_ge(S[pre + "_o_copied"], g * chunks + (c + 1))
                    settle(C)
                    for h in range(4):
                        p, u = HD * (h % 2), h // 2
                        for kc, (k0, KC, v) in enumerate(parts):
                            mm = pe.matmul(ps[p:p + HD, o_bank(u), u * P:u * P + C], v, at_pt[0:KC, kc, h, 0:C],
                                           start=(first and kc == 0), stop=(last and kc == len(parts) - 1))
                    if last:
                        mm.then_inc(S[pre + "_o_ready"], 1)

                for i in range(count + 1):
                    if i < count:
                        logits(*steps[i])
                    if i:
                        values(*steps[i - 1])

            pe.sem_inc(S["act_emptied"], 2)
            pe.sem_inc(S["dve_emptied"], 2)
            pe.wait_ge(S["consts_loaded"], 32)
            full = slice(0, T)
            pe_norm = lambda n: norm_sum(n, T, full)

            pe_norm(0)
            feed_forward(0)

            pe_norm(1)
            for i, (name, buf) in enumerate((("rk_r", T0), ("rk_k", T2), ("rk_v", T0))):
                pe.wait_ge(S["rk_mixed"], 8 * (i + 1))
                linear(name, lambda k, buf=buf: buf[:, k, :])
            pe.wait_ge(S["rk_mixed"], 32)
            linear("rk_w1", lambda k: T2[:, k, :])
            pe.wait_ge(S["act_emptied"], owners[tiles_done("rk_w1") - 1][1])
            linear("rk_w2", lambda k: rk_lora[:, 0, :])
            pe.wait_ge(S["rk_mixed"], 40)
            linear("rk_a1", lambda k: T0[:, k, :])
            pe.wait_ge(S["act_emptied"], owners[tiles_done("rk_a1") - 1][1])
            linear("rk_a2", lambda k: rk_lora[:, 1, :])
            pe.wait_ge(S["rk_mixed"], 48)
            linear("rk_g1", lambda k: T2[:, k, :])
            pe.wait_ge(S["act_emptied"], owners[tiles_done("rk_g1") - 1][1])
            linear("rk_g2", lambda k: rk_lora[:, 2 + k, :])
            pe.wait_ge(S["rk_kk_squared"], 1)
            pe.wait_ge(S["act_emptied"], owners[tiles_done("rk_g2") - 1][1])
            per_tile(head_ones, lambda i: T1[:, i, :], range(8), T, "rk_kk_summed")
            pe.wait_ge(S["rk_bonus_in"], 1)
            per_tile(head_ones, lambda i: T1[:, i, :], range(8), T, "rk_bonus_summed")
            pe.wait_ge(S["rk_prepared"], 1)
            with pe.Fori(0, 4) as g:
                pe.wait_ge(S["rk_staged"], g + 1)
                for j, c in enumerate(RK_ORDER):
                    rk_products(g, j, c)
                pe.wait_ge(S["rk_masked"], g * 6 + 6)
                pe.wait_ge(S["rk_tm_copied"], g * 3 + 3)
                settle(0)
                for n in range(LEVELS):
                    chunks = [c for c in RK_ORDER if n < RK_LEVELS[c]]
                    for c in chunks:
                        rk_under(g, c, n)
                    for c in chunks if n else ():
                        rk_merge(g, c, n)
                for c in range(3):
                    rk_state(g, c)
            pe.wait_ge(S["rk_y_copied"], 13)
            pe.wait_ge(S["rk_state_ready"], 8)
            per_tile(head_ones, lambda i: A[:, 24 + i, :], range(8), T, "rk_y_summed")
            pe.wait_ge(S["rk_y_squared"], 1)
            per_tile(head_ones, lambda i: T1[:, i, :], range(8), T, "rk_y_var")
            pe.wait_ge(S["rk_out_ready"], 1)
            linear("rk_o", lambda k: T0[:, k, :])

            pe_norm(2)
            feed_forward(1)
            pe_norm(3)
            feed_forward(2)

            pe_norm(4)
            pe.wait_ge(S["h_ready"], DT * 2)
            linear("at_in", lambda k: H[:, k, :])
            pe.wait_ge(S["ds_squared"], 1)
            per_tile(head_ones, lambda i: A[:, 20 + i, :], range(8), T, "ds_summed")
            pe.wait_ge(S["ds_rooted"], 1)
            per_tile(head_ones, lambda i: A[:, 28 + i, :], range(4), T, "ds_summed")
            pe.wait_ge(S["ds_normed"], 1)
            pe.wait_ge(S["ds_rooted"], 2)
            for i, first, count in ((0, 0, 8), (1, 8, 4), (2, 14, 5)):
                if i:
                    pe.wait_ge(S["ds_roped"], i)
                per_tile(rope_swap, lambda j: A[:, first + j, :], range(count), T, "ds_swapped")
            pe.wait_ge(S["ds_roped"], 3)
            for c, (t0, C) in enumerate(CHUNKS):
                for j in range(2):
                    pe.transpose(ps[0:C, c, j * P:(j + 1) * P], A[:, 12 + j, t0:t0 + C], ident)
                mm = pe.transpose(ps[0:C, c, 2 * P:3 * P], A[:, 19, t0:t0 + C], ident)
            mm.then_inc(S["ds_turned"], 1)
            pe.wait_ge(S["ds_turned_copied"], 1)
            for n, (t0, C) in enumerate(CHUNKS[1:]):
                if n:
                    pe.wait_ge(S["ds_relu"], n)
                for h in range(8):
                    p = HD * (h % 2)
                    mm = pe.matmul(ps[:, h, 0:T], A[p:p + HD, 14 + h // 2, t0:t0 + C], A[p:p + HD, 18, :],
                                   start=True, stop=True)
                mm.then_inc(S["ds_index_ready"], 1)
            pe.wait_ge(S["ds_relu"], 2)
            pe.wait_ge(S["ds_selected"], 2)
            with pe.Fori(0, 4) as g:
                attend(g, "ds", DSA_STEPS, lambda u: 7)
            pe.wait_ge(S["ds_o_copied"], 13)
            linear("at_o", lambda k: T2[:, k, :])
            pe_norm(5)
            feed_forward(3)

            norm_sum(6, SEQ, TB)
            pe.wait_ge(S["h_ready"], DT * 3)
            linear("ret_in", lambda k: H[:, k, TB], size=SEQ)
            pe.wait_ge(S["act_emptied"], owners[tiles_done("ret_in") - 1][1])
            per_tile(ret_swap, lambda i: A[:, i, TB], range(8), SEQ, "ret_swapped")
            pe.wait_ge(S["ret_roped"], 1)
            for c in range(2):
                for j in range(8):
                    mm = pe.transpose(ps[:, 2 * c + j // 4, (j % 4) * P:(j % 4 + 1) * P],
                                      A[:, 8 + j, N_META + c * P:N_META + (c + 1) * P], ident)
            mm.then_inc(S["ret_v_turned"], 1)
            for h in range(4):
                for kc in range(2):
                    mm = pe.matmul(ps[:, 4 + h, kc * SEQ:(kc + 1) * SEQ],
                                   A[:, 4 + h, N_META + kc * P:N_META + (kc + 1) * P], A[:, h, TB],
                                   start=True, stop=True)
            mm.then_inc(S["ret_scores"], 1)
            pe.wait_ge(S["ret_v_copied"], 1)
            pe.wait_ge(S["ret_masked"], 1)
            for j in range(8):
                for kc in range(2):
                    mm = pe.matmul(ps[:, j, 0:SEQ], ret_vt[:, kc, j, :], ret_st[:, j // 2, kc, :],
                                   start=(kc == 0), stop=(kc == 1))
            mm.then_inc(S["ret_o_ready"], 1)
            pe.wait_ge(S["ret_o_copied"], 1)
            for h in range(4):
                for j in range(2):
                    mm = pe.matmul(ps[:, h, 0:SEQ], ones, A[:, 40 + 2 * h + j, TB], start=(j == 0), stop=(j == 1))
            mm.then_inc(S["ret_summed"], 1)
            pe.wait_ge(S["ret_squared"], 1)
            for h in range(4):
                for j in range(2):
                    mm = pe.matmul(ps[:, h, 0:SEQ], ones, T0[:, 2 * h + j, TB], start=(j == 0), stop=(j == 1))
            mm.then_inc(S["ret_var"], 1)
            pe.wait_ge(S["ret_y_ready"], 1)
            linear("ret_out", lambda k: T0[:, k, TB], size=SEQ)
            linear("ret_mg", lambda k: H[:, k, TB], size=SEQ)
            pe.wait_ge(S["merged"], 1)
            linear("sc_in", lambda k: H[:, k, TB], size=SEQ)
            pe.wait_ge(S["sc_y_ready"], 1)
            linear("sc_out", lambda k: T0[:, k, TB], size=SEQ)
            linear("sc_mg", lambda k: H[:, k, TB], size=SEQ)
            pe.wait_ge(S["merged"], 2)

            linear("nsa_in", lambda k: H[:, k, TB], size=SEQ)
            pe.wait_ge(S["act_emptied"], owners[tiles_done("nsa_in") - 1][1])
            for c in range(2):
                t0 = N_META + c * P
                for j in range(4):
                    pe.transpose(ps[:, 4 + c, j * P:(j + 1) * P], A[:, 24 + j, t0:t0 + P], ident)
                mm = pe.transpose(ps[:, 6, c * P:(c + 1) * P], A[:, 28, t0:t0 + P], ident)
            mm.then_inc(S["ns_turned"], 1)
            pe.wait_ge(S["ns_blocks"], 1)
            linear("cmp_k1", lambda k: ns_blk[:, k, :], size=4 * N_CMP)
            pe.wait_ge(S["act_emptied"], owners[tiles_done("cmp_k1") - 1][1])
            linear("cmp_k2", lambda k: ns_cmp_hid[:, k, :], size=4 * N_CMP)
            pe.wait_ge(S["ns_blocks"], 2)
            pe.wait_ge(S["act_emptied"], owners[tiles_done("cmp_k2") - 1][1])
            linear("cmp_v1", lambda k: ns_blk[:, k, :], size=4 * N_CMP)
            pe.wait_ge(S["act_emptied"], owners[tiles_done("cmp_v1") - 1][1])
            s = stage_number("cmp_v2")
            tile = tiles_before[s]
            bank_free(tile)
            w = [weight_tile(STARTS[s] + k) for k in range(2)]
            assert STARTS[s] % PER < PER - 2
            for g in range(4):
                for k in range(2):
                    mm = pe.matmul(ps[0:N_CMP, tile % 4, g * HD:(g + 1) * HD],
                                   ns_cmp_hid[:, k, g * N_CMP:(g + 1) * N_CMP], w[k][:, 0:HD],
                                   start=(k == 0), stop=(k == 1))
            mm.then_inc(S["linear_ready"], 1)
            pe.wait_ge(S["act_emptied"], owners[tile][1])
            pe.wait_ge(S["ns_turned_copied"], 1)
            with pe.Fori(0, 4) as g:
                attend(g, "ns", NSA_STEPS, lambda u: 7 - u)
            pe.wait_ge(S["ns_o_copied"], 9)
            linear("nsa_out", lambda k: T1[:, k, TB], size=SEQ)
            linear("nsa_mg", lambda k: H[:, k, TB], size=SEQ)
            pe.wait_ge(S["merged"], 3)
            linear("mix_out", lambda k: T2[:, k, TB], size=SEQ)
            norm_sum(7, SEQ, TB)
            feed_forward(4, SEQ, TB)
            norm_sum(8, SEQ, TB)

        @block.scalar
        def _(act):
            def copy(o, i, scale=1.0):
                return act.activation(o, i, ACT.Copy, scale=scale)

            def linear(name, put, func=lambda i: ACT.Copy, bias=None, nth=0, size=T):
                s = stage_number(name, nth)
                for i in range(STAGES[s][2]):
                    tile = tiles_before[s] + i
                    act.wait_ge(S["linear_ready"], tile + 1)
                    kw = {} if bias is None else {"bias": bias[:, i:i + 1]}
                    act.activation(put(i), ps[:, tile % 4, 0:size], func(i), **kw).then_inc(S["act_emptied"], 1)

            def norm(n, size, tokens):
                if n:
                    act.wait_ge(S["x_updated"], n)
                else:
                    act.wait_ge(S["x_loaded"], 16)
                squares = normed if n in FFN_NORMS else T0
                act.activation(squares[:, :, tokens], X[:, :, tokens], ACT.Square).then_inc(S["squares_ready"], 1)
                act.wait_ge(S["square_sum_ready"], n + 1)
                act.activation(rms[:, 0, 0:size], ps[:, 4, 0:size], ACT.Sqrt, bias=eps(EPS_RMS), scale=1.0 / D
                               ).then_inc(S["rms_ready"], 1)

            def high_parts(f, i, turn=None):
                number = STARTS[FFN_STAGES[f]] // PER + i
                slot, value = number % RING, 16 * (number // RING + 1)
                act.wait_ge(S[f"slot{slot}_loaded"], value if turn is None else turn * 16 + value)
                for h in range(2):
                    half = 2 * (FFN_SLOTS * f + i) + h
                    if half >= SPLIT_RING:
                        value = half - SPLIT_RING + 2
                        act.wait_ge(S["halves_used"], value if turn is None else turn * 2 * RING + value)
                    copy(w_high[:, half % SPLIT_RING, :], wring[:, slot, h * HALF * P:(h + 1) * HALF * P]
                         ).then_inc(S["w_high_ready"], 1)

            def feed_forward(f, size=T, tokens=slice(0, T)):
                s = FFN_STAGES[f]
                base, a, d = tiles_before[s], act_before[s], dve_before[s]
                conv = STAGES[s][0] == "ffn2"
                high_parts(f, 0)
                for k in range(DT):
                    act.wait_ge(S["normed_ready"], DT * f + k + 1)
                    copy(in_high[:, k, tokens], normed[:, k, tokens]).then_inc(S["in_high_ready"], 1)
                high_parts(f, 1)

                def pair(turn, p):
                    after = lambda value, step: value if turn is None else turn * step + value
                    if conv:
                        act.wait_ge(S["conved"], after(2 * p + 2, 2 * RING))
                        for half in range(2):
                            act.wait_ge(S["linear_ready"], after(base + 2 * p + half + 1, 2 * RING))
                            copy(conv_in[:, p % 2, half, TB], ps[:, (base + 2 * p + half) % 4, 0:SEQ]
                                 ).then_inc(S["act_emptied"], 1)
                        high_parts(f, p + 2, turn)
                        act.wait_ge(S["conved"], after(2 * p + 5, 2 * RING))
                        if turn is not None or p >= 2:
                            act.wait_ge(S["hidden_split"], after(FT * f + p - 1, RING))
                        act.activation(silu_out[:, p % 2, TB], conv_out[:, p % 2, 0, TB], ACT.Silu
                                       ).then_inc(S["silu_ready"], 1)
                    else:
                        act.wait_ge(S["linear_ready"], after(base + 2 * p + 1, 2 * RING))
                        act.wait_ge(S["dve_emptied"], after(d + p - 1, RING))
                        act.activation(silu_out[:, p % 2, :], ps[:, (base + 2 * p) % 4, 0:T], ACT.Silu
                                       ).then_inc(S["act_emptied"], 1)
                        high_parts(f, p + 2, turn)

                alone = FT % RING
                for p in range(alone):
                    pair(None, p)
                with act.Fori(0, FT // RING) as turn:
                    for p in range(alone, alone + RING):
                        pair(turn, p)
                for i in range(FT + 2, FFN_SLOTS):
                    high_parts(f, i)

            def rk_turn(g, j, c):
                C = CHUNKS[c][1]
                act.wait_ge(S["rk_turned"], g * 3 + (j + 1))
                copy(rk_tm[c][0:C, 0:4, :], ps[0:C, 0, :].rearrange("p (a t) -> p a t", a=4))
                copy(rk_tm[c][0:C, 4:6, :], ps[0:C, 1, 0:256].rearrange("p (a t) -> p a t", a=2)
                     ).then_inc(S["rk_tm_copied"], 1)

            def rk_state(g, c):
                t0, C = CHUNKS[c]
                step = g * 3 + (c + 1)
                act.wait_ge(S["rk_sa_ready"], step)
                copy(rk_sa[0:C, :, :], ps[0:C, 3, 0:256].rearrange("p (a t) -> p a t", a=4)
                     ).then_inc(S["rk_sa_copied"], 1)
                act.wait_ge(S["rk_y_ready"], step)
                for par in range(2):
                    p = HD * par
                    ins = copy(A[p:p + HD, bass.ds(g * 2 + 24, 2), t0:t0 + C],
                               ps[p:p + HD, 4 + par, 0:256].rearrange("p (a t) -> p a t", a=2)[:, :, 0:C])
                ins.then_inc(S["rk_y_copied"], 1)

            def attend(g, pre, steps, put):
                count = len(steps)
                chunks = steps[-1][1] + 1

                def exponentials(n, c, t0, C, _, keys, *rest):
                    act.wait_ge(S[pre + "_max"], g * count + (n + 1))
                    for h in range(4):
                        row = at_p[0:C, n % 2, h, 0:keys.shape[1]]
                        ins = act.activation(row, row, ACT.Exp, bias=at_max[0:C, n % 2, h:h + 1],
                                             accum_out=at_sum[0:C, n % 2, h:h + 1])
                    ins.then_inc(S[pre + "_exp"], 1)

                def copies(n, c, t0, C, _, keys, bias, parts, first, last):
                    act.wait_ge(S[pre + "_turned_probs"], g * count + (n + 1))
                    for kc, (k0, KC, _) in enumerate(parts):
                        ins = copy(at_pt[0:KC, kc, :, 0:C],
                                   ps[0:KC, 4 + kc, :].rearrange("p (a t) -> p a t", a=4)[:, :, 0:C])
                    ins.then_inc(S[pre + "_probs_copied"], 1)
                    if last:
                        act.wait_ge(S[pre + "_o_ready"], g * chunks + (c + 1))
                        put(g, t0, C).then_inc(S[pre + "_o_copied"], 1)

                for i in range(count + 1):
                    if i < count:
                        exponentials(*steps[i])
                    if i:
                        copies(*steps[i - 1])

            full = slice(0, T)
            act.wait_ge(S["consts_loaded"], 32)
            norm(0, T, full)
            feed_forward(0)
            norm(1, T, full)
            linear("rk_r", lambda i: A[:, i, :])
            linear("rk_k", lambda i: A[:, 8 + i, :])
            linear("rk_v", lambda i: A[:, 16 + i, :])
            linear("rk_w1", lambda i: rk_lora[:, 0, :], lambda i: ACT.Tanh)
            linear("rk_w2", lambda i: A[:, 24 + i, :], lambda i: ACT.Sigmoid, param("w0"))
            linear("rk_a1", lambda i: rk_lora[:, 1, :])
            linear("rk_a2", lambda i: A[:, 32 + i, :], lambda i: ACT.Sigmoid, param("a0"))
            linear("rk_g1", lambda i: rk_lora[:, 2 + i, :], lambda i: ACT.Sigmoid)
            linear("rk_g2", lambda i: A[:, 40 + i, :])
            act.wait_ge(S["rk_kk_clamped"], 1)
            act.activation(T1[:, :, :], T1[:, :, :], ACT.Sqrt).then_inc(S["rk_kk_rooted"], 1)
            act.wait_ge(S["rk_logs_ready"], 1)
            act.activation(T1[:, :, :], T1[:, :, :], ACT.Exp).then_inc(S["rk_exps_ready"], 1)
            act.activation(A[:, 24:32, :], T2[:, :, :], ACT.Exp).then_inc(S["rk_exps_ready"], 1)
            act.drain()
            act.activation(T2[:, :, :], T2[:, :, :], ACT.Exp, scale=-1.0).then_inc(S["rk_exps_ready"], 1)
            act.activation(rk_mid_exp[:, :, :], rk_mid[:, :, :], ACT.Exp).then_inc(S["rk_exps_ready"], 1)
            act.sem_inc(S["rk_y_copied"], 1)
            with act.Fori(0, 4) as g:
                for j, c in enumerate(RK_ORDER):
                    rk_turn(g, j, c)
                for c in range(3):
                    rk_state(g, c)
            act.wait_ge(S["rk_y_var"], 1)
            act.activation(T1[:, :, :], ps[:, :, 0:T], ACT.Sqrt, bias=eps(EPS_LNX), scale=1.0 / HD
                           ).then_inc(S["rk_y_rooted"], 1)
            norm(2, T, full)
            feed_forward(1)
            norm(3, T, full)
            feed_forward(2)
            norm(4, T, full)
            linear("at_in", lambda i: A[:, i, :])
            for n, (first, count) in enumerate(((20, 8), (28, 4))):
                act.wait_ge(S["ds_summed"], n + 1)
                act.activation(A[:, first:first + count, :], ps[:, 0:count, 0:T], ACT.Sqrt, bias=eps(EPS_RMS),
                               scale=1.0 / HD).then_inc(S["ds_rooted"], 1)
            act.wait_ge(S["ds_turned"], 1)
            for c, (t0, C) in enumerate(CHUNKS):
                ins = copy(at_vtm[0:C, c, :], ps[0:C, c, 0:256])
                if c:
                    ins = copy(ds_wi[:, c - 1, :], ps[:, c, 256:264], scale=8 ** -0.5 * HD ** -0.5)
            ins.then_inc(S["ds_turned_copied"], 1)
            for n in range(2):
                act.wait_ge(S["ds_index_ready"], n + 1)
                if n:
                    act.wait_ge(S["ds_scored"], n)
                act.activation(T0[:, :, :], ps[:, :, 0:T], ACT.Relu).then_inc(S["ds_relu"], 1)
            act.sem_inc(S["ds_o_copied"], 1)

            def put_ds(g, t0, C):
                return copy(T2[:, bass.ds(g * 2, 2), t0:t0 + C],
                            ps[:, 7, 0:256].rearrange("p (a t) -> p a t", a=2)[:, :, 0:C])

            with act.Fori(0, 4) as g:
                attend(g, "ds", DSA_STEPS, put_ds)
            norm(5, T, full)
            feed_forward(3)

            norm(6, SEQ, TB)
            act.dma_start(ret_decay, decay).then_inc(S["decay_loaded"], 16)
            linear("ret_in", lambda i: A[:, i, TB], lambda i: ACT.Silu if i >= 16 else ACT.Copy, size=SEQ)
            act.wait_ge(S["ret_v_turned"], 1)
            copy(ret_vt.rearrange("p c j v -> p (c j v)"), ps[:, 0:4, :].rearrange("p a b -> p (a b)")
                 ).then_inc(S["ret_v_copied"], 1)
            act.wait_ge(S["ret_o_ready"], 1)
            copy(A[:, 40:48, TB], ps[:, :, 0:SEQ]).then_inc(S["ret_o_copied"], 1)
            act.wait_ge(S["ret_var"], 1)
            act.activation(T1[:, 0:4, TB], ps[:, 0:4, 0:SEQ], ACT.Sqrt, bias=eps(EPS_RET), scale=1.0 / SEQ
                           ).then_inc(S["ret_rooted"], 1)
            linear("ret_out", lambda i: A[:, i, TB], size=SEQ)
            linear("ret_mg", lambda i: A[:, 8 + i, TB], lambda i: ACT.Sigmoid, size=SEQ)
            act.wait_ge(S["merged"], 1)
            linear("sc_in", lambda i: A[:, i, TB], size=SEQ)
            linear("sc_out", lambda i: A[:, 24 + i, TB], size=SEQ)
            linear("sc_mg", lambda i: A[:, 32 + i, TB], lambda i: ACT.Sigmoid, size=SEQ)
            act.wait_ge(S["merged"], 2)
            linear("nsa_in", lambda i: A[:, i, TB], lambda i: ACT.Sigmoid if i == 28 else ACT.Copy, size=SEQ)
            act.wait_ge(S["ns_turned"], 1)
            for c in range(2):
                copy(at_vtm[:, 2 * c:2 * c + 2, :], ps[:, 4 + c, :].rearrange("p (a v) -> p a v", a=2))
                ins = copy(ns_gate[:, c, :], ps[:, 6, c * P:c * P + 48])
            ins.then_inc(S["ns_turned_copied"], 1)
            linear("cmp_k1", lambda i: ns_cmp_hid[:, i, :], lambda i: ACT.Gelu_apprx_tanh, size=4 * N_CMP)
            linear("cmp_k2", lambda i: ns_cmp_k[:, :], size=4 * N_CMP)
            linear("cmp_v1", lambda i: ns_cmp_hid[:, i, :], lambda i: ACT.Gelu_apprx_tanh, size=4 * N_CMP)
            tile = tiles_before[stage_number("cmp_v2")]
            act.wait_ge(S["linear_ready"], tile + 1)
            copy(ns_cmp_v[0:N_CMP, :, :], ps[0:N_CMP, tile % 4, 0:256].rearrange("p (a v) -> p a v", a=4)
                 ).then_inc(S["act_emptied"], 1)
            act.sem_inc(S["ns_o_copied"], 1)

            def put_ns(g, t0, C):
                copy(T1[:, bass.ds(g * 2, 1), t0:t0 + C], ps[:, 7:8, 0:C])
                return copy(T1[:, bass.ds(g * 2 + 1, 1), t0:t0 + C], ps[:, 6:7, P:P + C])

            with act.Fori(0, 4) as g:
                attend(g, "ns", NSA_STEPS, put_ns)
            linear("nsa_out", lambda i: A[:, i, TB], size=SEQ)
            linear("nsa_mg", lambda i: A[:, 8 + i, TB], lambda i: ACT.Sigmoid, size=SEQ)
            norm(7, SEQ, TB)
            feed_forward(4, SEQ, TB)
            norm(8, SEQ, TB)

        @block.gpsimd
        def _(pool):
            def low_parts(f, i, turn=None):
                slot = (STARTS[FFN_STAGES[f]] // PER + i) % RING
                for h in range(2):
                    half = 2 * (FFN_SLOTS * f + i) + h
                    pool.wait_ge(S["w_high_ready"], half + 1 if turn is None else turn * 2 * RING + (half + 1))
                    pool.tensor_tensor(w_low[:, half % SPLIT_RING, :], wring[:, slot, h * HALF * P:(h + 1) * HALF * P],
                                       w_high[:, half % SPLIT_RING, :].bitcast(F32), ALU.subtract
                                       ).then_inc(S["w_split"], 1)
                pool.drain()
                pool.sem_inc(S["slots_split"], 1)

            for f in range(len(FFN_STAGES)):
                with pool.Fori(0, FFN_SLOTS // RING) as turn:
                    for i in range(RING):
                        low_parts(f, i, turn)
                for i in range(FFN_SLOTS // RING * RING, FFN_SLOTS):
                    low_parts(f, i)

        @block.vector
        def _(dve):
            def tt(o, a, b, op):
                return dve.tensor_tensor(o, a, b, op)

            def stt(o, a, scalar, b, op0, op1):
                return dve.scalar_tensor_tensor(out=o, in0=a, scalar=scalar, in1=b, op0=op0, op1=op1)

            def tiles_of(v, n, size):
                return v.unsqueeze(2).to_broadcast([P, n, size])

            def tokens_of(v, n):
                return v.unsqueeze(1).to_broadcast([v.shape[0], n, v.shape[1]])

            def norm(n, size, tokens, gain, done="h_ready"):
                dve.wait_ge(S["rms_ready"], n + 1)
                dve.reciprocal(rms[:, 1, 0:size], rms[:, 0, 0:size])
                dve.drain()
                if n not in FFN_NORMS:
                    for k in range(DT):
                        stt(H[:, k, tokens], X[:, k, tokens], gain[:, k:k + 1], rms[:, 1, 0:size], ALU.mult, ALU.mult
                            ).then_inc(S[done], 1)
                    return
                f = FFN_NORMS.index(n)
                for k in range(DT + 1):
                    if k < DT:
                        stt(normed[:, k, tokens], X[:, k, tokens], gain[:, k:k + 1], rms[:, 1, 0:size],
                            ALU.mult, ALU.mult).then_inc(S["normed_ready"], 1)
                    if k:
                        dve.wait_ge(S["in_high_ready"], DT * f + k)
                        tt(in_low[:, k - 1, tokens], normed[:, k - 1, tokens], in_high[:, k - 1, tokens].bitcast(F32),
                           ALU.subtract).then_inc(S["in_split"], 1)

            def split_hidden(turn, p, tokens):
                tile = bass.ds(turn * 2 + p, 1)
                dve.drain()
                dve.tensor_copy(hid_high[:, tile, tokens], hidden[:, p:p + 1, tokens])
                dve.drain()
                tt(hid_low[:, tile, tokens], hidden[:, p:p + 1, tokens], hid_high[:, tile, tokens].bitcast(F32),
                   ALU.subtract).then_inc(S["hidden_split"], 1)

            def feed_forward(s):
                base, a = tiles_before[s], act_before[s]
                with dve.Fori(0, FT // 2) as turn:
                    for p in range(2):
                        dve.wait_ge(S["linear_ready"], turn * 4 + (base + 2 * p + 2))
                        dve.wait_ge(S["act_emptied"], turn * 2 + (a + p + 1))
                        tt(hidden[:, p, :], ps[:, (base + 2 * p + 1) % 4, 0:T], silu_out[:, p, :], ALU.mult
                           ).then_inc(S["dve_emptied"], 1)
                        split_hidden(turn, p, slice(0, T))

            def conv_feed_forward(s):
                a = act_before[s]
                at = PARAMS["ffn_conv"][0]
                dve.memset(conv_in[:, :, :, N_META - 2:N_META], 0.0)
                dve.drain()
                dve.sem_inc(S["conved"], 4)
                with dve.Fori(0, FT // 2) as turn:
                    for p in range(2):
                        for half in range(2):
                            tap = lambda n: par[:, bass.ds(turn * 2 + (at + 44 * n + 22 * half + p), 1)]
                            src, dst = conv_in[:, p, half, :], conv_out[:, p, half, TB]
                            dve.wait_ge(S["act_emptied"], turn * 4 + (a + 2 * p + half + 1))
                            dve.tensor_scalar(dst, src[:, TB], tap(2), None, ALU.mult)
                            dve.drain()
                            stt(dst, src[:, N_META - 1:T - 1], tap(1), dst, ALU.mult, ALU.add)
                            dve.drain()
                            stt(dst, src[:, N_META - 2:T - 2], tap(0), dst, ALU.mult, ALU.add
                                ).then_inc(S["conved"], 1)
                        dve.drain()
                        dve.wait_ge(S["silu_ready"], turn * 2 + (p + 1))
                        tt(hidden[:, p, TB], silu_out[:, p, TB], conv_out[:, p, 1, TB], ALU.mult)
                        split_hidden(turn, p, TB)

            def residual(name, nth=0, size=T, tokens=slice(0, T), factor=1.0):
                s = stage_number(name, nth)
                for i in range(DT):
                    tile = tiles_before[s] + i
                    dve.wait_ge(S["linear_ready"], tile + 1)
                    stt(X[:, i, tokens], ps[:, tile % 4, 0:size], factor, X[:, i, tokens], ALU.mult, ALU.add
                        ).then_inc(S["dve_emptied"], 1)
                dve.drain()
                dve.sem_inc(S["x_updated"], 1)

            def rk_prepare():
                dve.drain()
                tt(T1[:, :, 1:T], H[:, :, 0:T - 1], H[:, :, 1:T], ALU.subtract)
                dve.tensor_scalar(T1[:, :, 0:1], H[:, :, 0:1], -1.0, None, ALU.mult)
                dve.drain()
                names = ("rk_r", "rk_k", "rk_v", "rk_w1", "rk_a1", "rk_g1")
                for i, m in enumerate((0, 2, 3, 1, 4, 5)):
                    if i >= 2:
                        dve.wait_ge(S["linear_ready"], tiles_done(names[i - 2]))
                    for k in range(DT):
                        stt((T0, T2)[i % 2][:, k, :], T1[:, k, :], param("mix", m)[:, k:k + 1], H[:, k, :],
                            ALU.mult, ALU.add).then_inc(S["rk_mixed"], 1)
                R, K, V, W, B, G = (A[:, 8 * i:8 * i + 8, :] for i in range(6))
                dve.wait_ge(S["act_emptied"], owners[tiles_done("rk_g2") - 1][1])
                tt(T0[:, :, :], K, tiles_of(param("k_k"), DT, T), ALU.mult)
                dve.drain()
                tt(T1[:, :, :], T0[:, :, :], T0[:, :, :], ALU.mult).then_inc(S["rk_kk_squared"], 1)
                tt(T2[:, :, :], R, tiles_of(param("r_k"), DT, T), ALU.mult)
                dve.wait_ge(S["rk_kk_summed"], 1)
                dve.tensor_scalar(T1[:, :, :], ps[:, :, 0:T], 1e-24, None, ALU.max).then_inc(S["rk_kk_clamped"], 1)
                stt(H[:, :, :], B, -1.0, tiles_of(param("k_a"), DT, T), ALU.add, ALU.mult)
                dve.drain()
                stt(K, H[:, :, :], 1.0, K, ALU.add, ALU.mult)
                dve.wait_ge(S["rk_kk_rooted"], 1)
                dve.reciprocal(T1[:, :, :], T1[:, :, :])
                dve.drain()
                tt(T0[:, :, :], T0[:, :, :], T1[:, :, :], ALU.mult)
                dve.drain()
                tt(B, B, T0[:, :, :], ALU.mult)
                tt(T1[:, :, :], T2[:, :, :], K, ALU.mult).then_inc(S["rk_bonus_in"], 1)
                dve.tensor_scalar(W, W, -float(np.exp(-0.5)), None, ALU.mult)
                dve.drain()
                for k in range(DT):
                    dve.tensor_tensor_scan(T2[:, k, :], const("reset"), A[:, 24 + k, :], 0.0, ALU.mult, ALU.add)
                dve.wait_ge(S["rk_bonus_summed"], 1)
                tt(H[:, :, :], ps[:, :, 0:T], V, ALU.mult)
                dve.drain()
                for c, (t0, C) in enumerate(CHUNKS):
                    dve.tensor_copy(rk_mid[:, c, :], T2[:, :, t0 + C // 2])
                dve.drain()
                for c, (t0, C) in enumerate(CHUNKS):
                    tt(T2[:, :, t0:t0 + C], T2[:, :, t0:t0 + C], tiles_of(rk_mid[:, c, :], DT, C), ALU.subtract)
                dve.drain()
                tt(T1[:, :, :], T2[:, :, :], W, ALU.subtract)
                dve.drain()
                dve.sem_inc(S["rk_logs_ready"], 1)
                dve.wait_ge(S["rk_exps_ready"], 1)
                stt(T0[:, :, :], T0[:, :, :], -1.0, T1[:, :, :], ALU.mult, ALU.mult)
                dve.wait_ge(S["rk_exps_ready"], 2)
                tt(R, R, W, ALU.mult)
                for c, (t0, C) in enumerate(CHUNKS):
                    dve.tensor_copy(rk_end[:, c, :], A[:, 24:32, t0 + C - 1])
                dve.wait_ge(S["rk_exps_ready"], 3)
                tt(B, B, T2[:, :, :], ALU.mult)
                tt(K, K, T2[:, :, :], ALU.mult)
                dve.wait_ge(S["rk_exps_ready"], 4)
                dve.drain()
                tt(rk_end[:, 0:2, :], rk_end[:, 0:2, :], rk_mid_exp[:, 1:3, :], ALU.mult)
                dve.drain()
                dve.sem_inc(S["rk_prepared"], 1)

            def rk_mask(g, j, c):
                C = CHUNKS[c][1]
                mask = tri[0:C, :, 0:C].unsqueeze(1).to_broadcast([C, 4, 2, C])
                for i, bank, o in ((0, (2, 6)[j % 2], rk_lb[c]), (1, 4, rk_lk[c])):
                    dve.wait_ge(S["rk_products_ready"], g * 6 + (2 * j + i + 1))
                    v = ps[0:C, bank:bank + 2, :].rearrange("p b (u a t) -> p (b u) a t", u=2, a=2)[:, :, :, 0:C]
                    tt(o[0:C, :, :, :], v, mask, ALU.mult).then_inc(S["rk_masked"], 1)

            def rk_first_level(g, chunks):
                eye = lambda C: tokens_of(ident[0:C, 0:C], 4)
                for c in chunks:
                    C = CHUNKS[c][1]
                    tt(rk_xt[c][0:C, :, :], rk_lb[c][0:C, :, 0, :], tokens_of(const("level_0t")[0:C, 0:C], 4),
                       ALU.mult)
                for c in chunks:
                    C = CHUNKS[c][1]
                    dve.wait_ge(S[f"rk_under{c}_ready"], g * RK_LEVELS[c] + 1)
                    tt(rk_x[c][0:C, :, :], rk_level_bank(c, 0), tokens_of(level[0:C, 0, 0:C], 4), ALU.mult)
                dve.drain()
                for c in chunks:
                    C = CHUNKS[c][1]
                    for x in (rk_x[c][0:C, :, :], rk_xt[c][0:C, :, :]):
                        tt(x, x, eye(C), ALU.add).then_inc(S[f"rk_x{c}_added"], 1)

            def rk_level(g, n, chunks):
                for c in chunks:
                    C = CHUNKS[c][1]
                    dve.wait_ge(S[f"rk_under{c}_ready"], g * RK_LEVELS[c] + (n + 1))
                    tt(rk_ym[c][0:C, :, :], rk_level_bank(c, 0), tokens_of(level[0:C, n, 0:C], 4), ALU.mult
                       ).then_inc(S[f"rk_under{c}_masked"], 1)
                for c in chunks:
                    C = CHUNKS[c][1]
                    dve.wait_ge(S[f"rk_merge{c}_ready"], g * (RK_LEVELS[c] - 1) + n)
                    for i, x in ((1, rk_x[c][0:C, :, :]), (2, rk_xt[c][0:C, :, :])):
                        if i == 2 or n < RK_LEVELS[c] - 1:
                            tt(x, rk_level_bank(c, i), x, ALU.add).then_inc(S[f"rk_x{c}_added"], 1)

            def rk_state(g, c):
                C = CHUNKS[c][1]
                step = g * 3 + (c + 1)
                dve.wait_ge(S["rk_z_ready"], step)
                dve.tensor_copy(rk_z[0:C, :, :].rearrange("p (b u) v -> p b (u v)", b=2), ps[0:C, 0:2, 0:P]
                                ).then_inc(S["rk_z_copied"], 1)
                if c < 2:
                    dve.wait_ge(S["rk_s_ready"], g * 2 + (c + 1))
                    for par in range(2):
                        p = slice(HD * par, HD * par + HD)
                        v = ps[p, 6 + par, 0:P].rearrange("p (u v) -> p u v", u=2)
                        scale = rk_sc[p, c, :].unsqueeze(2).to_broadcast([HD, 2, HD])
                        if c:
                            tt(rk_s[p, 1, :, :], v, rk_s[p, 0, :, :], ALU.add)
                            dve.drain()
                            ins = tt(rk_s[p, 1, :, :], rk_s[p, 1, :, :], scale, ALU.mult)
                        else:
                            ins = tt(rk_s[p, 0, :, :], v, scale, ALU.mult)
                    ins.then_inc(S["rk_state_ready"], 1)

            def rk_stage(g):
                dve.wait_ge(S["rk_y_copied"], g * 3 + 1)
                for i, src in enumerate((T0[:, bass.ds(g * 2, 2), :], A[:, bass.ds(g * 2, 2), :])):
                    dve.tensor_copy(rk_ar[:, :, i, :], src)
                for i, first in enumerate((32, 8, 16)):
                    dve.tensor_copy(rk_bkv[:, i, :, :], A[:, bass.ds(g * 2 + first, 2), :])
                dve.tensor_copy(rk_sc[:, :, :], rk_end[:, 0:2, bass.ds(g * 2, 2)])
                dve.drain()
                dve.sem_inc(S["rk_staged"], 1)

            def rk_finish():
                Y = A[:, 24:32, :]
                dve.wait_ge(S["rk_y_summed"], 1)
                stt(Y, ps[:, :, 0:T], -1.0 / HD, Y, ALU.mult, ALU.add)
                dve.drain()
                tt(T1[:, :, :], Y, Y, ALU.mult).then_inc(S["rk_y_squared"], 1)
                dve.wait_ge(S["rk_y_rooted"], 1)
                dve.reciprocal(T1[:, :, :], T1[:, :, :])
                dve.drain()
                tt(Y, Y, T1[:, :, :], ALU.mult)
                dve.drain()
                for k in range(DT):
                    dve.tensor_scalar(A[:, 24 + k, :], A[:, 24 + k, :], param("lnx_g")[:, k:k + 1],
                                      param("lnx_b")[:, k:k + 1], ALU.mult, ALU.add)
                dve.drain()
                tt(Y, Y, H[:, :, :], ALU.add)
                dve.drain()
                tt(T0[:, :, :], Y, A[:, 40:48, :], ALU.mult).then_inc(S["rk_out_ready"], 1)

            def rope(first, count, swapped):
                tt(T0[:, 0:count, :], ps[:, 0:count, 0:T], tokens_of(const("sin"), count), ALU.mult)
                x = A[:, first:first + count, :]
                tt(x, x, tokens_of(const("cos"), count), ALU.mult)
                dve.drain()
                tt(x, x, T0[:, 0:count, :], ALU.add).then_inc(S[swapped], 1)

            def attend(g, pre, steps, gates):
                count = len(steps)

                def biased(n, c, t0, C, branch, keys, bias, *rest):
                    p = at_p[0:C, n % 2, :, 0:keys.shape[1]]
                    dve.wait_ge(S[pre + "_logits"], g * count + (n + 1))
                    stt(p, ps[0:C, 0:4, 0:keys.shape[1]], HD ** -0.5, tokens_of(bias[0:C, :], 4), ALU.mult, ALU.add
                        ).then_inc(S[pre + "_biased"], 1)
                    dve.drain()
                    dve.tensor_reduce(at_max[0:C, n % 2, :], p, AX_X, ALU.max, negate=True).then_inc(S[pre + "_max"], 1)

                def weighted(n, c, t0, C, branch, keys, *rest):
                    nk, inv = keys.shape[1], at_inv[0:C, n % 2, :]
                    p = at_p[0:C, n % 2, :, 0:nk]
                    dve.wait_ge(S[pre + "_exp"], g * count + (n + 1))
                    dve.reciprocal(inv, at_sum[0:C, n % 2, :])
                    dve.drain()
                    if gates:
                        tt(inv, inv, at_gg[:, c, :].rearrange("p (h b) -> p b h", b=3)[:, branch, :], ALU.mult)
                        dve.drain()
                    tt(p, p, inv.unsqueeze(2).to_broadcast([C, 4, nk]), ALU.mult).then_inc(S[pre + "_probs"], 1)

                for i in range(count + 1):
                    if i < count:
                        biased(*steps[i])
                    if i:
                        weighted(*steps[i - 1])

            def ds_select(n):
                c = n + 1
                score, a, b = T2[:, 0, :], T2[:, 1, :], T2[:, 2, :]
                dve.wait_ge(S["ds_relu"], n + 1)
                dve.tensor_scalar(score, T0[:, 0, :], ds_wi[:, n, 0:1], None, ALU.mult)
                for h in range(1, 8):
                    dve.drain()
                    ins = stt(score, T0[:, h, :], ds_wi[:, n, h:h + 1], score, ALU.mult, ALU.add)
                ins.then_inc(S["ds_scored"], 1)
                dve.drain()
                tt(score, score, const("causal")[:, c, :], ALU.mult)
                dve.drain()
                tt(a, score, const("neg")[:, c, :], ALU.add)
                for _ in range(8):
                    dve.drain()
                    dve.max(ds_top[:, :], a)
                    dve.drain()
                    dve.match_replace(b, ds_top[:, :], a, -3e38)
                    a, b = b, a
                dve.drain()
                stt(b, a, -2e38, const("causal")[:, c, :], ALU.is_lt, ALU.mult)
                dve.drain()
                dve.tensor_scalar(T1[:, c, :], b, -NEG, NEG, ALU.mult, ALU.add).then_inc(S["ds_selected"], 1)

            full = slice(0, T)
            dve.wait_ge(S["consts_loaded"], 32)
            norm(0, T, full, param("norm", 0))
            feed_forward(0)
            residual("ffn_out", 0, factor=0.5)
            norm(1, T, full, param("norm", 1))
            rk_prepare()
            with dve.Fori(0, 4) as g:
                rk_stage(g)
                for j, c in enumerate(RK_ORDER):
                    rk_mask(g, j, c)
                dve.drain()
                for n in range(LEVELS):
                    (rk_level(g, n, [c for c in RK_ORDER if n < RK_LEVELS[c]]) if n else
                     rk_first_level(g, RK_ORDER))
                for c in range(3):
                    rk_state(g, c)
            rk_finish()
            residual("rk_o")
            norm(2, T, full, param("norm", 2))
            feed_forward(stage_number("ffn", 1))
            residual("ffn_out", 1, factor=0.5)
            norm(3, T, full, param("norm", 3))
            feed_forward(stage_number("ffn", 2))
            residual("ffn_out", 2, factor=0.5)
            norm(4, T, full, param("norm", 4))
            dve.wait_ge(S["act_emptied"], owners[tiles_done("at_in") - 1][1])
            tt(A[:, 20:32, :], A[:, 0:12, :], A[:, 0:12, :], ALU.mult).then_inc(S["ds_squared"], 1)
            dve.wait_ge(S["ds_rooted"], 2)
            dve.reciprocal(A[:, 20:32, :], A[:, 20:32, :])
            dve.drain()
            stt(A[:, 0:8, :], A[:, 0:8, :], column("q_g"), A[:, 20:28, :], ALU.mult, ALU.mult)
            stt(A[:, 8:12, :], A[:, 8:12, :], column("k_g"), A[:, 28:32, :], ALU.mult, ALU.mult
                ).then_inc(S["ds_normed"], 1)
            for n, (first, count) in enumerate(((0, 8), (8, 4), (14, 5))):
                dve.wait_ge(S["ds_swapped"], n + 1)
                dve.drain()
                rope(first, count, "ds_roped")
            dve.tensor_copy(T1[:, 0, :], const("neg")[:, 0, :])
            dve.wait_ge(S["ds_turned_copied"], 1)
            for n in range(2):
                ds_select(n)
            with dve.Fori(0, 4) as g:
                dve.wait_ge(S["ds_o_copied"], g * 3 + 1)
                dve.tensor_copy(at_q[:, :, :], A[:, bass.ds(g * 2, 2), :])
                dve.tensor_copy(at_kg[:, 0:1, :], A[:, bass.ds(g + 8, 1), :])
                dve.tensor_copy(at_vg[0:N_META, 0:1, :], at_vtm[0:N_META, 0:1, bass.ds(g * HD, HD)])
                dve.tensor_copy(at_vg[:, 1:3, :], at_vtm[:, 1:3, bass.ds(g * HD, HD)])
                dve.drain()
                dve.sem_inc(S["ds_staged"], 1)
                attend(g, "ds", DSA_STEPS, False)
            residual("at_o")
            norm(5, T, full, param("norm", 5))
            feed_forward(stage_number("ffn", 3))
            residual("ffn_out", 3, factor=0.5)

            norm(6, SEQ, TB, param("norm2"))
            dve.wait_ge(S["ret_swapped"], 1)
            tt(T0[:, :, TB], ps[:, :, 0:SEQ], tokens_of(const("ret_sin"), DT), ALU.mult)
            tt(A[:, 0:8, TB], A[:, 0:8, TB], tokens_of(const("ret_cos"), DT), ALU.mult)
            dve.drain()
            tt(A[:, 0:8, TB], A[:, 0:8, TB], T0[:, :, TB], ALU.add).then_inc(S["ret_roped"], 1)
            dve.wait_ge(S["ret_scores"], 1)
            dve.wait_ge(S["decay_loaded"], 16)
            tt(ret_st.rearrange("p h c q -> p (h c q)"), ps[:, 4:8, :].rearrange("p a b -> p (a b)"), ret_decay,
               ALU.mult).then_inc(S["ret_masked"], 1)
            dve.wait_ge(S["ret_summed"], 1)
            pair = lambda v, j: v.rearrange("p (h j) t -> p h j t", j=2)[:, :, j, :]
            for j in range(2):
                o = pair(A[:, 40:48, TB], j)
                stt(o, ps[:, 0:4, 0:SEQ], -1.0 / SEQ, o, ALU.mult, ALU.add)
            dve.drain()
            tt(T0[:, :, TB], A[:, 40:48, TB], A[:, 40:48, TB], ALU.mult).then_inc(S["ret_squared"], 1)
            dve.wait_ge(S["ret_rooted"], 1)
            dve.reciprocal(T1[:, 4:8, TB], T1[:, 0:4, TB])
            dve.drain()
            for j in range(2):
                o = pair(A[:, 40:48, TB], j)
                tt(o, o, T1[:, 4:8, TB], ALU.mult)
            dve.drain()
            for k in range(DT):
                ins = stt(T0[:, k, TB], A[:, 40 + k, TB], param("ret_norm")[:, k:k + 1], A[:, 16 + k, TB],
                          ALU.mult, ALU.mult)
            ins.then_inc(S["ret_y_ready"], 1)
            dve.wait_ge(S["act_emptied"], owners[tiles_done("ret_mg") - 1][1])
            tt(T2[:, :, TB], A[:, 0:8, TB], A[:, 8:16, TB], ALU.mult).then_inc(S["merged"], 1)
            dve.wait_ge(S["act_emptied"], owners[tiles_done("sc_in") - 1][1])
            tt(A[:, 8:16, TB], A[:, 8:16, TB], A[:, 16:24, TB], ALU.mult)
            dve.memset(A[:, 8:16, N_META - 2:N_META], 0.0)
            for tap in (2, 1, 0):
                dve.drain()
                for k in range(DT):
                    w = param("sc_conv", tap)[:, k:k + 1]
                    src = A[:, 8 + k, N_META - 2 + tap:T - 2 + tap]
                    if tap == 2:
                        dve.tensor_scalar(T0[:, k, TB], src, w, None, ALU.mult)
                    else:
                        stt(T0[:, k, TB], src, w, T0[:, k, TB], ALU.mult, ALU.add)
            dve.drain()
            tt(T0[:, :, TB], T0[:, :, TB], A[:, 0:8, TB], ALU.mult).then_inc(S["sc_y_ready"], 1)
            dve.wait_ge(S["act_emptied"], owners[tiles_done("sc_mg") - 1][1])
            tt(A[:, 24:32, TB], A[:, 24:32, TB], A[:, 32:40, TB], ALU.mult)
            dve.drain()
            tt(T2[:, :, TB], T2[:, :, TB], A[:, 24:32, TB], ALU.add).then_inc(S["merged"], 1)
            dve.wait_ge(S["act_emptied"], owners[tiles_done("nsa_in") - 1][1])
            for kv in range(2):
                if kv:
                    dve.wait_ge(S["linear_ready"], tiles_done("cmp_k1"))
                for half in range(2):
                    p = slice(HD * half, HD * half + HD)
                    for m0 in range(2):
                        for g in range(4):
                            src = A[p, 8 + 4 * kv + g, TB].rearrange("p (c l) -> p l c", l=16)
                            o = ns_blk[p, 8 * m0:8 * m0 + 8, g * N_CMP:(g + 1) * N_CMP]
                            at = PARAMS["cmp_pos"][0] + 16 * kv + 8 * m0
                            pos = par[p, at:at + 8].unsqueeze(2).to_broadcast([HD, 8, N_CMP])
                            ins = tt(o, src[:, half::2, m0:m0 + N_CMP], pos, ALU.add)
                ins.then_inc(S["ns_blocks"], 1)
            dve.wait_ge(S["ns_turned_copied"], 1)
            for c in range(2):
                at = CONSTS["any_cmp"][0] + c
                o = ns_gate[:, c, :].rearrange("p (h b) -> p b h", b=3)[:, 0, :]
                dve.tensor_scalar(o, o, con[:, at:at + 1], None, ALU.mult)
            dve.wait_ge(S["act_emptied"], owners[tiles_done("cmp_v2") - 1][1])
            dve.drain()
            with dve.Fori(0, 4) as g:
                dve.wait_ge(S["ns_o_copied"], g * 2 + 1)
                dve.tensor_copy(at_q[:, :, TB], A[:, bass.ds(g * 2, 2), TB])
                for b in range(2):
                    dve.tensor_copy(at_kg[:, b:b + 1, TB], A[:, bass.ds(g + (16 + 4 * b), 1), TB])
                dve.tensor_copy(at_vg[:, 0:4, :], at_vtm[:, :, bass.ds(g * HD, HD)])
                dve.tensor_copy(ns_kc[:, :], ns_cmp_k[:, bass.ds(g * N_CMP, N_CMP)])
                dve.tensor_copy(ns_vc[0:N_CMP, :], ns_cmp_v[0:N_CMP, bass.ds(g, 1), :].rearrange("p a v -> p (a v)"))
                dve.tensor_copy(at_gg[:, :, :], ns_gate[:, :, bass.ds(g * 12, 12)])
                dve.drain()
                dve.sem_inc(S["ns_staged"], 1)
                attend(g, "ns", NSA_STEPS, True)
            dve.wait_ge(S["act_emptied"], owners[tiles_done("nsa_mg") - 1][1])
            tt(A[:, 0:8, TB], A[:, 0:8, TB], A[:, 8:16, TB], ALU.mult)
            dve.drain()
            tt(T2[:, :, TB], T2[:, :, TB], A[:, 0:8, TB], ALU.add).then_inc(S["merged"], 1)
            residual("mix_out", size=SEQ, tokens=TB)
            norm(7, SEQ, TB, param("ffn_norm2"))
            conv_feed_forward(stage_number("ffn2"))
            residual("ffn_out", 4, SEQ, TB)
            norm(8, SEQ, TB, param("final"), "final_ready")


def weight_stream(inp):
    def tiles(w, interleave=False):
        k, n = w.shape
        kt, nt = -(-k // P), -(-n // P)
        if (k, n) != (kt * P, nt * P):
            w = np.pad(w, ((0, kt * P - k), (0, nt * P - n)))
        t = w.reshape(kt, P, nt, P).transpose(2, 0, 1, 3)
        if interleave:
            t = np.stack([t[:nt // 2], t[nt // 2:]], axis=1)
        return t.reshape(kt * nt, P, P)

    def twice(w):
        k, n = w.shape
        return np.repeat(w.reshape(k, n // HD, 1, HD), 2, axis=2).reshape(k, 2 * n)

    def ffn(i, j):
        return [tiles(inp["ffn_w_in"][i, j], True)], [tiles(inp["ffn_w_out"][i, j])]

    at = inp["at_w_in"][0]
    z = inp["w_in_2"][0]
    cut = np.cumsum([0, 512, 512, 1024, 1024, 1024, 1024, 1024, 1024, 1536, 48, 3072])
    z = [z[:, a:b] for a, b in zip(cut[:-1], cut[1:])]
    kc, vc, ks, vs, kw, vw = np.split(z[8], 6, axis=1)
    mg = np.split(z[10], 3, axis=1)
    many = lambda *ws: [tiles(w) for w in ws]
    per_stage = [
        *ffn(0, 0), many(inp["rk_w_r"][0]), many(inp["rk_w_k"][0]), many(inp["rk_w_v"][0]),
        many(inp["rk_w1"][0]), many(inp["rk_w2"][0]), many(inp["rk_a1"][0]), many(inp["rk_a2"][0]),
        many(inp["rk_g1"][0]), many(inp["rk_g2"][0]), many(inp["rk_w_o"][0]),
        *ffn(0, 1), *ffn(1, 0),
        many(at[:, :1024], twice(at[:, 1024:1280]), at[:, 1280:1536], at[:, 1536:2048], twice(at[:, 2048:2112]),
             at[:, 2112:]),
        many(inp["at_w_o"][0]), *ffn(1, 1),
        many(z[0], z[1], z[2], z[3]), many(inp["w_ret_out_2"][0]), many(mg[0]),
        many(z[4], z[5], z[6]), many(inp["w_sc_out_2"][0]), many(mg[1]),
        many(z[7], twice(kc), twice(vc), twice(ks), twice(kw), vs, vw, z[9]),
        many(inp["nsa_cmp_w1_2"][0, 0]), many(twice(inp["nsa_cmp_w2_2"][0, 0])),
        many(inp["nsa_cmp_w1_2"][0, 1]), many(inp["nsa_cmp_w2_2"][0, 1]),
        many(inp["w_nsa_out_2"][0]), many(mg[2]), many(inp["w_mix_out_2"][0]),
        [tiles(inp["w_ffn_up_2"][0], True)], [tiles(inp["w_ffn_down_2"][0])],
    ]
    out = np.zeros((N_SLOTS * PER, P, P), np.float32)
    assert len(per_stage) == len(STAGES)
    for start, (name, kt, nt), parts in zip(STARTS, STAGES, per_stage):
        assert sum(len(t) for t in parts) == kt * nt, name
        for t in parts:
            out[start:start + len(t)] = t
            start += len(t)
    return np.ascontiguousarray(out.reshape(N_SLOTS, PER, P, P).transpose(0, 2, 1, 3)).reshape(N_SLOTS, P, PER * P)


def parameters(inp):
    f = lambda v: np.reshape(v, (-1, P)).T
    pos = inp["nsa_cmp_pos_2"][0].reshape(2, 16, P)
    cols = {
        "norm": f(inp["norm_g"]), "mix": f(inp["rk_mix"]), "w0": f(inp["rk_w0"]), "a0": f(inp["rk_a0"]),
        "k_k": f(inp["rk_k_k"]), "k_a": f(inp["rk_k_a"]), "r_k": f(inp["rk_r_k"]), "lnx_g": f(inp["rk_lnx_g"]),
        "lnx_b": f(inp["rk_lnx_b"]), "q_g": f(np.tile(inp["at_q_g"][0], 2)), "k_g": f(np.tile(inp["at_k_g"][0], 2)),
        "norm2": f(inp["attn_norm_w_2"]), "ret_norm": f(inp["ret_norm_w_2"]), "sc_conv": f(inp["sc_conv_w_2"]),
        "cmp_pos": f(pos), "ffn_norm2": f(inp["ffn_norm_w_2"]), "ffn_conv": f(inp["ffn_conv_w_2"]),
        "final": f(inp["final_norm_w_2"]),
    }
    for name, (_, n) in PARAMS.items():
        assert cols[name].shape[1] == n, name
    return np.concatenate([cols[n] for n in PARAMS], axis=1)


def kernel(**inputs):
    import concourse.bacc as _bacc
    from concourse.bass_utils import run_bass_kernel_spmd as _run

    inp = {k: np.asarray(v) for k, v in inputs.items()}
    x = np.concatenate([inp["meta"], inp["x"][0]], axis=0)
    arrays = {
        "stream": weight_stream(inp),
        "x_in": x.T.reshape(DT, P, T).transpose(1, 0, 2),
        "params": parameters(inp),
        "consts": constants(),
        "decay": retention_decay(),
    }
    arrays = {k: np.ascontiguousarray(v) for k, v in arrays.items()}
    nc = _bacc.Bacc("TRN2", target_bir_lowering=False, num_devices=1)
    args = [nc.dram_tensor(k, v.shape, F32, kind="ExternalInput").ap() for k, v in arrays.items()]
    out = nc.dram_tensor("out", (P, DT * SEQ), F32, kind="ExternalOutput").ap()
    build(nc, *args, out)
    got = _run(nc, [arrays], core_ids=[0]).results[0]["out"]
    return np.ascontiguousarray(np.reshape(got, (P, DT, SEQ)).transpose(2, 1, 0)).reshape(1, SEQ, D)
```

```python
from contextlib import ExitStack

import numpy as np

import concourse.bass as bass
from concourse import mybir

ALU = mybir.AluOpType
ACT = mybir.ActivationFunctionType
F32 = mybir.dt.float32
F32R = mybir.dt.float32r
AX_X = mybir.AxisListType.X

P = 128
D = 1024
DT = D // P
SEQ = 256
N_META = 16
T = SEQ + N_META
CHUNKS = [(0, N_META), (N_META, P), (N_META + P, P)]
HD = 64
FF = 2816
FT = FF // P
N_CMP = 15
RING = 4
PER = 16
HALF = PER // 2
SPLIT_RING = 4
FFN_SLOTS = 3 * FT * DT // PER
LEVELS = 7
NEG = -1e30

STAGES = [
    ("ffn", DT, 2 * FT), ("ffn_out", FT, DT),
    ("rk_r", DT, 8), ("rk_k", DT, 8), ("rk_v", DT, 8), ("rk_w1", DT, 1), ("rk_w2", 1, 8),
    ("rk_a1", DT, 1), ("rk_a2", 1, 8), ("rk_g1", DT, 2), ("rk_g2", 2, 8), ("rk_o", DT, 8),
    ("ffn", DT, 2 * FT), ("ffn_out", FT, DT),
    ("ffn", DT, 2 * FT), ("ffn_out", FT, DT),
    ("at_in", DT, 20), ("at_o", DT, 8),
    ("ffn", DT, 2 * FT), ("ffn_out", FT, DT),
    ("ret_in", DT, 24), ("ret_mg", DT, 8), ("ret_out", DT, 8),
    ("sc_in", DT, 24), ("sc_mg", DT, 8), ("sc_out", DT, 8),
    ("nsa_in", DT, 29), ("nsa_mg", DT, 8), ("cmp_k1", 16, 2), ("cmp_k2", 2, 1), ("cmp_v1", 16, 2), ("cmp_v2", 2, 1),
    ("nsa_out", DT, 8),
    ("mix_out", DT, 8),
    ("ffn2", DT, 2 * FT), ("ffn_out", FT, DT),
]


def whole(name):
    return name in ("rk_w1", "rk_w2", "rk_a1", "rk_a2", "rk_g1", "rk_g2") or name.startswith("cmp_")


def stage_starts():
    starts, at = [], 0
    for s, (name, kt, nt) in enumerate(STAGES):
        if name in ("ffn", "ffn2") or whole(name) != whole(STAGES[s - 1][0]):
            at = -(-at // PER) * PER
        starts.append(at)
        at += kt * nt
    return starts, -(-at // PER)


STARTS, N_SLOTS = stage_starts()
WHOLE_SLOTS = {(start + i) // PER for start, (name, kt, nt) in zip(STARTS, STAGES) if whole(name)
               for i in range(kt * nt)}
SPLIT_SLOTS = [n for n in range(N_SLOTS) if n not in WHOLE_SLOTS]


def half_at(pos):
    return 2 * (pos // PER - len([n for n in WHOLE_SLOTS if n < pos // PER])) + pos % PER // HALF

PARAMS = {}


def _param(name, columns):
    PARAMS[name] = (sum(c for _, c in PARAMS.values()), columns)


for _n, _c in (("norm", 48), ("mix", 48), ("w0", 8), ("a0", 8), ("k_k", 8), ("k_a", 8), ("r_k", 8),
               ("lnx_g", 8), ("lnx_b", 8), ("q_g", 1), ("k_g", 1), ("norm2", 8), ("ret_norm", 8),
               ("sc_conv", 24), ("cmp_pos", 32), ("ffn_norm2", 8), ("ffn_conv", 132), ("final", 8)):
    _param(_n, _c)
N_PARAM = sum(c for _, c in PARAMS.values())

CONSTS = {}


def _const(name, *shape):
    CONSTS[name] = (sum(int(np.prod(s)) for _, s in CONSTS.values()), shape)


for _n, _s in (("ident", (P,)), ("ones", (P,)), ("head_ones", (P,)), ("rope_swap", (P,)), ("ret_swap", (P,)),
               ("level", (LEVELS, P)), ("level_0t", (P,)), ("tri", (2, P)), ("reset", (T,)), ("cos", (T,)), ("sin", (T,)),
               ("ret_cos", (SEQ,)), ("ret_sin", (SEQ,)), ("causal", (3, T)), ("neg", (3, T)),
               ("neg_cmp", (2, N_CMP)), ("any_cmp", (2,)), ("eps", (3,))):
    _const(_n, *_s)
N_CONST = sum(int(np.prod(s)) for _, s in CONSTS.values())
EPS_RMS, EPS_LNX, EPS_RET = range(3)


def constants():
    c = {n: np.zeros((P,) + s, np.float32) for n, (_, s) in CONSTS.items()}
    r = np.arange(P)
    c["ident"][:] = np.eye(P)
    c["ones"][:] = 1
    c["head_ones"][:] = (r[:, None] // HD == r[None, :] // HD)
    for name, width, half in (("rope_swap", HD, 8), ("ret_swap", P, 64)):
        for base in range(0, P, width):
            for d in range(half):
                c[name][base + d + half, base + d] = -1
                c[name][base + d, base + half + d] = 1
    for n in range(LEVELS):
        m = 1 << n
        t, s = r[:, None], r[None, :]
        c["level"][:, n] = (t // (2 * m) == s // (2 * m)) & (t // m % 2 == 1) & (s // m % 2 == 0)
    c["level_0t"][:] = c["level"][:, 0].T
    c["tri"][:, 0] = r[:, None] < r[None, :]
    c["tri"][:, 1] = r[:, None] <= r[None, :]
    c["reset"][:] = 1
    for t0, _ in CHUNKS:
        c["reset"][:, t0] = 0
    inv = (np.float32(500000.0) ** (-np.arange(0, 16, 2, dtype=np.float32) / 16)).astype(np.float32)
    ang = (np.arange(T, dtype=np.float32)[:, None] * inv).astype(np.float32)
    d = r % HD
    c["cos"][:] = np.where(d[:, None] < 16, np.cos(ang).T[d % 8], 1)
    c["sin"][:] = np.where(d[:, None] < 16, np.sin(ang).T[d % 8], 0)
    theta = (np.float32(10000.0) ** (-np.linspace(0, 1, 64, dtype=np.float32))).astype(np.float32)
    ang = (np.arange(SEQ, dtype=np.float32)[:, None] * theta).astype(np.float32)
    c["ret_cos"][:] = np.cos(ang).T[r % 64]
    c["ret_sin"][:] = np.sin(ang).T[r % 64]
    for n, (t0, size) in enumerate(CHUNKS):
        c["causal"][:, n] = np.arange(T)[None] <= t0 + r[:, None]
    c["neg"][:] = (c["causal"] - 1) * -NEG
    for n in range(2):
        t = n * P + r
        c["neg_cmp"][:, n] = np.where(np.arange(N_CMP) * 16 + 31 <= t[:, None], 0, NEG)
        c["any_cmp"][:, n] = t >= 31
    c["eps"][:] = (1e-6, 64e-5, 1e-6)
    return np.concatenate([c[n].reshape(P, -1) for n in CONSTS], axis=1)


def retention_decay():
    gamma = np.log1p(-(2.0 ** (-5.0 - np.arange(4))))
    key = np.arange(P)[:, None, None] + np.arange(2)[None, :, None] * P
    rel = np.arange(SEQ)[None, None, :] - key
    out = [np.where(rel >= 0, np.exp(g * np.maximum(rel, 0)), 0) * P ** -0.5 for g in gamma]
    return np.stack(out, axis=1).astype(np.float32).reshape(P, -1)


def build(nc, stream, x_in, params, consts, decay, out):
    with ExitStack() as ctx:
        class Semaphores(dict):
            def __missing__(self, name):
                self[name] = ctx.enter_context(nc.semaphore(name))
                return self[name]

        S = Semaphores()

        place = [-(-nc.sbuf_base // 32) * 32]

        def at_next(name, shape, dtype=F32):
            t = nc.alloc_sbuf_tensor_at(name, shape, dtype, offset=place[0])
            place[0] += -(-int(np.prod(shape[1:])) * 4 // 32) * 32
            return t

        X = at_next("X", [P, DT, T])
        wring = at_next("wring", [P, RING, PER * P])
        par = at_next("par", [P, N_PARAM])
        con = at_next("con", [P, N_CONST])
        rms = at_next("rms", [P, 2, T])
        small = at_next("small", [P, 704])
        shared = place[0]
        w_high = at_next("w_high", [P, SPLIT_RING, HALF * P], F32R)
        w_low = at_next("w_low", [P, SPLIT_RING, HALF * P], F32R)
        place[0] = shared
        group = at_next("group", [P, 9664])
        in_high = at_next("in_high", [P, DT, T], F32R)
        in_low = at_next("in_low", [P, DT, T], F32R)
        alone = place[0]
        H = at_next("H", [P, DT, T])
        out_parts = place[0]
        T0 = at_next("T0", [P, DT, T])
        T1 = at_next("T1", [P, DT, T])
        T2 = at_next("T2", [P, DT, T])
        A = at_next("A", [P, 48, T])
        place[0] = out_parts
        out_high = at_next("out_high", [P, DT, T], F32R)
        out_low = at_next("out_low", [P, DT, T], F32R)
        place[0] = alone
        hid_high = at_next("hid_high", [P, FT, T], F32R)
        hid_low = at_next("hid_low", [P, FT, T], F32R)
        normed = at_next("normed", [P, DT, T])
        silu_out = at_next("silu_out", [P, 2, T])
        hidden = at_next("hidden", [P, 2, T])
        conv_in = at_next("conv_in", [P, 2, 2, T])
        conv_out = at_next("conv_out", [P, 2, 2, T])
        ps = ctx.enter_context(nc.psum_tensor("ps", [P, 8, 512], F32))

        def const(name):
            at, shape = CONSTS[name]
            v = con[:, at:at + int(np.prod(shape))]
            return v.rearrange("p (a b) -> p a b", a=shape[0]) if len(shape) == 2 else v

        def param(name, n=0):
            at = PARAMS[name][0] + 8 * n
            return par[:, at:at + 8]

        def column(name, n=0):
            at = PARAMS[name][0] + n
            return par[:, at:at + 1]

        def eps(n):
            at = CONSTS["eps"][0] + n
            return con[:, at:at + 1]

        def carve(owner, *shapes):
            at, views = 0, []
            for shape in shapes:
                n = int(np.prod(shape))
                v = owner[:, at:at + n]
                if len(shape) == 2:
                    v = v.rearrange("p (a b) -> p a b", a=shape[0])
                if len(shape) == 3:
                    v = v.rearrange("p (a b c) -> p a b c", a=shape[0], b=shape[1])
                if len(shape) == 4:
                    v = v.rearrange("p (a b c d) -> p a b c d", a=shape[0], b=shape[1], c=shape[2])
                views.append(v)
                at += n
            assert at <= owner.shape[1], at
            return views

        ident, ones, head_ones = const("ident"), const("ones"), const("head_ones")
        rope_swap, ret_swap, level, tri = const("rope_swap"), const("ret_swap"), const("level"), const("tri")

        RK_ORDER = (1, 2, 0)
        RK_LEVELS = [C.bit_length() - 1 for _, C in CHUNKS]
        rk_ar, rk_bkv, rk_s, rk_sc, *rest = carve(
            group, (2, 2, T), (3, 2, T), (2, 2, HD), (2, 2), *[(6, P)] * 3, *[(4, 2, C) for _, C in CHUNKS] * 2)
        rk_tm, rk_lb, rk_lk = rest[0:3], rest[3:6], rest[6:9]
        rest = carve(T1[:, :, :].rearrange("p a t -> p (a t)"), *[(4, C) for _, C in CHUNKS] * 2)
        rk_x, rk_xt = rest[0:3], rest[3:6]
        *rk_ym, rk_z, rk_sa = carve(T2[:, :, :].rearrange("p a t -> p (a t)"), *[(4, C) for _, C in CHUNKS],
                                    (4, HD), (4, HD))
        rk_mid, rk_mid_exp, rk_end = carve(small, (3, 8), (3, 8), (3, 8))
        (rk_lora,) = carve(group, (4, T))
        (at_q, at_kg, at_vg, at_p, at_pt, at_vtm, at_gg, at_max, at_sum, at_inv) = carve(
            group, (2, T), (2, T), (6, HD), (2, 4, T), (3, 4, P), (4, 256), (2, 12), (2, 4), (2, 4), (2, 4))
        (ns_blk,) = carve(group[:, 2 * SPLIT_RING * HALF * P:], (16, 4 * N_CMP))
        (ns_gate, ns_cmp_hid, ns_cmp_k, ns_cmp_v, ns_kc, ns_vc, ds_wi, ds_top) = carve(
            small, (2, 48), (2, 4 * N_CMP), (4 * N_CMP,), (4, HD), (N_CMP,), (HD,), (2, 8), (8,))
        ret_vt = A[:, 24:32, :].rearrange("p a t -> p (a t)")[:, 0:2048].rearrange("p (c j v) -> p c j v", c=2, j=8)
        ret_st = A[:, 32:40, :].rearrange("p a t -> p (a t)")[:, 0:2048].rearrange("p (h c q) -> p h c q", h=4, c=2)
        ret_decay = T1[:, :, :].rearrange("p a t -> p (a t)")[:, 0:2048]

        DSA_STEPS = [(c, c, t0, C, 0, at_kg[:, 0, 0:t0 + C], T1[:, c, 0:t0 + C],
                      [(k0, KC, at_vg[0:KC, kc, :]) for kc, (k0, KC) in enumerate(CHUNKS[:c + 1])], True, True)
                     for c, (t0, C) in enumerate(CHUNKS)]
        NSA_STEPS = []
        for c in range(2):
            t0, keys = N_META + c * P, (c + 1) * P
            NSA_STEPS.append((3 * c, c, t0, P, 0, ns_kc[:, :], const("neg_cmp")[:, c, :],
                              [(0, N_CMP, ns_vc[0:N_CMP, :])], True, False))
            for b in range(2):
                NSA_STEPS.append((3 * c + 1 + b, c, t0, P, 1 + b, at_kg[:, b, N_META:N_META + keys],
                                  const("neg")[:, 1 + c, N_META:N_META + keys],
                                  [(kc * P, P, at_vg[:, 2 * kc + b, :]) for kc in range(c + 1)], False, b == 1))

        block = ctx.enter_context(nc.Block())
        TB = slice(N_META, T)

        def rk_level_bank(c, i):
            C = CHUNKS[c][1]
            bank, at = ((6 + i // 2, i % 2 * 256), (i, 0), (3 + i, 0))[c]
            return ps[0:C, bank, at:at + 4 * C].rearrange("p (q t) -> p q t", q=4)

        EMPTIED_BY = {"rk_o": "dve", "at_o": "dve", "mix_out": "dve", "ffn_out": "dve", "cmp_v2": "act"}
        tiles_before, act_before, dve_before, owners = [], [], [], []
        n_act = n_dve = 2
        for name, kt, nt in STAGES:
            tiles_before.append(len(owners))
            act_before.append(n_act)
            dve_before.append(n_dve)
            for i in range(nt):
                if name == "ffn":
                    by = "act" if i % 2 == 0 else "dve"
                else:
                    by = EMPTIED_BY.get(name, "act")
                if by == "act":
                    n_act += 1
                    owners.append(("act_emptied", n_act))
                else:
                    n_dve += 1
                    owners.append(("dve_emptied", n_dve))

        FFN_STAGES = [i for i, st in enumerate(STAGES) if st[0] in ("ffn", "ffn2")]
        FFN_NORMS = (0, 2, 3, 5, 7)
        SPLIT_NORMS = (0, 2, 3, 4, 5, 6, 7)
        BEFORE_NORM = [None] + [i for i, st in enumerate(STAGES) if st[0] in ("ffn_out", "rk_o", "at_o", "mix_out")]
        OUTS = ("rk_o", "at_o", "ret_out", "sc_out", "nsa_out", "mix_out")

        def stage_number(name, nth=0):
            return [i for i, s in enumerate(STAGES) if s[0] == name][nth]

        def tiles_done(name, nth=0):
            s = stage_number(name, nth)
            return tiles_before[s] + STAGES[s][2]

        @block.sync
        def _(sp):
            sp.dma_start(con[:, :], consts).then_inc(S["consts_loaded"], 16)
            sp.dma_start(par[:, :], params).then_inc(S["consts_loaded"], 16)
            sp.dma_start(X[:, :, :], x_in).then_inc(S["x_loaded"], 16)
            loaded = [S[f"slot{i}_loaded"] for i in range(RING)]

            def load(slot, number):
                sp.dma_start(wring[:, slot, :], stream[number]).then_inc(loaded[slot], 16)

            for n in range(RING):
                load(n, n)
            runs = []
            counts = {"slots_split": 0, "slots_used": 0}
            for n in range(N_SLOTS - RING):
                name = "slots_used" if n in WHOLE_SLOTS else "slots_split"
                counts[name] += 1
                if runs and runs[-1][2] == name:
                    runs[-1][1] += 1
                else:
                    runs.append([n + RING, 1, name, counts[name]])
            for first, count, name, value in runs:
                whole = count // RING * RING
                if whole > RING:
                    with sp.Fori(0, count // RING) as r:
                        for n in range(RING):
                            slot = (first + n) % RING
                            sp.wait_ge(S[name], r * RING + (value + n))
                            sp.dma_start(wring[:, slot, :], stream[bass.ds(r * RING + (first + n), 1)].rearrange(
                                "a p n -> p (a n)")).then_inc(loaded[slot], 16)
                else:
                    whole = 0
                for n in range(whole, count):
                    sp.wait_ge(S[name], value + n)
                    load((first + n) % RING, first + n)
            sp.wait_ge(S["final_ready"], DT)
            sp.dma_start(out.rearrange("p (a t) -> p a t", a=DT), H[:, :, TB]).then_inc(S["out_stored"], 16)
            sp.wait_ge(S["out_stored"], 16)

        @block.tensor
        def _(pe):
            used_pending = [False]
            half_pending = [1]
            next_half = [0]

            def weight_tile(pos, turn=None):
                number, j = divmod(pos, PER)
                slot = number % RING
                if j == 0:
                    value = 16 * (number // RING + 1)
                    pe.wait_ge(S[f"slot{slot}_loaded"], value if turn is None else turn * 16 + value)
                return wring[:, slot, j * P:(j + 1) * P]

            def out_tile(bank, pos, rhs, kt, turn=None, size=T, before_k=None):
                for k in range(kt):
                    w = weight_tile(pos + k, turn)
                    if before_k:
                        before_k(k)
                    mm = pe.matmul(ps[:, bank, 0:size], w, rhs(k), start=(k == 0), stop=(k == kt - 1))
                    if k == kt - 1:
                        mm.then_inc(S["linear_ready"], 1)
                    elif used_pending[0]:
                        mm.then_inc(S["slots_used"], 1)
                        used_pending[0] = False
                    if (pos + k) % PER == PER - 1:
                        assert not used_pending[0]
                        used_pending[0] = True

            def bank_free(tile):
                if tile >= 4:
                    name, value = owners[tile - 4]
                    pe.wait_ge(S[name], value)

            def split_out_tile(bank, pos, kt, high, low, turn=None, size=T, before_k=None):
                for k in range(kt):
                    half, j = half_at(pos + k), (pos + k) % HALF
                    if j == 0:
                        if turn is None:
                            half_pending[0] += half - next_half[0]
                        next_half[0] = half + 1
                        pe.wait_ge(S["w_split"], half + 1 if turn is None else turn * 2 * RING + (half + 1))
                    w = slice(j * P, (j + 1) * P)
                    wh, wl = w_high[:, half % SPLIT_RING, w], w_low[:, half % SPLIT_RING, w]
                    if before_k:
                        before_k(k)
                    o = ps[:, bank, 0:size]
                    mm = pe.matmul(o, wh, high(k), start=(k == 0), stop=False)
                    if half_pending[0]:
                        mm.then_inc(S["halves_used"], half_pending[0])
                        half_pending[0] = 0
                    mm = pe.matmul(o, wh, low(k), start=False, stop=False)
                    if used_pending[0]:
                        mm.then_inc(S["slots_used"], 1)
                        used_pending[0] = False
                    mm = pe.matmul(o, wl, high(k), start=False, stop=(k == kt - 1))
                    if j == HALF - 1:
                        half_pending[0] = 1
                mm.then_inc(S["linear_ready"], 1)

            def linear(name, rhs, nth=0, size=T, before_k=None):
                s = stage_number(name, nth)
                _, kt, nt = STAGES[s]
                for i in range(nt):
                    tile = tiles_before[s] + i
                    bank_free(tile)
                    out_tile(tile % 4, STARTS[s] + i * kt, rhs, kt, None, size, before_k if i == 0 else None)

            def split_linear(name, high, low, size=T, before_k=None):
                s = stage_number(name)
                _, kt, nt = STAGES[s]
                for i in range(nt):
                    tile = tiles_before[s] + i
                    bank_free(tile)
                    split_out_tile(tile % 4, STARTS[s] + i * kt, kt, high, low, None, size,
                                   before_k if i == 0 else None)
                    if s in BEFORE_NORM and i >= 2:
                        norm_sum(BEFORE_NORM.index(s), i - 2, size)

            def normed_linear(name, n, size=T, tokens=slice(0, T)):
                split_linear(name, lambda k: in_high[:, k, tokens], lambda k: in_low[:, k, tokens], size,
                             lambda k: pe.wait_ge(S["in_split"], DT * SPLIT_NORMS.index(n) + k + 1))

            def out_linear(name, size=T, tokens=slice(0, T)):
                split_linear(name, lambda k: out_high[:, k, tokens], lambda k: out_low[:, k, tokens], size,
                             lambda k: pe.wait_ge(S["out_split"], 4 * OUTS.index(name) + k // 2 + 1))

            def feed_forward(f, size=T, tokens=slice(0, T)):
                s = FFN_STAGES[f]
                base, a, d = tiles_before[s], act_before[s], dve_before[s]
                conv = STAGES[s][0] == "ffn2"
                for tile in range(base, base + 4):
                    if tile >= 4:
                        bank_free(tile)

                def pair(turn, p):
                    for half in range(2):
                        if conv:
                            value, step, name = a + 2 * (p - 2) + half + 1, 2 * RING, "act_emptied"
                        elif half == 0:
                            value, step, name = a + p - 1, RING, "act_emptied"
                        else:
                            value, step, name = d + p - 1, RING, "dve_emptied"
                        pe.wait_ge(S[name], value if turn is None else turn * step + value)
                        there = None
                        if p == half == 0:
                            there = lambda k: pe.wait_ge(S["in_split"], DT * SPLIT_NORMS.index(FFN_NORMS[f]) + k + 1)
                        split_out_tile((base + 2 * p + half) % 4, STARTS[s] + (2 * p + half) * DT, DT,
                                       lambda k: in_high[:, k, tokens], lambda k: in_low[:, k, tokens],
                                       turn, size, there)

                assert half_pending[0]
                alone = FT % RING
                for p in range(alone):
                    pair(None, p)
                with pe.Fori(0, FT // RING) as turn:
                    for p in range(alone, alone + RING):
                        pair(turn, p)
                next_half[0] = half_at(STARTS[s + 1])
                s += 1
                for i in range(DT):
                    tile = tiles_before[s] + i
                    bank_free(tile)
                    split_out_tile(tile % 4, STARTS[s] + i * FT, FT,
                                   lambda k: hid_high[:, k, tokens], lambda k: hid_low[:, k, tokens], None, size,
                                   (lambda k: pe.wait_ge(S["hidden_split"], FT * f + k + 1)) if i == 0 else None)
                    if i >= 2 and BEFORE_NORM.index(s) != 6:
                        norm_sum(BEFORE_NORM.index(s), i - 2, size)

            def norm_sum(n, k, size):
                pe.wait_ge(S["squares_ready"], DT * n + k + 1)
                mm = pe.matmul(ps[:, 4, 0:size], ones, normed[:, k, T - size:T], start=(k == 0), stop=(k == DT - 1))
                if k == DT - 1:
                    mm.then_inc(S["square_sum_ready"], 1)

            def norm_sums(n, size=T, first=DT - 2):
                for k in range(first, DT):
                    norm_sum(n, k, size)

            def per_tile(weights, source, banks, size, done):
                for i, bank in enumerate(banks):
                    mm = pe.matmul(ps[:, bank, 0:size], weights, source(i), start=True, stop=True)
                mm.then_inc(S[done], 1)

            def settle(C):
                if C < 32:
                    pe.sem_inc(S["few_rows_waited"], 1)

            rk_heads = [(2 * par + u, par, u, HD * par) for par in range(2) for u in range(2)]

            def rk_products(g, j, c):
                t0, C = CHUNKS[c]
                now = slice(t0, t0 + C)
                if j:
                    pe.wait_ge(S["rk_tm_copied"], g * 3 + j)
                settle(C)
                for i in range(3):
                    for u in range(2):
                        n = 2 * i + u
                        mm = pe.transpose(ps[0:C, n // 4, n % 4 * P:(n % 4 + 1) * P], rk_bkv[:, i, u, now], ident)
                mm.then_inc(S["rk_turned"], 1)
                for i, bank in ((0, (2, 6)[j % 2]), (1, 4)):
                    if i and j:
                        pe.wait_ge(S["rk_masked"], g * 6 + 2 * j)
                        settle(C)
                    for q, par, u, p in rk_heads:
                        o = ps[0:C, bank + par, u * 256:(u + 1) * 256].rearrange("p (a t) -> p a t", a=2)[:, :, 0:C]
                        mm = pe.matmul(o, rk_bkv[p:p + HD, i, u, now], rk_ar[p:p + HD, u, :, now],
                                       start=True, stop=True)
                    mm.then_inc(S["rk_products_ready"], 1)

            def rk_under(g, c, n):
                C, nl = CHUNKS[c][1], RK_LEVELS[c]
                if n:
                    pe.wait_ge(S[f"rk_x{c}_added"], g * (2 * nl - 1) + (2 * n - 1))
                    settle(C)
                for q in range(4):
                    mm = pe.matmul(rk_level_bank(c, 0)[:, q, :], rk_lb[c][0:C, q, 0, :],
                                   rk_x[c][0:C, q, :] if n else ident[0:C, 0:C], start=True, stop=True)
                mm.then_inc(S[f"rk_under{c}_ready"], 1)

            def rk_merge(g, c, n):
                C, nl = CHUNKS[c][1], RK_LEVELS[c]
                pe.wait_ge(S[f"rk_x{c}_added"], g * (2 * nl - 1) + 2 * n)
                pe.wait_ge(S[f"rk_under{c}_masked"], g * (nl - 1) + n)
                settle(C)
                for q in range(4):
                    xt, y = rk_xt[c][0:C, q, :], rk_ym[c][0:C, q, :]
                    if n < nl - 1:
                        pe.matmul(rk_level_bank(c, 1)[:, q, :], xt, y, start=True, stop=True)
                    mm = pe.matmul(rk_level_bank(c, 2)[:, q, :], y, xt, start=True, stop=True)
                mm.then_inc(S[f"rk_merge{c}_ready"], 1)

            def rk_state(g, c):
                t0, C = CHUNKS[c]
                step = g * 3 + (c + 1)
                now = slice(t0, t0 + C)
                tm, lb, lk = rk_tm[c], rk_lb[c], rk_lk[c]
                if c:
                    pe.wait_ge(S["rk_state_ready"], g * 2 + c)
                for q, par, u, p in rk_heads:
                    o = ps[0:C, par, u * HD:(u + 1) * HD]
                    if c:
                        pe.matmul(o, rk_ar[p:p + HD, u, 0, now], rk_s[p:p + HD, c - 1, u, :], start=True, stop=False)
                    mm = pe.matmul(o, lk[0:C, q, 0, :], tm[0:C, 4 + u, p:p + HD], start=(c == 0), stop=True)
                mm.then_inc(S["rk_z_ready"], 1)
                pe.wait_ge(S["rk_z_copied"], step)
                pe.wait_ge(S[f"rk_x{c}_added"], (g + 1) * (2 * RK_LEVELS[c] - 1))
                settle(C)
                for q in range(4):
                    mm = pe.matmul(ps[0:C, 3, q * HD:(q + 1) * HD], rk_xt[c][0:C, q, :], rk_z[0:C, q, :],
                                   start=True, stop=True)
                mm.then_inc(S["rk_sa_ready"], 1)
                pe.wait_ge(S["rk_sa_copied"], step)
                settle(0)
                if c < 2:
                    for q, par, u, p in rk_heads:
                        o = ps[p:p + HD, 6 + par, u * HD:(u + 1) * HD]
                        pe.matmul(o, tm[0:C, u, p:p + HD], rk_sa[0:C, q, :], start=True, stop=False)
                        mm = pe.matmul(o, tm[0:C, 2 + u, p:p + HD], tm[0:C, 4 + u, p:p + HD],
                                       start=False, stop=True)
                    mm.then_inc(S["rk_s_ready"], 1)
                pe.wait_ge(S["rk_y_copied"], step)
                if c == 0:
                    pe.wait_ge(S["rk_x2_added"], (g + 1) * (2 * RK_LEVELS[2] - 1))
                settle(0)
                for q, par, u, p in rk_heads:
                    o = ps[p:p + HD, 4 + par, u * P:u * P + C]
                    if c:
                        pe.matmul(o, rk_s[p:p + HD, c - 1, u, :], rk_ar[p:p + HD, u, 1, now], start=True, stop=False)
                    pe.matmul(o, rk_sa[0:C, q, :], lb[0:C, q, 1, :], start=(c == 0), stop=False)
                    mm = pe.matmul(o, tm[0:C, 4 + u, p:p + HD], lk[0:C, q, 1, :], start=False, stop=True)
                mm.then_inc(S["rk_y_ready"], 1)

            def attend(g, pre, steps, o_bank):
                count, chunks = len(steps), steps[-1][1] + 1

                def logits(n, c, t0, C, _, keys, *rest):
                    if n == 0:
                        pe.wait_ge(S[pre + "_staged"], g + 1)
                    else:
                        pe.wait_ge(S[pre + "_biased"], g * count + n)
                    settle(C)
                    for h in range(4):
                        p = HD * (h % 2)
                        mm = pe.matmul(ps[0:C, h, 0:keys.shape[1]], at_q[p:p + HD, h // 2, t0:t0 + C],
                                       keys[p:p + HD, :], start=True, stop=True)
                    mm.then_inc(S[pre + "_logits"], 1)

                def values(n, c, t0, C, _, keys, bias, parts, first, last):
                    pe.wait_ge(S[pre + "_probs"], g * count + (n + 1))
                    settle(C)
                    for kc, (k0, KC, _) in enumerate(parts):
                        for h in range(4):
                            mm = pe.transpose(ps[0:KC, 4 + kc, h * P:h * P + C], at_p[0:C, n % 2, h, k0:k0 + KC],
                                              ident[0:C, 0:C])
                    mm.then_inc(S[pre + "_turned_probs"], 1)
                    pe.wait_ge(S[pre + "_probs_copied"], g * count + (n + 1))
                    if first:
                        pe.wait_ge(S[pre + "_o_copied"], g * chunks + (c + 1))
                    settle(C)
                    for h in range(4):
                        p, u = HD * (h % 2), h // 2
                        for kc, (k0, KC, v) in enumerate(parts):
                            mm = pe.matmul(ps[p:p + HD, o_bank(u), u * P:u * P + C], v, at_pt[0:KC, kc, h, 0:C],
                                           start=(first and kc == 0), stop=(last and kc == len(parts) - 1))
                    if last:
                        mm.then_inc(S[pre + "_o_ready"], 1)

                for i in range(count + 1):
                    if i < count:
                        logits(*steps[i])
                    if i:
                        values(*steps[i - 1])

            pe.sem_inc(S["act_emptied"], 2)
            pe.sem_inc(S["dve_emptied"], 2)
            pe.wait_ge(S["consts_loaded"], 32)
            full = slice(0, T)
            norm_sums(0, first=0)
            feed_forward(0)

            norm_sums(1)
            for i, (name, high, low) in enumerate((("rk_r", in_high, in_low), ("rk_k", out_high, out_low),
                                                   ("rk_v", in_high, in_low))):
                split_linear(name, lambda k: high[:, k, :], lambda k: low[:, k, :],
                             before_k=lambda k: pe.wait_ge(S["rk_mixed"], 4 * i + k // 2 + 1))
            pe.wait_ge(S["rk_mixed"], 20)
            linear("rk_w1", lambda k: T0[:, k, :])
            pe.wait_ge(S["act_emptied"], owners[tiles_done("rk_w1") - 1][1])
            linear("rk_w2", lambda k: rk_lora[:, 0, :])
            pe.wait_ge(S["rk_mixed"], 28)
            linear("rk_a1", lambda k: T1[:, k, :])
            pe.wait_ge(S["act_emptied"], owners[tiles_done("rk_a1") - 1][1])
            linear("rk_a2", lambda k: rk_lora[:, 1, :])
            pe.wait_ge(S["rk_mixed"], 36)
            linear("rk_g1", lambda k: T0[:, k, :])
            pe.wait_ge(S["act_emptied"], owners[tiles_done("rk_g1") - 1][1])
            linear("rk_g2", lambda k: rk_lora[:, 2 + k, :])
            pe.wait_ge(S["rk_kk_squared"], 1)
            pe.wait_ge(S["act_emptied"], owners[tiles_done("rk_g2") - 1][1])
            per_tile(head_ones, lambda i: T1[:, i, :], range(8), T, "rk_kk_summed")
            pe.wait_ge(S["rk_bonus_in"], 1)
            per_tile(head_ones, lambda i: T1[:, i, :], range(8), T, "rk_bonus_summed")
            pe.wait_ge(S["rk_prepared"], 1)
            with pe.Fori(0, 4) as g:
                pe.wait_ge(S["rk_staged"], g + 1)
                for j, c in enumerate(RK_ORDER):
                    rk_products(g, j, c)
                pe.wait_ge(S["rk_masked"], g * 6 + 6)
                pe.wait_ge(S["rk_tm_copied"], g * 3 + 3)
                settle(0)
                for n in range(LEVELS):
                    chunks = [c for c in RK_ORDER if n < RK_LEVELS[c]]
                    for c in chunks:
                        rk_under(g, c, n)
                    for c in chunks if n else ():
                        rk_merge(g, c, n)
                for c in range(3):
                    rk_state(g, c)
            pe.wait_ge(S["rk_y_copied"], 13)
            pe.wait_ge(S["rk_state_ready"], 8)
            per_tile(head_ones, lambda i: A[:, 24 + i, :], range(8), T, "rk_y_summed")
            pe.wait_ge(S["rk_y_squared"], 1)
            per_tile(head_ones, lambda i: T1[:, i, :], range(8), T, "rk_y_var")
            out_linear("rk_o")

            norm_sums(2)
            feed_forward(1)
            norm_sums(3)
            feed_forward(2)

            norm_sums(4)
            normed_linear("at_in", 4)
            pe.wait_ge(S["ds_squared"], 1)
            per_tile(head_ones, lambda i: A[:, 20 + i, :], range(8), T, "ds_summed")
            pe.wait_ge(S["ds_rooted"], 1)
            per_tile(head_ones, lambda i: A[:, 28 + i, :], range(4), T, "ds_summed")
            pe.wait_ge(S["ds_normed"], 1)
            pe.wait_ge(S["ds_rooted"], 2)
            for i, first, count in ((0, 0, 8), (1, 8, 4), (2, 14, 5)):
                if i:
                    pe.wait_ge(S["ds_roped"], i)
                per_tile(rope_swap, lambda j: A[:, first + j, :], range(count), T, "ds_swapped")
            pe.wait_ge(S["ds_roped"], 3)
            for c, (t0, C) in enumerate(CHUNKS):
                for j in range(2):
                    pe.transpose(ps[0:C, c, j * P:(j + 1) * P], A[:, 12 + j, t0:t0 + C], ident)
                mm = pe.transpose(ps[0:C, c, 2 * P:3 * P], A[:, 19, t0:t0 + C], ident)
            mm.then_inc(S["ds_turned"], 1)
            pe.wait_ge(S["ds_turned_copied"], 1)
            for n, (t0, C) in enumerate(CHUNKS[1:]):
                if n:
                    pe.wait_ge(S["ds_relu"], n)
                for h in range(8):
                    p = HD * (h % 2)
                    mm = pe.matmul(ps[:, h, 0:T], A[p:p + HD, 14 + h // 2, t0:t0 + C], A[p:p + HD, 18, :],
                                   start=True, stop=True)
                mm.then_inc(S["ds_index_ready"], 1)
            pe.wait_ge(S["ds_relu"], 2)
            pe.wait_ge(S["ds_selected"], 2)
            with pe.Fori(0, 4) as g:
                attend(g, "ds", DSA_STEPS, lambda u: 7)
            out_linear("at_o")
            norm_sums(5)
            feed_forward(3)

            norm_sums(6, SEQ, 0)
            normed_linear("ret_in", 6, SEQ, TB)
            pe.wait_ge(S["act_emptied"], owners[tiles_done("ret_in") - 1][1])
            per_tile(ret_swap, lambda i: A[:, i, TB], range(8), SEQ, "ret_swapped")
            pe.wait_ge(S["ret_roped"], 1)
            for c in range(2):
                for j in range(8):
                    mm = pe.transpose(ps[:, 2 * c + j // 4, (j % 4) * P:(j % 4 + 1) * P],
                                      A[:, 8 + j, N_META + c * P:N_META + (c + 1) * P], ident)
            mm.then_inc(S["ret_v_turned"], 1)
            for h in range(4):
                for kc in range(2):
                    mm = pe.matmul(ps[:, 4 + h, kc * SEQ:(kc + 1) * SEQ],
                                   A[:, 4 + h, N_META + kc * P:N_META + (kc + 1) * P], A[:, h, TB],
                                   start=True, stop=True)
            mm.then_inc(S["ret_scores"], 1)
            pe.wait_ge(S["ret_v_copied"], 1)
            pe.wait_ge(S["ret_masked"], 1)
            for j in range(8):
                for kc in range(2):
                    mm = pe.matmul(ps[:, j, 0:SEQ], ret_vt[:, kc, j, :], ret_st[:, j // 2, kc, :],
                                   start=(kc == 0), stop=(kc == 1))
            mm.then_inc(S["ret_o_ready"], 1)
            pe.wait_ge(S["ret_o_copied"], 1)
            for h in range(4):
                for j in range(2):
                    mm = pe.matmul(ps[:, h, 0:SEQ], ones, A[:, 40 + 2 * h + j, TB], start=(j == 0), stop=(j == 1))
            mm.then_inc(S["ret_summed"], 1)
            pe.wait_ge(S["ret_squared"], 1)
            for h in range(4):
                for j in range(2):
                    mm = pe.matmul(ps[:, h, 0:SEQ], ones, T0[:, 2 * h + j, TB], start=(j == 0), stop=(j == 1))
            mm.then_inc(S["ret_var"], 1)
            pe.wait_ge(S["ret_rooted"], 1)
            normed_linear("ret_mg", 6, SEQ, TB)
            out_linear("ret_out", SEQ, TB)
            normed_linear("sc_in", 6, SEQ, TB)
            normed_linear("sc_mg", 6, SEQ, TB)
            out_linear("sc_out", SEQ, TB)

            normed_linear("nsa_in", 6, SEQ, TB)
            normed_linear("nsa_mg", 6, SEQ, TB)
            pe.wait_ge(S["act_emptied"], owners[tiles_done("nsa_in") - 1][1])
            for c in range(2):
                t0 = N_META + c * P
                for j in range(4):
                    pe.transpose(ps[:, 4 + c, j * P:(j + 1) * P], A[:, 24 + j, t0:t0 + P], ident)
                mm = pe.transpose(ps[:, 6, c * P:(c + 1) * P], A[:, 28, t0:t0 + P], ident)
            mm.then_inc(S["ns_turned"], 1)
            pe.wait_ge(S["ns_blocks"], 1)
            linear("cmp_k1", lambda k: ns_blk[:, k, :], size=4 * N_CMP)
            pe.wait_ge(S["act_emptied"], owners[tiles_done("cmp_k1") - 1][1])
            linear("cmp_k2", lambda k: ns_cmp_hid[:, k, :], size=4 * N_CMP)
            pe.wait_ge(S["ns_blocks"], 2)
            pe.wait_ge(S["act_emptied"], owners[tiles_done("cmp_k2") - 1][1])
            linear("cmp_v1", lambda k: ns_blk[:, k, :], size=4 * N_CMP)
            pe.wait_ge(S["act_emptied"], owners[tiles_done("cmp_v1") - 1][1])
            s = stage_number("cmp_v2")
            tile = tiles_before[s]
            bank_free(tile)
            w = [weight_tile(STARTS[s] + k) for k in range(2)]
            assert STARTS[s] % PER < PER - 2
            for g in range(4):
                for k in range(2):
                    mm = pe.matmul(ps[0:N_CMP, tile % 4, g * HD:(g + 1) * HD],
                                   ns_cmp_hid[:, k, g * N_CMP:(g + 1) * N_CMP], w[k][:, 0:HD],
                                   start=(k == 0), stop=(k == 1))
            mm.then_inc(S["linear_ready"], 1)
            used_pending[0] = True
            pe.wait_ge(S["act_emptied"], owners[tile][1])
            pe.wait_ge(S["ns_turned_copied"], 1)
            with pe.Fori(0, 4) as g:
                attend(g, "ns", NSA_STEPS, lambda u: 7 - u)
            out_linear("nsa_out", SEQ, TB)
            out_linear("mix_out", SEQ, TB)
            norm_sums(7, SEQ)
            feed_forward(4, SEQ, TB)
            norm_sums(8, SEQ)

        @block.scalar
        def _(act):
            def copy(o, i, scale=1.0):
                return act.activation(o, i, ACT.Copy, scale=scale)

            def linear(name, put, func=lambda i: ACT.Copy, bias=None, nth=0, size=T):
                s = stage_number(name, nth)
                for i in range(STAGES[s][2]):
                    tile = tiles_before[s] + i
                    act.wait_ge(S["linear_ready"], tile + 1)
                    kw = {} if bias is None else {"bias": bias[:, i:i + 1]}
                    act.activation(put(i), ps[:, tile % 4, 0:size], func(i), **kw).then_inc(S["act_emptied"], 1)

            squared = [0]

            def square(k):
                n, k = divmod(k, DT)
                if n:
                    act.wait_ge(S["dve_emptied"], dve_before[BEFORE_NORM[n]] + k + 1)
                tokens = TB if n >= 6 else slice(0, T)
                act.activation(normed[:, k, tokens], X[:, k, tokens], ACT.Square).then_inc(S["squares_ready"], 1)
                squared[0] += 1

            def norm(n, size, tokens):
                if n in FFN_NORMS:
                    high_parts(FFN_NORMS.index(n), 0)
                if n == 0:
                    act.wait_ge(S["x_loaded"], 16)
                for k in range(squared[0], DT * n + DT):
                    square(k)
                act.wait_ge(S["square_sum_ready"], n + 1)
                act.activation(rms[:, 0, 0:size], ps[:, 4, 0:size], ACT.Sqrt, bias=eps(EPS_RMS), scale=1.0 / D
                               ).then_inc(S["rms_ready"], 1)

            def high_part(half, turn=None):
                number, h = SPLIT_SLOTS[half // 2], half % 2
                slot, value = number % RING, 16 * (number // RING + 1)
                if h == 0:
                    act.wait_ge(S[f"slot{slot}_loaded"], value if turn is None else turn * 16 + value)
                if half >= SPLIT_RING:
                    value = half - SPLIT_RING + 2
                    act.wait_ge(S["halves_used"], value if turn is None else turn * 2 * RING + value)
                copy(w_high[:, half % SPLIT_RING, :], wring[:, slot, h * HALF * P:(h + 1) * HALF * P]
                     ).then_inc(S["w_high_ready"], 1)

            def high_parts(f, i, turn=None):
                for h in range(2):
                    high_part(half_at(STARTS[FFN_STAGES[f]]) + 2 * i + h, turn)

            done = [0]

            def high_parts_to(half):
                for n in range(done[0], half):
                    high_part(n)
                done[0] = max(done[0], half)

            def begin(name):
                high_parts_to(half_at(STARTS[stage_number(name)]) + 2)

            def split_linear(name, put=None, func=lambda i: ACT.Copy, size=T):
                s = last = stage_number(name)
                while not whole(STAGES[last + 1][0]) and STAGES[last + 1][0] not in ("at_o", "ffn", "ffn2"):
                    last += 1
                end = -(-half_at(STARTS[last] + STAGES[last][1] * STAGES[last][2]) // 2) * 2
                for i in range(STAGES[s][2]):
                    high_parts_to(min(half_at(STARTS[s]) + i + 4, end))
                    if not put and i:
                        square(squared[0])
                    tile = tiles_before[s] + i
                    if put:
                        act.wait_ge(S["linear_ready"], tile + 1)
                        act.activation(put(i), ps[:, tile % 4, 0:size], func(i)).then_inc(S["act_emptied"], 1)

            def input_high(n, tokens, source):
                for k in range(DT):
                    act.wait_ge(S["normed_ready"], DT * SPLIT_NORMS.index(n) + k + 1)
                    copy(in_high[:, k, tokens], source[:, k, tokens]).then_inc(S["in_high_ready"], 1)

            def feed_forward(f, size=T, tokens=slice(0, T)):
                s = FFN_STAGES[f]
                base, a, d = tiles_before[s], act_before[s], dve_before[s]
                conv = STAGES[s][0] == "ffn2"
                input_high(FFN_NORMS[f], tokens, normed)
                high_parts(f, 1)

                def pair(turn, p):
                    after = lambda value, step: value if turn is None else turn * step + value
                    if conv:
                        act.wait_ge(S["conved"], after(2 * p + 2, 2 * RING))
                        for half in range(2):
                            act.wait_ge(S["linear_ready"], after(base + 2 * p + half + 1, 2 * RING))
                            copy(conv_in[:, p % 2, half, TB], ps[:, (base + 2 * p + half) % 4, 0:SEQ]
                                 ).then_inc(S["act_emptied"], 1)
                        high_parts(f, p + 2, turn)
                        act.wait_ge(S["conved"], after(2 * p + 5, 2 * RING))
                        if turn is not None or p >= 2:
                            act.wait_ge(S["hidden_split"], after(FT * f + p - 1, RING))
                        act.activation(silu_out[:, p % 2, TB], conv_out[:, p % 2, 0, TB], ACT.Silu
                                       ).then_inc(S["silu_ready"], 1)
                    else:
                        act.wait_ge(S["linear_ready"], after(base + 2 * p + 1, 2 * RING))
                        act.wait_ge(S["dve_emptied"], after(d + p - 1, RING))
                        act.activation(silu_out[:, p % 2, :], ps[:, (base + 2 * p) % 4, 0:T], ACT.Silu
                                       ).then_inc(S["act_emptied"], 1)
                        high_parts(f, p + 2, turn)

                alone = FT % RING
                for p in range(alone):
                    pair(None, p)
                with act.Fori(0, FT // RING) as turn:
                    for p in range(alone, alone + RING):
                        pair(turn, p)
                for i in range(FT + 2, FFN_SLOTS):
                    high_parts(f, i)
                    for k in range(DT):
                        if (2 * FT * DT + (k + 1) * FT) / HALF <= 2 * i + 1 - 3 and squared[0] % DT == k:
                            square(squared[0])
                done[0] = half_at(STARTS[s]) + 2 * FFN_SLOTS

            def rk_turn(g, j, c):
                C = CHUNKS[c][1]
                act.wait_ge(S["rk_turned"], g * 3 + (j + 1))
                copy(rk_tm[c][0:C, 0:4, :], ps[0:C, 0, :].rearrange("p (a t) -> p a t", a=4))
                copy(rk_tm[c][0:C, 4:6, :], ps[0:C, 1, 0:256].rearrange("p (a t) -> p a t", a=2)
                     ).then_inc(S["rk_tm_copied"], 1)

            def rk_state(g, c):
                t0, C = CHUNKS[c]
                step = g * 3 + (c + 1)
                act.wait_ge(S["rk_sa_ready"], step)
                copy(rk_sa[0:C, :, :], ps[0:C, 3, 0:256].rearrange("p (a t) -> p a t", a=4)
                     ).then_inc(S["rk_sa_copied"], 1)
                act.wait_ge(S["rk_y_ready"], step)
                for par in range(2):
                    p = HD * par
                    ins = copy(A[p:p + HD, bass.ds(g * 2 + 24, 2), t0:t0 + C],
                               ps[p:p + HD, 4 + par, 0:256].rearrange("p (a t) -> p a t", a=2)[:, :, 0:C])
                ins.then_inc(S["rk_y_copied"], 1)

            def attend(g, pre, steps, put):
                count = len(steps)
                chunks = steps[-1][1] + 1

                def exponentials(n, c, t0, C, _, keys, *rest):
                    act.wait_ge(S[pre + "_max"], g * count + (n + 1))
                    for h in range(4):
                        row = at_p[0:C, n % 2, h, 0:keys.shape[1]]
                        ins = act.activation(row, row, ACT.Exp, bias=at_max[0:C, n % 2, h:h + 1],
                                             accum_out=at_sum[0:C, n % 2, h:h + 1])
                    ins.then_inc(S[pre + "_exp"], 1)

                def copies(n, c, t0, C, _, keys, bias, parts, first, last):
                    act.wait_ge(S[pre + "_turned_probs"], g * count + (n + 1))
                    for kc, (k0, KC, _) in enumerate(parts):
                        ins = copy(at_pt[0:KC, kc, :, 0:C],
                                   ps[0:KC, 4 + kc, :].rearrange("p (a t) -> p a t", a=4)[:, :, 0:C])
                    ins.then_inc(S[pre + "_probs_copied"], 1)
                    if last:
                        act.wait_ge(S[pre + "_o_ready"], g * chunks + (c + 1))
                        put(g, t0, C).then_inc(S[pre + "_o_copied"], 1)

                for i in range(count + 1):
                    if i < count:
                        exponentials(*steps[i])
                    if i:
                        copies(*steps[i - 1])

            full = slice(0, T)
            act.wait_ge(S["consts_loaded"], 32)
            norm(0, T, full)
            feed_forward(0)
            begin("rk_r")
            norm(1, T, full)
            split_linear("rk_r", lambda i: A[:, i, :])
            split_linear("rk_k", lambda i: A[:, 8 + i, :])
            split_linear("rk_v", lambda i: A[:, 16 + i, :])
            linear("rk_w1", lambda i: rk_lora[:, 0, :], lambda i: ACT.Tanh)
            linear("rk_w2", lambda i: A[:, 24 + i, :], lambda i: ACT.Sigmoid, param("w0"))
            linear("rk_a1", lambda i: rk_lora[:, 1, :])
            linear("rk_a2", lambda i: A[:, 32 + i, :], lambda i: ACT.Sigmoid, param("a0"))
            linear("rk_g1", lambda i: rk_lora[:, 2 + i, :], lambda i: ACT.Sigmoid)
            linear("rk_g2", lambda i: A[:, 40 + i, :])
            act.wait_ge(S["rk_kk_clamped"], 1)
            act.activation(T1[:, :, :], T1[:, :, :], ACT.Sqrt).then_inc(S["rk_kk_rooted"], 1)
            act.wait_ge(S["rk_logs_ready"], 1)
            act.activation(T1[:, :, :], T1[:, :, :], ACT.Exp).then_inc(S["rk_exps_ready"], 1)
            act.activation(A[:, 24:32, :], T2[:, :, :], ACT.Exp).then_inc(S["rk_exps_ready"], 1)
            act.drain()
            act.activation(T2[:, :, :], T2[:, :, :], ACT.Exp, scale=-1.0).then_inc(S["rk_exps_ready"], 1)
            act.activation(rk_mid_exp[:, :, :], rk_mid[:, :, :], ACT.Exp).then_inc(S["rk_exps_ready"], 1)
            act.sem_inc(S["rk_y_copied"], 1)
            with act.Fori(0, 4) as g:
                for j, c in enumerate(RK_ORDER):
                    rk_turn(g, j, c)
                for c in range(3):
                    rk_state(g, c)
            begin("rk_o")
            act.wait_ge(S["rk_y_var"], 1)
            act.activation(T1[:, :, :], ps[:, :, 0:T], ACT.Sqrt, bias=eps(EPS_LNX), scale=1.0 / HD
                           ).then_inc(S["rk_y_rooted"], 1)
            split_linear("rk_o")
            norm(2, T, full)
            feed_forward(1)
            norm(3, T, full)
            feed_forward(2)
            begin("at_in")
            norm(4, T, full)
            input_high(4, full, T0)
            split_linear("at_in", lambda i: A[:, i, :])
            for n, (first, count) in enumerate(((20, 8), (28, 4))):
                act.wait_ge(S["ds_summed"], n + 1)
                act.activation(A[:, first:first + count, :], ps[:, 0:count, 0:T], ACT.Sqrt, bias=eps(EPS_RMS),
                               scale=1.0 / HD).then_inc(S["ds_rooted"], 1)
            act.wait_ge(S["ds_turned"], 1)
            for c, (t0, C) in enumerate(CHUNKS):
                ins = copy(at_vtm[0:C, c, :], ps[0:C, c, 0:256])
                if c:
                    ins = copy(ds_wi[:, c - 1, :], ps[:, c, 256:264], scale=8 ** -0.5 * HD ** -0.5)
            ins.then_inc(S["ds_turned_copied"], 1)
            for n in range(2):
                act.wait_ge(S["ds_index_ready"], n + 1)
                if n:
                    act.wait_ge(S["ds_scored"], n)
                act.activation(T0[:, :, :], ps[:, :, 0:T], ACT.Relu).then_inc(S["ds_relu"], 1)
            act.sem_inc(S["ds_o_copied"], 1)

            def put_ds(g, t0, C):
                return copy(T2[:, bass.ds(g * 2, 2), t0:t0 + C],
                            ps[:, 7, 0:256].rearrange("p (a t) -> p a t", a=2)[:, :, 0:C])

            with act.Fori(0, 4) as g:
                attend(g, "ds", DSA_STEPS, put_ds)
            begin("at_o")
            split_linear("at_o")
            norm(5, T, full)
            feed_forward(3)

            begin("ret_in")
            norm(6, SEQ, TB)
            act.dma_start(ret_decay, decay).then_inc(S["decay_loaded"], 16)
            input_high(6, TB, T0)
            split_linear("ret_in", lambda i: A[:, i, TB], lambda i: ACT.Silu if i >= 16 else ACT.Copy, size=SEQ)
            act.wait_ge(S["ret_v_turned"], 1)
            copy(ret_vt.rearrange("p c j v -> p (c j v)"), ps[:, 0:4, :].rearrange("p a b -> p (a b)")
                 ).then_inc(S["ret_v_copied"], 1)
            act.wait_ge(S["ret_o_ready"], 1)
            copy(A[:, 40:48, TB], ps[:, :, 0:SEQ]).then_inc(S["ret_o_copied"], 1)
            act.wait_ge(S["ret_var"], 1)
            act.activation(T1[:, 0:4, TB], ps[:, 0:4, 0:SEQ], ACT.Sqrt, bias=eps(EPS_RET), scale=1.0 / SEQ
                           ).then_inc(S["ret_rooted"], 1)
            split_linear("ret_mg", lambda i: A[:, 8 + i, TB], lambda i: ACT.Sigmoid, size=SEQ)
            split_linear("ret_out", lambda i: A[:, i, TB], size=SEQ)
            act.wait_ge(S["merged"], 1)
            split_linear("sc_in", lambda i: A[:, i, TB], size=SEQ)
            split_linear("sc_mg", lambda i: A[:, 32 + i, TB], lambda i: ACT.Sigmoid, size=SEQ)
            split_linear("sc_out", lambda i: A[:, 24 + i, TB], size=SEQ)
            act.wait_ge(S["merged"], 2)
            split_linear("nsa_in", lambda i: A[:, i, TB], lambda i: ACT.Sigmoid if i == 28 else ACT.Copy, size=SEQ)
            split_linear("nsa_mg", lambda i: A[:, 32 + i, TB], lambda i: ACT.Sigmoid, size=SEQ)
            act.wait_ge(S["w_split"], done[0])
            act.wait_ge(S["ns_turned"], 1)
            for c in range(2):
                copy(at_vtm[:, 2 * c:2 * c + 2, :], ps[:, 4 + c, :].rearrange("p (a v) -> p a v", a=2))
                ins = copy(ns_gate[:, c, :], ps[:, 6, c * P:c * P + 48])
            ins.then_inc(S["ns_turned_copied"], 1)
            linear("cmp_k1", lambda i: ns_cmp_hid[:, i, :], lambda i: ACT.Gelu_apprx_tanh, size=4 * N_CMP)
            linear("cmp_k2", lambda i: ns_cmp_k[:, :], size=4 * N_CMP)
            linear("cmp_v1", lambda i: ns_cmp_hid[:, i, :], lambda i: ACT.Gelu_apprx_tanh, size=4 * N_CMP)
            tile = tiles_before[stage_number("cmp_v2")]
            act.wait_ge(S["linear_ready"], tile + 1)
            copy(ns_cmp_v[0:N_CMP, :, :], ps[0:N_CMP, tile % 4, 0:256].rearrange("p (a v) -> p a v", a=4)
                 ).then_inc(S["act_emptied"], 1)
            act.sem_inc(S["ns_o_copied"], 1)

            def put_ns(g, t0, C):
                copy(H[:, bass.ds(g * 2, 1), t0:t0 + C], ps[:, 7:8, 0:C])
                return copy(H[:, bass.ds(g * 2 + 1, 1), t0:t0 + C], ps[:, 6:7, P:P + C])

            with act.Fori(0, 4) as g:
                attend(g, "ns", NSA_STEPS, put_ns)
            begin("nsa_out")
            split_linear("nsa_out", lambda i: A[:, i, TB], size=SEQ)
            split_linear("mix_out")
            norm(7, SEQ, TB)
            feed_forward(4, SEQ, TB)
            norm(8, SEQ, TB)

        @block.gpsimd
        def _(pool):
            def low_parts(slot, half, turn=None):
                for h in range(2):
                    value = half + h + 1
                    pool.wait_ge(S["w_high_ready"], value if turn is None else turn * 2 * RING + value)
                    pool.tensor_tensor(w_low[:, (half + h) % SPLIT_RING, :],
                                       wring[:, slot, h * HALF * P:(h + 1) * HALF * P],
                                       w_high[:, (half + h) % SPLIT_RING, :].bitcast(F32), ALU.subtract
                                       ).then_inc(S["w_split"], 1)
                pool.drain()
                pool.sem_inc(S["slots_split"], 1)

            runs = []
            for n in SPLIT_SLOTS:
                if runs and n == sum(runs[-1]):
                    runs[-1][1] += 1
                else:
                    runs.append([n, 1])
            for first, count in runs:
                half = half_at(first * PER)
                with pool.Fori(0, count // RING) as turn:
                    for i in range(RING):
                        low_parts((first + i) % RING, half + 2 * i, turn)
                for i in range(count // RING * RING, count):
                    low_parts((first + i) % RING, half + 2 * i)

        @block.vector
        def _(dve):
            def tt(o, a, b, op):
                return dve.tensor_tensor(o, a, b, op)

            def stt(o, a, scalar, b, op0, op1):
                return dve.scalar_tensor_tensor(out=o, in0=a, scalar=scalar, in1=b, op0=op0, op1=op1)

            def tiles_of(v, n, size):
                return v.unsqueeze(2).to_broadcast([P, n, size])

            def tokens_of(v, n):
                return v.unsqueeze(1).to_broadcast([v.shape[0], n, v.shape[1]])

            def norm(n, size, tokens, gain, done="h_ready"):
                dve.drain()
                dve.wait_ge(S["rms_ready"], n + 1)
                dve.reciprocal(rms[:, 1, 0:size], rms[:, 0, 0:size])
                dve.drain()
                if n not in SPLIT_NORMS:
                    for k in range(DT):
                        stt(H[:, k, tokens], X[:, k, tokens], gain[:, k:k + 1], rms[:, 1, 0:size], ALU.mult, ALU.mult
                            ).then_inc(S[done], 1)
                    return
                f = SPLIT_NORMS.index(n)
                source = normed if n in FFN_NORMS else T0
                for k in range(DT + 1):
                    if k < DT:
                        stt(source[:, k, tokens], X[:, k, tokens], gain[:, k:k + 1], rms[:, 1, 0:size],
                            ALU.mult, ALU.mult).then_inc(S["normed_ready"], 1)
                    if k:
                        dve.wait_ge(S["in_high_ready"], DT * f + k)
                        tt(in_low[:, k - 1, tokens], source[:, k - 1, tokens], in_high[:, k - 1, tokens].bitcast(F32),
                           ALU.subtract).then_inc(S["in_split"], 1)

            def split_out(source, tokens=slice(0, T)):
                for j in range(5):
                    dve.drain()
                    if j < 4:
                        k = slice(2 * j, 2 * j + 2)
                        dve.tensor_copy(out_high[:, k, tokens], source[:, k, tokens])
                    if j:
                        k = slice(2 * j - 2, 2 * j)
                        tt(out_low[:, k, tokens], source[:, k, tokens], out_high[:, k, tokens].bitcast(F32),
                           ALU.subtract).then_inc(S["out_split"], 1)

            def split_hidden(turn, p, tokens):
                tile = bass.ds(turn * 2 + p, 1)
                dve.drain()
                dve.tensor_copy(hid_high[:, tile, tokens], hidden[:, p:p + 1, tokens])
                dve.drain()
                tt(hid_low[:, tile, tokens], hidden[:, p:p + 1, tokens], hid_high[:, tile, tokens].bitcast(F32),
                   ALU.subtract).then_inc(S["hidden_split"], 1)

            def feed_forward(s):
                base, a = tiles_before[s], act_before[s]
                with dve.Fori(0, FT // 2) as turn:
                    for p in range(2):
                        dve.wait_ge(S["linear_ready"], turn * 4 + (base + 2 * p + 2))
                        dve.wait_ge(S["act_emptied"], turn * 2 + (a + p + 1))
                        tt(hidden[:, p, :], ps[:, (base + 2 * p + 1) % 4, 0:T], silu_out[:, p, :], ALU.mult
                           ).then_inc(S["dve_emptied"], 1)
                        split_hidden(turn, p, slice(0, T))

            def conv_feed_forward(s):
                a = act_before[s]
                at = PARAMS["ffn_conv"][0]
                dve.memset(conv_in[:, :, :, N_META - 2:N_META], 0.0)
                dve.drain()
                dve.sem_inc(S["conved"], 4)
                with dve.Fori(0, FT // 2) as turn:
                    for p in range(2):
                        for half in range(2):
                            tap = lambda n: par[:, bass.ds(turn * 2 + (at + 44 * n + 22 * half + p), 1)]
                            src, dst = conv_in[:, p, half, :], conv_out[:, p, half, TB]
                            dve.wait_ge(S["act_emptied"], turn * 4 + (a + 2 * p + half + 1))
                            dve.tensor_scalar(dst, src[:, TB], tap(2), None, ALU.mult)
                            dve.drain()
                            stt(dst, src[:, N_META - 1:T - 1], tap(1), dst, ALU.mult, ALU.add)
                            dve.drain()
                            stt(dst, src[:, N_META - 2:T - 2], tap(0), dst, ALU.mult, ALU.add
                                ).then_inc(S["conved"], 1)
                        dve.drain()
                        dve.wait_ge(S["silu_ready"], turn * 2 + (p + 1))
                        tt(hidden[:, p, TB], silu_out[:, p, TB], conv_out[:, p, 1, TB], ALU.mult)
                        split_hidden(turn, p, TB)

            def residual(name, nth=0, size=T, tokens=slice(0, T), factor=1.0):
                s = stage_number(name, nth)
                for i in range(DT):
                    tile = tiles_before[s] + i
                    dve.wait_ge(S["linear_ready"], tile + 1)
                    stt(X[:, i, tokens], ps[:, tile % 4, 0:size], factor, X[:, i, tokens], ALU.mult, ALU.add
                        ).then_inc(S["dve_emptied"], 1)

            def rk_prepare():
                dve.drain()
                tt(T2[:, :, 1:T], H[:, :, 0:T - 1], H[:, :, 1:T], ALU.subtract)
                dve.tensor_scalar(T2[:, :, 0:1], H[:, :, 0:1], -1.0, None, ALU.mult)
                dve.drain()

                def mix(o, m, k):
                    return stt(o, T2[:, k, :], param("mix", m)[:, k:k + 1], H[:, k, :], ALU.mult, ALU.add)

                mixed = A[:, 40:48, :]
                for i, (m, high, low) in enumerate(((0, in_high, in_low), (2, out_high, out_low),
                                                    (3, in_high, in_low))):
                    if i == 2:
                        dve.wait_ge(S["linear_ready"], tiles_done("rk_r"))
                    for j in range(6):
                        if j < 4:
                            mix(mixed[:, 2 * j, :], m, 2 * j)
                            mix(mixed[:, 2 * j + 1, :], m, 2 * j + 1)
                        if 1 <= j <= 4:
                            k = slice(2 * j - 2, 2 * j)
                            dve.tensor_copy(high[:, k, :], mixed[:, k, :])
                        if j >= 2:
                            k = slice(2 * j - 4, 2 * j - 2)
                            tt(low[:, k, :], mixed[:, k, :], high[:, k, :].bitcast(F32), ALU.subtract
                               ).then_inc(S["rk_mixed"], 1)
                        dve.drain()
                for m, o, before in ((1, T0, "rk_k"), (4, T1, "rk_k"), (5, T0, "rk_w1")):
                    dve.wait_ge(S["linear_ready"], tiles_done(before))
                    for k in range(DT):
                        mix(o[:, k, :], m, k).then_inc(S["rk_mixed"], 1)
                R, K, V, W, B, G = (A[:, 8 * i:8 * i + 8, :] for i in range(6))
                dve.wait_ge(S["act_emptied"], owners[tiles_done("rk_g2") - 1][1])
                tt(T0[:, :, :], K, tiles_of(param("k_k"), DT, T), ALU.mult)
                dve.drain()
                tt(T1[:, :, :], T0[:, :, :], T0[:, :, :], ALU.mult).then_inc(S["rk_kk_squared"], 1)
                tt(T2[:, :, :], R, tiles_of(param("r_k"), DT, T), ALU.mult)
                dve.wait_ge(S["rk_kk_summed"], 1)
                dve.tensor_scalar(T1[:, :, :], ps[:, :, 0:T], 1e-24, None, ALU.max).then_inc(S["rk_kk_clamped"], 1)
                stt(H[:, :, :], B, -1.0, tiles_of(param("k_a"), DT, T), ALU.add, ALU.mult)
                dve.drain()
                stt(K, H[:, :, :], 1.0, K, ALU.add, ALU.mult)
                dve.wait_ge(S["rk_kk_rooted"], 1)
                dve.reciprocal(T1[:, :, :], T1[:, :, :])
                dve.drain()
                tt(T0[:, :, :], T0[:, :, :], T1[:, :, :], ALU.mult)
                dve.drain()
                tt(B, B, T0[:, :, :], ALU.mult)
                tt(T1[:, :, :], T2[:, :, :], K, ALU.mult).then_inc(S["rk_bonus_in"], 1)
                dve.tensor_scalar(W, W, -float(np.exp(-0.5)), None, ALU.mult)
                dve.drain()
                for k in range(DT):
                    dve.tensor_tensor_scan(T2[:, k, :], const("reset"), A[:, 24 + k, :], 0.0, ALU.mult, ALU.add)
                dve.wait_ge(S["rk_bonus_summed"], 1)
                tt(H[:, :, :], ps[:, :, 0:T], V, ALU.mult)
                dve.drain()
                for c, (t0, C) in enumerate(CHUNKS):
                    dve.tensor_copy(rk_mid[:, c, :], T2[:, :, t0 + C // 2])
                dve.drain()
                for c, (t0, C) in enumerate(CHUNKS):
                    tt(T2[:, :, t0:t0 + C], T2[:, :, t0:t0 + C], tiles_of(rk_mid[:, c, :], DT, C), ALU.subtract)
                dve.drain()
                tt(T1[:, :, :], T2[:, :, :], W, ALU.subtract)
                dve.drain()
                dve.sem_inc(S["rk_logs_ready"], 1)
                dve.wait_ge(S["rk_exps_ready"], 1)
                stt(T0[:, :, :], T0[:, :, :], -1.0, T1[:, :, :], ALU.mult, ALU.mult)
                dve.wait_ge(S["rk_exps_ready"], 2)
                tt(R, R, W, ALU.mult)
                for c, (t0, C) in enumerate(CHUNKS):
                    dve.tensor_copy(rk_end[:, c, :], A[:, 24:32, t0 + C - 1])
                dve.wait_ge(S["rk_exps_ready"], 3)
                tt(B, B, T2[:, :, :], ALU.mult)
                tt(K, K, T2[:, :, :], ALU.mult)
                dve.wait_ge(S["rk_exps_ready"], 4)
                dve.drain()
                tt(rk_end[:, 0:2, :], rk_end[:, 0:2, :], rk_mid_exp[:, 1:3, :], ALU.mult)
                dve.drain()
                dve.sem_inc(S["rk_prepared"], 1)

            def rk_mask(g, j, c):
                C = CHUNKS[c][1]
                mask = tri[0:C, :, 0:C].unsqueeze(1).to_broadcast([C, 4, 2, C])
                for i, bank, o in ((0, (2, 6)[j % 2], rk_lb[c]), (1, 4, rk_lk[c])):
                    dve.wait_ge(S["rk_products_ready"], g * 6 + (2 * j + i + 1))
                    v = ps[0:C, bank:bank + 2, :].rearrange("p b (u a t) -> p (b u) a t", u=2, a=2)[:, :, :, 0:C]
                    tt(o[0:C, :, :, :], v, mask, ALU.mult).then_inc(S["rk_masked"], 1)

            def rk_first_level(g, chunks):
                eye = lambda C: tokens_of(ident[0:C, 0:C], 4)
                for c in chunks:
                    C = CHUNKS[c][1]
                    tt(rk_xt[c][0:C, :, :], rk_lb[c][0:C, :, 0, :], tokens_of(const("level_0t")[0:C, 0:C], 4),
                       ALU.mult)
                for c in chunks:
                    C = CHUNKS[c][1]
                    dve.wait_ge(S[f"rk_under{c}_ready"], g * RK_LEVELS[c] + 1)
                    tt(rk_x[c][0:C, :, :], rk_level_bank(c, 0), tokens_of(level[0:C, 0, 0:C], 4), ALU.mult)
                dve.drain()
                for c in chunks:
                    C = CHUNKS[c][1]
                    for x in (rk_x[c][0:C, :, :], rk_xt[c][0:C, :, :]):
                        tt(x, x, eye(C), ALU.add).then_inc(S[f"rk_x{c}_added"], 1)

            def rk_level(g, n, chunks):
                for c in chunks:
                    C = CHUNKS[c][1]
                    dve.wait_ge(S[f"rk_under{c}_ready"], g * RK_LEVELS[c] + (n + 1))
                    tt(rk_ym[c][0:C, :, :], rk_level_bank(c, 0), tokens_of(level[0:C, n, 0:C], 4), ALU.mult
                       ).then_inc(S[f"rk_under{c}_masked"], 1)
                for c in chunks:
                    C = CHUNKS[c][1]
                    dve.wait_ge(S[f"rk_merge{c}_ready"], g * (RK_LEVELS[c] - 1) + n)
                    for i, x in ((1, rk_x[c][0:C, :, :]), (2, rk_xt[c][0:C, :, :])):
                        if i == 2 or n < RK_LEVELS[c] - 1:
                            tt(x, rk_level_bank(c, i), x, ALU.add).then_inc(S[f"rk_x{c}_added"], 1)

            def rk_state(g, c):
                C = CHUNKS[c][1]
                step = g * 3 + (c + 1)
                dve.wait_ge(S["rk_z_ready"], step)
                dve.tensor_copy(rk_z[0:C, :, :].rearrange("p (b u) v -> p b (u v)", b=2), ps[0:C, 0:2, 0:P]
                                ).then_inc(S["rk_z_copied"], 1)
                if c < 2:
                    dve.wait_ge(S["rk_s_ready"], g * 2 + (c + 1))
                    for par in range(2):
                        p = slice(HD * par, HD * par + HD)
                        v = ps[p, 6 + par, 0:P].rearrange("p (u v) -> p u v", u=2)
                        scale = rk_sc[p, c, :].unsqueeze(2).to_broadcast([HD, 2, HD])
                        if c:
                            tt(rk_s[p, 1, :, :], v, rk_s[p, 0, :, :], ALU.add)
                            dve.drain()
                            ins = tt(rk_s[p, 1, :, :], rk_s[p, 1, :, :], scale, ALU.mult)
                        else:
                            ins = tt(rk_s[p, 0, :, :], v, scale, ALU.mult)
                    ins.then_inc(S["rk_state_ready"], 1)

            def rk_stage(g):
                dve.wait_ge(S["rk_y_copied"], g * 3 + 1)
                for i, src in enumerate((T0[:, bass.ds(g * 2, 2), :], A[:, bass.ds(g * 2, 2), :])):
                    dve.tensor_copy(rk_ar[:, :, i, :], src)
                for i, first in enumerate((32, 8, 16)):
                    dve.tensor_copy(rk_bkv[:, i, :, :], A[:, bass.ds(g * 2 + first, 2), :])
                dve.tensor_copy(rk_sc[:, :, :], rk_end[:, 0:2, bass.ds(g * 2, 2)])
                dve.drain()
                dve.sem_inc(S["rk_staged"], 1)

            def rk_finish():
                Y = A[:, 24:32, :]
                dve.wait_ge(S["rk_y_summed"], 1)
                stt(Y, ps[:, :, 0:T], -1.0 / HD, Y, ALU.mult, ALU.add)
                dve.drain()
                tt(T1[:, :, :], Y, Y, ALU.mult).then_inc(S["rk_y_squared"], 1)
                dve.wait_ge(S["rk_y_rooted"], 1)
                dve.reciprocal(T1[:, :, :], T1[:, :, :])
                dve.drain()
                tt(Y, Y, T1[:, :, :], ALU.mult)
                dve.drain()
                for k in range(DT):
                    dve.tensor_scalar(A[:, 24 + k, :], A[:, 24 + k, :], param("lnx_g")[:, k:k + 1],
                                      param("lnx_b")[:, k:k + 1], ALU.mult, ALU.add)
                dve.drain()
                tt(Y, Y, H[:, :, :], ALU.add)
                dve.drain()
                tt(Y, Y, A[:, 40:48, :], ALU.mult)
                split_out(Y)

            def rope(first, count, swapped):
                tt(T0[:, 0:count, :], ps[:, 0:count, 0:T], tokens_of(const("sin"), count), ALU.mult)
                x = A[:, first:first + count, :]
                tt(x, x, tokens_of(const("cos"), count), ALU.mult)
                dve.drain()
                tt(x, x, T0[:, 0:count, :], ALU.add).then_inc(S[swapped], 1)

            def attend(g, pre, steps, gates):
                count = len(steps)

                def biased(n, c, t0, C, branch, keys, bias, *rest):
                    p = at_p[0:C, n % 2, :, 0:keys.shape[1]]
                    dve.wait_ge(S[pre + "_logits"], g * count + (n + 1))
                    stt(p, ps[0:C, 0:4, 0:keys.shape[1]], HD ** -0.5, tokens_of(bias[0:C, :], 4), ALU.mult, ALU.add
                        ).then_inc(S[pre + "_biased"], 1)
                    dve.drain()
                    dve.tensor_reduce(at_max[0:C, n % 2, :], p, AX_X, ALU.max, negate=True).then_inc(S[pre + "_max"], 1)

                def weighted(n, c, t0, C, branch, keys, *rest):
                    nk, inv = keys.shape[1], at_inv[0:C, n % 2, :]
                    p = at_p[0:C, n % 2, :, 0:nk]
                    dve.wait_ge(S[pre + "_exp"], g * count + (n + 1))
                    dve.reciprocal(inv, at_sum[0:C, n % 2, :])
                    dve.drain()
                    if gates:
                        tt(inv, inv, at_gg[:, c, :].rearrange("p (h b) -> p b h", b=3)[:, branch, :], ALU.mult)
                        dve.drain()
                    tt(p, p, inv.unsqueeze(2).to_broadcast([C, 4, nk]), ALU.mult).then_inc(S[pre + "_probs"], 1)

                for i in range(count + 1):
                    if i < count:
                        biased(*steps[i])
                    if i:
                        weighted(*steps[i - 1])

            def ds_select(n):
                c = n + 1
                score, a, b = T2[:, 0, :], T2[:, 1, :], T2[:, 2, :]
                dve.wait_ge(S["ds_relu"], n + 1)
                dve.tensor_scalar(score, T0[:, 0, :], ds_wi[:, n, 0:1], None, ALU.mult)
                for h in range(1, 8):
                    dve.drain()
                    ins = stt(score, T0[:, h, :], ds_wi[:, n, h:h + 1], score, ALU.mult, ALU.add)
                ins.then_inc(S["ds_scored"], 1)
                dve.drain()
                tt(score, score, const("causal")[:, c, :], ALU.mult)
                dve.drain()
                tt(a, score, const("neg")[:, c, :], ALU.add)
                for _ in range(8):
                    dve.drain()
                    dve.max(ds_top[:, :], a)
                    dve.drain()
                    dve.match_replace(b, ds_top[:, :], a, -3e38)
                    a, b = b, a
                dve.drain()
                stt(b, a, -2e38, const("causal")[:, c, :], ALU.is_lt, ALU.mult)
                dve.drain()
                dve.tensor_scalar(T1[:, c, :], b, -NEG, NEG, ALU.mult, ALU.add).then_inc(S["ds_selected"], 1)

            full = slice(0, T)
            dve.wait_ge(S["consts_loaded"], 32)
            norm(0, T, full, param("norm", 0))
            feed_forward(0)
            residual("ffn_out", 0, factor=0.5)
            norm(1, T, full, param("norm", 1))
            rk_prepare()
            with dve.Fori(0, 4) as g:
                rk_stage(g)
                for j, c in enumerate(RK_ORDER):
                    rk_mask(g, j, c)
                dve.drain()
                for n in range(LEVELS):
                    (rk_level(g, n, [c for c in RK_ORDER if n < RK_LEVELS[c]]) if n else
                     rk_first_level(g, RK_ORDER))
                for c in range(3):
                    rk_state(g, c)
            rk_finish()
            residual("rk_o")
            norm(2, T, full, param("norm", 2))
            feed_forward(stage_number("ffn", 1))
            residual("ffn_out", 1, factor=0.5)
            norm(3, T, full, param("norm", 3))
            feed_forward(stage_number("ffn", 2))
            residual("ffn_out", 2, factor=0.5)
            norm(4, T, full, param("norm", 4))
            dve.wait_ge(S["act_emptied"], owners[tiles_done("at_in") - 1][1])
            tt(A[:, 20:32, :], A[:, 0:12, :], A[:, 0:12, :], ALU.mult).then_inc(S["ds_squared"], 1)
            dve.wait_ge(S["ds_rooted"], 2)
            dve.reciprocal(A[:, 20:32, :], A[:, 20:32, :])
            dve.drain()
            stt(A[:, 0:8, :], A[:, 0:8, :], column("q_g"), A[:, 20:28, :], ALU.mult, ALU.mult)
            stt(A[:, 8:12, :], A[:, 8:12, :], column("k_g"), A[:, 28:32, :], ALU.mult, ALU.mult
                ).then_inc(S["ds_normed"], 1)
            for n, (first, count) in enumerate(((0, 8), (8, 4), (14, 5))):
                dve.wait_ge(S["ds_swapped"], n + 1)
                dve.drain()
                rope(first, count, "ds_roped")
            dve.tensor_copy(T1[:, 0, :], const("neg")[:, 0, :])
            dve.wait_ge(S["ds_turned_copied"], 1)
            for n in range(2):
                ds_select(n)
            with dve.Fori(0, 4) as g:
                dve.wait_ge(S["ds_o_copied"], g * 3 + 1)
                dve.tensor_copy(at_q[:, :, :], A[:, bass.ds(g * 2, 2), :])
                dve.tensor_copy(at_kg[:, 0:1, :], A[:, bass.ds(g + 8, 1), :])
                dve.tensor_copy(at_vg[0:N_META, 0:1, :], at_vtm[0:N_META, 0:1, bass.ds(g * HD, HD)])
                dve.tensor_copy(at_vg[:, 1:3, :], at_vtm[:, 1:3, bass.ds(g * HD, HD)])
                dve.drain()
                dve.sem_inc(S["ds_staged"], 1)
                attend(g, "ds", DSA_STEPS, False)
            dve.wait_ge(S["ds_o_copied"], 13)
            split_out(T2)
            residual("at_o")
            norm(5, T, full, param("norm", 5))
            feed_forward(stage_number("ffn", 3))
            residual("ffn_out", 3, factor=0.5)

            norm(6, SEQ, TB, param("norm2"))
            dve.wait_ge(S["ret_swapped"], 1)
            tt(T0[:, :, TB], ps[:, :, 0:SEQ], tokens_of(const("ret_sin"), DT), ALU.mult)
            tt(A[:, 0:8, TB], A[:, 0:8, TB], tokens_of(const("ret_cos"), DT), ALU.mult)
            dve.drain()
            tt(A[:, 0:8, TB], A[:, 0:8, TB], T0[:, :, TB], ALU.add).then_inc(S["ret_roped"], 1)
            dve.wait_ge(S["ret_scores"], 1)
            dve.wait_ge(S["decay_loaded"], 16)
            tt(ret_st.rearrange("p h c q -> p (h c q)"), ps[:, 4:8, :].rearrange("p a b -> p (a b)"), ret_decay,
               ALU.mult).then_inc(S["ret_masked"], 1)
            dve.wait_ge(S["ret_summed"], 1)
            pair = lambda v, j: v.rearrange("p (h j) t -> p h j t", j=2)[:, :, j, :]
            for j in range(2):
                o = pair(A[:, 40:48, TB], j)
                stt(o, ps[:, 0:4, 0:SEQ], -1.0 / SEQ, o, ALU.mult, ALU.add)
            dve.drain()
            tt(T0[:, :, TB], A[:, 40:48, TB], A[:, 40:48, TB], ALU.mult).then_inc(S["ret_squared"], 1)
            dve.wait_ge(S["ret_rooted"], 1)
            dve.reciprocal(T1[:, 4:8, TB], T1[:, 0:4, TB])
            dve.drain()
            for j in range(2):
                o = pair(A[:, 40:48, TB], j)
                tt(o, o, T1[:, 4:8, TB], ALU.mult)
            dve.drain()
            for k in range(DT):
                stt(H[:, k, TB], A[:, 40 + k, TB], param("ret_norm")[:, k:k + 1], A[:, 16 + k, TB],
                    ALU.mult, ALU.mult)
            split_out(H, TB)
            dve.wait_ge(S["act_emptied"], owners[tiles_done("ret_out") - 1][1])
            tt(T2[:, :, TB], A[:, 0:8, TB], A[:, 8:16, TB], ALU.mult).then_inc(S["merged"], 1)
            dve.wait_ge(S["act_emptied"], owners[tiles_done("sc_in") - 1][1])
            tt(A[:, 8:16, TB], A[:, 8:16, TB], A[:, 16:24, TB], ALU.mult)
            dve.memset(A[:, 8:16, N_META - 2:N_META], 0.0)
            for tap in (2, 1, 0):
                dve.drain()
                for k in range(DT):
                    w = param("sc_conv", tap)[:, k:k + 1]
                    src = A[:, 8 + k, N_META - 2 + tap:T - 2 + tap]
                    if tap == 2:
                        dve.tensor_scalar(H[:, k, TB], src, w, None, ALU.mult)
                    else:
                        stt(H[:, k, TB], src, w, H[:, k, TB], ALU.mult, ALU.add)
            dve.drain()
            tt(H[:, :, TB], H[:, :, TB], A[:, 0:8, TB], ALU.mult)
            split_out(H, TB)
            dve.wait_ge(S["act_emptied"], owners[tiles_done("sc_out") - 1][1])
            tt(A[:, 24:32, TB], A[:, 24:32, TB], A[:, 32:40, TB], ALU.mult)
            dve.drain()
            tt(T2[:, :, TB], T2[:, :, TB], A[:, 24:32, TB], ALU.add).then_inc(S["merged"], 1)
            dve.wait_ge(S["act_emptied"], owners[tiles_done("nsa_in") - 1][1])
            for kv in range(2):
                if kv:
                    dve.wait_ge(S["linear_ready"], tiles_done("cmp_k1"))
                for half in range(2):
                    p = slice(HD * half, HD * half + HD)
                    for m0 in range(2):
                        for g in range(4):
                            src = A[p, 8 + 4 * kv + g, TB].rearrange("p (c l) -> p l c", l=16)
                            o = ns_blk[p, 8 * m0:8 * m0 + 8, g * N_CMP:(g + 1) * N_CMP]
                            at = PARAMS["cmp_pos"][0] + 16 * kv + 8 * m0
                            pos = par[p, at:at + 8].unsqueeze(2).to_broadcast([HD, 8, N_CMP])
                            ins = tt(o, src[:, half::2, m0:m0 + N_CMP], pos, ALU.add)
                ins.then_inc(S["ns_blocks"], 1)
            dve.wait_ge(S["ns_turned_copied"], 1)
            for c in range(2):
                at = CONSTS["any_cmp"][0] + c
                o = ns_gate[:, c, :].rearrange("p (h b) -> p b h", b=3)[:, 0, :]
                dve.tensor_scalar(o, o, con[:, at:at + 1], None, ALU.mult)
            dve.wait_ge(S["act_emptied"], owners[tiles_done("cmp_v2") - 1][1])
            dve.drain()
            with dve.Fori(0, 4) as g:
                dve.wait_ge(S["ns_o_copied"], g * 2 + 1)
                dve.tensor_copy(at_q[:, :, TB], A[:, bass.ds(g * 2, 2), TB])
                for b in range(2):
                    dve.tensor_copy(at_kg[:, b:b + 1, TB], A[:, bass.ds(g + (16 + 4 * b), 1), TB])
                dve.tensor_copy(at_vg[:, 0:4, :], at_vtm[:, :, bass.ds(g * HD, HD)])
                dve.tensor_copy(ns_kc[:, :], ns_cmp_k[:, bass.ds(g * N_CMP, N_CMP)])
                dve.tensor_copy(ns_vc[0:N_CMP, :], ns_cmp_v[0:N_CMP, bass.ds(g, 1), :].rearrange("p a v -> p (a v)"))
                dve.tensor_copy(at_gg[:, :, :], ns_gate[:, :, bass.ds(g * 12, 12)])
                dve.drain()
                dve.sem_inc(S["ns_staged"], 1)
                attend(g, "ns", NSA_STEPS, True)
            dve.wait_ge(S["ns_o_copied"], 9)
            split_out(H, TB)
            dve.wait_ge(S["act_emptied"], owners[tiles_done("nsa_out") - 1][1])
            tt(A[:, 0:8, TB], A[:, 0:8, TB], A[:, 32:40, TB], ALU.mult)
            dve.drain()
            tt(T2[:, :, TB], T2[:, :, TB], A[:, 0:8, TB], ALU.add)
            split_out(T2, TB)
            residual("mix_out", size=SEQ, tokens=TB)
            norm(7, SEQ, TB, param("ffn_norm2"))
            conv_feed_forward(stage_number("ffn2"))
            residual("ffn_out", 4, SEQ, TB)
            norm(8, SEQ, TB, param("final"), "final_ready")


def weight_stream(inp):
    def tiles(w, interleave=False):
        k, n = w.shape
        kt, nt = -(-k // P), -(-n // P)
        if (k, n) != (kt * P, nt * P):
            w = np.pad(w, ((0, kt * P - k), (0, nt * P - n)))
        t = w.reshape(kt, P, nt, P).transpose(2, 0, 1, 3)
        if interleave:
            t = np.stack([t[:nt // 2], t[nt // 2:]], axis=1)
        return t.reshape(kt * nt, P, P)

    def twice(w):
        k, n = w.shape
        return np.repeat(w.reshape(k, n // HD, 1, HD), 2, axis=2).reshape(k, 2 * n)

    def ffn(i, j):
        return [tiles(inp["ffn_w_in"][i, j], True)], [tiles(inp["ffn_w_out"][i, j])]

    at = inp["at_w_in"][0]
    z = inp["w_in_2"][0]
    cut = np.cumsum([0, 512, 512, 1024, 1024, 1024, 1024, 1024, 1024, 1536, 48, 3072])
    z = [z[:, a:b] for a, b in zip(cut[:-1], cut[1:])]
    kc, vc, ks, vs, kw, vw = np.split(z[8], 6, axis=1)
    mg = np.split(z[10], 3, axis=1)
    many = lambda *ws: [tiles(w) for w in ws]
    per_stage = [
        *ffn(0, 0), many(inp["rk_w_r"][0]), many(inp["rk_w_k"][0]), many(inp["rk_w_v"][0]),
        many(inp["rk_w1"][0]), many(inp["rk_w2"][0]), many(inp["rk_a1"][0]), many(inp["rk_a2"][0]),
        many(inp["rk_g1"][0]), many(inp["rk_g2"][0]), many(inp["rk_w_o"][0]),
        *ffn(0, 1), *ffn(1, 0),
        many(at[:, :1024], twice(at[:, 1024:1280]), at[:, 1280:1536], at[:, 1536:2048], twice(at[:, 2048:2112]),
             at[:, 2112:]),
        many(inp["at_w_o"][0]), *ffn(1, 1),
        many(z[0], z[1], z[2], z[3]), many(mg[0]), many(inp["w_ret_out_2"][0]),
        many(z[4], z[5], z[6]), many(mg[1]), many(inp["w_sc_out_2"][0]),
        many(z[7], twice(kc), twice(vc), twice(ks), twice(kw), vs, vw, z[9]),
        many(mg[2]), many(inp["nsa_cmp_w1_2"][0, 0]), many(twice(inp["nsa_cmp_w2_2"][0, 0])),
        many(inp["nsa_cmp_w1_2"][0, 1]), many(inp["nsa_cmp_w2_2"][0, 1]),
        many(inp["w_nsa_out_2"][0]), many(inp["w_mix_out_2"][0]),
        [tiles(inp["w_ffn_up_2"][0], True)], [tiles(inp["w_ffn_down_2"][0])],
    ]
    out = np.zeros((N_SLOTS * PER, P, P), np.float32)
    assert len(per_stage) == len(STAGES)
    for start, (name, kt, nt), parts in zip(STARTS, STAGES, per_stage):
        assert sum(len(t) for t in parts) == kt * nt, name
        for t in parts:
            out[start:start + len(t)] = t
            start += len(t)
    return np.ascontiguousarray(out.reshape(N_SLOTS, PER, P, P).transpose(0, 2, 1, 3)).reshape(N_SLOTS, P, PER * P)


def parameters(inp):
    f = lambda v: np.reshape(v, (-1, P)).T
    pos = inp["nsa_cmp_pos_2"][0].reshape(2, 16, P)
    cols = {
        "norm": f(inp["norm_g"]), "mix": f(inp["rk_mix"]), "w0": f(inp["rk_w0"]), "a0": f(inp["rk_a0"]),
        "k_k": f(inp["rk_k_k"]), "k_a": f(inp["rk_k_a"]), "r_k": f(inp["rk_r_k"]), "lnx_g": f(inp["rk_lnx_g"]),
        "lnx_b": f(inp["rk_lnx_b"]), "q_g": f(np.tile(inp["at_q_g"][0], 2)), "k_g": f(np.tile(inp["at_k_g"][0], 2)),
        "norm2": f(inp["attn_norm_w_2"]), "ret_norm": f(inp["ret_norm_w_2"]), "sc_conv": f(inp["sc_conv_w_2"]),
        "cmp_pos": f(pos), "ffn_norm2": f(inp["ffn_norm_w_2"]), "ffn_conv": f(inp["ffn_conv_w_2"]),
        "final": f(inp["final_norm_w_2"]),
    }
    for name, (_, n) in PARAMS.items():
        assert cols[name].shape[1] == n, name
    return np.concatenate([cols[n] for n in PARAMS], axis=1)


def kernel(**inputs):
    import concourse.bacc as _bacc
    from concourse.bass_utils import run_bass_kernel_spmd as _run

    inp = {k: np.asarray(v) for k, v in inputs.items()}
    x = np.concatenate([inp["meta"], inp["x"][0]], axis=0)
    arrays = {
        "stream": weight_stream(inp),
        "x_in": x.T.reshape(DT, P, T).transpose(1, 0, 2),
        "params": parameters(inp),
        "consts": constants(),
        "decay": retention_decay(),
    }
    arrays = {k: np.ascontiguousarray(v) for k, v in arrays.items()}
    nc = _bacc.Bacc("TRN2", target_bir_lowering=False, num_devices=1)
    args = [nc.dram_tensor(k, v.shape, F32, kind="ExternalInput").ap() for k, v in arrays.items()]
    out = nc.dram_tensor("out", (P, DT * SEQ), F32, kind="ExternalOutput").ap()
    build(nc, *args, out)
    got = _run(nc, [arrays], core_ids=[0]).results[0]["out"]
    return np.ascontiguousarray(np.reshape(got, (P, DT, SEQ)).transpose(2, 1, 0)).reshape(1, SEQ, D)
```
